# Optimizing a Trainium2 kernel written in Bass

```python
import math
import jax
import jax.numpy as jnp
from jax import lax
import numpy as np

D_MODEL = 1024
BATCH = 1
SEQ = 128
DEPTH = 1
DEC_BATCH = 1
DEC_SEQ = 512
PAST_LEN = 256

GRID_W = 64
HEAD_DIM = 64
GROUP_W = D_MODEL // 4
D_MIX = 4 * GROUP_W
H_A = GROUP_W // HEAD_DIM
DK_A = HEAD_DIM
DV_A = HEAD_DIM
W_A = H_A * HEAD_DIM
H_B = GROUP_W // HEAD_DIM
DK_B = HEAD_DIM
DV_B = HEAD_DIM
W_B = H_B * HEAD_DIM
H_C = GROUP_W // HEAD_DIM
DK_C = HEAD_DIM
DV_C = HEAD_DIM
W_C = H_C * HEAD_DIM
W_D = GROUP_W
GDN_CONV = 5
HYENA_CONV = 3
HYENA_ORDER = 2
CHUNK = 64
HGRN_CHUNK = 16
POS_BANDS = 16
POS_DIM = 1 + 2 * POS_BANDS
FILTER_HIDDEN = 64
HYENA_TARGET = 1e-2
HYENA_FAST_DECAY = 0.3
HYENA_SLOW_DECAY = 1.5
N_EXPERTS = 64
TOP_K = 8
D_EXPERT = 128
D_SHARED = 128
ROUTED_SCALE = 2.5
EPS = 1e-6
IN_SIZES = (W_A, W_A, W_A, W_A, 2 * H_A, 2 * H_A,
            W_B, W_B, W_B, 2 * W_B,
            W_C, W_C, W_C, W_C, 2 * H_C, 2 * H_C,
            3 * W_D)
N_IN = 4 * W_A + 4 * H_A + 5 * W_B + 4 * W_C + 4 * H_C + 3 * W_D

kernel_name = 'hybrid_flow_trunk_ctx_and_denoise'

def _rmsnorm(x, g):
    xf = x.astype(jnp.float32)
    y = xf * lax.rsqrt(jnp.mean(xf * xf, axis=-1, keepdims=True) + EPS)
    return (y * g.astype(jnp.float32)).astype(x.dtype)

def _head_rmsnorm(o, g):
    return o * lax.rsqrt(jnp.mean(o * o, axis=-1, keepdims=True) + EPS) * g

def _l2norm(x):
    return x * lax.rsqrt(jnp.sum(x * x, axis=-1, keepdims=True) + EPS)

def _split(t, sizes):
    out, start = [], 0
    for s in sizes:
        out.append(t[..., start:start + s])
        start += s
    return out

def _heads(t, n_heads):
    b, l, _ = t.shape
    return t.reshape(b, l, n_heads, -1).transpose(0, 2, 1, 3)

def _merge(t):
    b, h, l, d = t.shape
    return t.transpose(0, 2, 1, 3).reshape(b, l, h * d)

def _flip(t):
    return jnp.flip(t, axis=2)

def _to_colmajor(t, rows):
    b, l, ch = t.shape
    return t.reshape(b, rows, GRID_W, ch).transpose(0, 2, 1, 3).reshape(b, l, ch)

def _from_colmajor(t, rows):
    b, l, ch = t.shape
    return t.reshape(b, GRID_W, rows, ch).transpose(0, 2, 1, 3).reshape(b, l, ch)

def _dwconv(x, w):
    width = w.shape[0]
    return lax.conv_general_dilated(x, w[:, None, :].astype(x.dtype), (1,), [(width // 2, width // 2)],
                                    dimension_numbers=('NWC', 'WIO', 'NWC'),
                                    feature_group_count=x.shape[-1])

def _chunks(t, size):
    b, h, l = t.shape[:3]
    return jnp.moveaxis(t.reshape(b, h, l // size, size, *t.shape[3:]), 2, 0)

def _unchunk(t):
    n, b, h, c = t.shape[:4]
    return jnp.moveaxis(t, 0, 2).reshape(b, h, n * c, *t.shape[4:])

def _adaln(cond, w_mod, b_mod):
    m = jax.nn.silu(cond) @ w_mod + b_mod
    return m.reshape(cond.shape[0], 6, D_MODEL)

def _hgrn_lower_bounds(lb_logits):
    p = jax.nn.softmax(lb_logits.astype(jnp.float32), axis=0)
    return jnp.cumsum(p, axis=0) - p[0:1]

def _gdn_chunked(q, k, v, g, beta, s0):
    c = CHUNK
    q, k, v, g, beta = (_chunks(t, c) for t in (q, k, v, g, beta))
    gc = jnp.cumsum(g, axis=-1)
    incl = jnp.tril(jnp.ones((c, c), dtype=bool))
    strict = jnp.tril(jnp.ones((c, c), dtype=bool), -1)
    decay = jnp.exp(jnp.where(incl, gc[..., :, None] - gc[..., None, :], -jnp.inf))
    kb = k * beta[..., None]
    lmat = jnp.where(strict, jnp.einsum('nbhid,nbhjd->nbhij', kb, k) * decay, 0.0)
    eye = jnp.eye(c, dtype=q.dtype)
    tmat = lax.linalg.triangular_solve(eye + lmat, jnp.broadcast_to(eye, lmat.shape),
                                       left_side=True, lower=True, unit_diagonal=True)
    u = tmat @ (v * beta[..., None])
    w = tmat @ (kb * jnp.exp(gc)[..., None])
    attn = jnp.einsum('nbhid,nbhjd->nbhij', q, k) * decay
    q_dec = q * jnp.exp(gc)[..., None]
    k_dec = k * jnp.exp(gc[..., -1:] - gc)[..., None]
    g_last = jnp.exp(gc[..., -1])

    def step(s, xs):
        u_i, w_i, qd_i, kd_i, a_i, gl_i = xs
        v_new = u_i - w_i @ s
        o = qd_i @ s + a_i @ v_new
        s = s * gl_i[..., None, None] + jnp.einsum('bhcd,bhce->bhde', kd_i, v_new)
        return s, o

    s_fin, o = lax.scan(step, s0, (u, w, q_dec, k_dec, attn, g_last))
    return _unchunk(o), s_fin

def _gdn_mixer(q, k, v, gate, a, b, s0, conv_w, a_log, dt_bias, norm_g):
    bsz, l, _ = q.shape
    qkv = jax.nn.silu(_dwconv(jnp.concatenate([q, k, v], axis=-1), conv_w))
    q, k, v = jnp.split(qkv, 3, axis=-1)
    q = _l2norm(_heads(q, H_A)) * DK_A ** -0.5
    k = _l2norm(_heads(k, H_A))
    v = _heads(v, H_A)
    a = a.reshape(bsz, l, 2, H_A).transpose(2, 0, 3, 1)
    b = b.reshape(bsz, l, 2, H_A).transpose(2, 0, 3, 1)
    g = -jnp.exp(a_log)[:, None, :, None] * jax.nn.softplus(a + dt_bias[:, None, :, None])
    beta = jax.nn.sigmoid(b)
    o_f, s_f = _gdn_chunked(q, k, v, g[0], beta[0], s0[:, 0])
    o_b, s_b = _gdn_chunked(_flip(q), _flip(k), _flip(v), _flip(g[1]), _flip(beta[1]), s0[:, 1])
    o = _merge(_head_rmsnorm(o_f + _flip(o_b), norm_g))
    return o * jax.nn.silu(gate), jnp.stack([s_f, s_b], axis=1)

def _gla_chunked(q, k, v, logf, s0):
    c = HGRN_CHUNK
    q, k, v, logf = (_chunks(t, c) for t in (q, k, v, logf))
    gc = jnp.cumsum(logf, axis=-2)
    incl = jnp.tril(jnp.ones((c, c), dtype=bool))[..., None]
    decay = jnp.exp(jnp.where(incl, gc[..., :, None, :] - gc[..., None, :, :], -jnp.inf))
    attn = jnp.einsum('nbhid,nbhjd,nbhijd->nbhij', q, k, decay)
    q_dec = q * jnp.exp(gc)
    k_dec = k * jnp.exp(gc[..., -1:, :] - gc)
    g_last = jnp.exp(gc[..., -1, :])

    def step(s, xs):
        qd_i, kd_i, v_i, a_i, gl_i = xs
        o = qd_i @ s + a_i @ v_i
        s = s * gl_i[..., None] + jnp.einsum('bhcd,bhce->bhde', kd_i, v_i)
        return s, o

    s_fin, o = lax.scan(step, s0, (q_dec, k_dec, v, attn, g_last))
    return _unchunk(o), s_fin

def _hgrn_mixer(q, i, gate, f, s0, lb, norm_g, rows):
    if rows is not None:
        q, i, f = (_to_colmajor(t, rows) for t in (q, i, f))
    bsz, l, _ = q.shape
    forget = lb + (1.0 - lb) * jax.nn.sigmoid(f.reshape(bsz, l, 2, W_B))
    logf = jnp.log(forget)
    key = 1.0 - forget
    q = _heads(q, H_B)
    i = _heads(i, H_B)
    o_f, s_f = _gla_chunked(q, _heads(key[:, :, 0], H_B), i, _heads(logf[:, :, 0], H_B), s0[:, 0])
    o_b, s_b = _gla_chunked(_flip(q), _flip(_heads(key[:, :, 1], H_B)), _flip(i),
                            _flip(_heads(logf[:, :, 1], H_B)), s0[:, 1])
    o = _merge(_head_rmsnorm(o_f + _flip(o_b), norm_g))
    if rows is not None:
        o = _from_colmajor(o, rows)
    return o * jax.nn.sigmoid(gate), jnp.stack([s_f, s_b], axis=1)

def _mlstm_chunked(q, k, v, ig, logf, c0, n0, m0):
    c = CHUNK
    q, k, v, ig, logf = (_chunks(t, c) for t in (q, k, v, ig, logf))
    bc = jnp.cumsum(logf, axis=-1)
    incl = jnp.tril(jnp.ones((c, c), dtype=bool))
    dmat = jnp.where(incl, bc[..., :, None] - bc[..., None, :] + ig[..., None, :], -jnp.inf)
    dmax = jnp.max(dmat, axis=-1)
    qk = jnp.einsum('nbhid,nbhjd->nbhij', q, k)

    def step(carry, xs):
        cm, nv, m = carry
        q_i, k_i, v_i, b_i, d_i, dmax_i, qk_i = xs
        a = b_i + m[..., None]
        m_t = jnp.maximum(a, dmax_i)
        inter = jnp.exp(a - m_t)
        wmat = jnp.exp(d_i - m_t[..., None]) * qk_i
        num = inter[..., None] * (q_i @ cm) + wmat @ v_i
        den = inter * jnp.einsum('bhcd,bhd->bhc', q_i, nv) + jnp.sum(wmat, axis=-1)
        h = num / jnp.maximum(jnp.abs(den), jnp.exp(-m_t))[..., None]
        m_new = m_t[..., -1]
        carry_w = jnp.exp(a[..., -1] - m_new)
        wk = jnp.exp(d_i[..., -1, :] - m_new[..., None])
        cm = carry_w[..., None, None] * cm + jnp.einsum('bhc,bhcd,bhce->bhde', wk, k_i, v_i)
        nv = carry_w[..., None] * nv + jnp.einsum('bhc,bhcd->bhd', wk, k_i)
        return (cm, nv, m_new), h

    (cf, nf, mf), h = lax.scan(step, (c0, n0, m0), (q, k, v, bc, dmat, dmax, qk))
    return _unchunk(h), cf, nf, mf

def _mlstm_mixer(q, k, v, ogate, ig, fg, c0, n0, m0, f_bias, norm_g):
    bsz, l, _ = q.shape
    q = _heads(q, H_C)
    k = _heads(k, H_C) * DK_C ** -0.5
    v = _heads(v, H_C)
    ig = ig.reshape(bsz, l, 2, H_C).transpose(2, 0, 3, 1)
    logf = jax.nn.log_sigmoid(fg.reshape(bsz, l, 2, H_C).transpose(2, 0, 3, 1) + f_bias[:, None, :, None])
    h_f, cf, nf, mf = _mlstm_chunked(q, k, v, ig[0], logf[0], c0[:, 0], n0[:, 0], m0[:, 0])
    h_b, cb, nb, mb = _mlstm_chunked(_flip(q), _flip(k), _flip(v), _flip(ig[1]), _flip(logf[1]),
                                     c0[:, 1], n0[:, 1], m0[:, 1])
    h = _merge(_head_rmsnorm(h_f + _flip(h_b), norm_g))
    return (h * jax.nn.sigmoid(ogate), jnp.stack([cf, cb], axis=1), jnp.stack([nf, nb], axis=1),
            jnp.stack([mf, mb], axis=1))

def _hyena_filters(length, w1, b1, w2, b2, w3, freq):
    t = jnp.arange(length, dtype=jnp.float32)
    tn = jnp.linspace(0.0, 1.0, length, dtype=jnp.float32)
    bands = jnp.linspace(1e-4, POS_BANDS - 1, POS_BANDS, dtype=jnp.float32)
    ang = (2.0 * math.pi / length) * t[:, None] * bands[None, :]
    feats = jnp.concatenate([tn[:, None], jnp.cos(ang), -jnp.sin(ang)], axis=-1)
    hid = jnp.sin(freq * (feats @ w1 + b1))
    hid = jnp.sin(freq * (hid @ w2 + b2))
    h = (hid @ w3).reshape(length, HYENA_ORDER, 2, W_D)
    deltas = jnp.abs(jnp.linspace(math.log(HYENA_TARGET) / HYENA_SLOW_DECAY,
                                  math.log(HYENA_TARGET) / HYENA_FAST_DECAY, W_D, dtype=jnp.float32))
    h = h * jnp.exp(-tn[:, None] * deltas[None, :])[:, None, None, :]
    zero = jnp.zeros((1, HYENA_ORDER, W_D), jnp.float32)
    circ = jnp.concatenate([h[:, :, 0], zero, h[:0:-1, :, 1]], axis=0)
    circ = circ * lax.rsqrt(jnp.sum(circ * circ, axis=0, keepdims=True) + EPS)
    return jnp.fft.rfft(circ, axis=0)

def _hyena_mixer(u, conv_w, w1, b1, w2, b2, w3, freq, dbias):
    bsz, l, _ = u.shape
    u = _dwconv(u, conv_w)
    v, x1, x2 = jnp.split(u, 3, axis=-1)
    hf = _hyena_filters(l, w1, b1, w2, b2, w3, freq)

    def longconv(z, o):
        zf = jnp.fft.rfft(z, n=2 * l, axis=1)
        return jnp.fft.irfft(zf * hf[None, :, o], n=2 * l, axis=1)[:, :l] + dbias[o] * z

    z = x1 * longconv(v, 0)
    return x2 * longconv(z, 1)

def _moe(x, router_w, router_bias, w_gate, w_up, w_down, sh_gate, sh_up, sh_down):
    bsz, l, d = x.shape
    t = x.reshape(bsz * l, d)
    scores = jax.nn.sigmoid((t @ router_w).astype(jnp.float32))
    _, idx = lax.top_k(scores + router_bias.astype(jnp.float32), TOP_K)
    sel = jnp.take_along_axis(scores, idx, axis=-1)
    wts = sel / jnp.sum(sel, axis=-1, keepdims=True) * ROUTED_SCALE
    gates = jnp.einsum('tk,tke->te', wts, jax.nn.one_hot(idx, N_EXPERTS, dtype=jnp.float32)).astype(x.dtype)
    hid = jax.nn.silu(jnp.einsum('td,edf->tef', t, w_gate)) * jnp.einsum('td,edf->tef', t, w_up)
    routed = jnp.einsum('tef,efd->td', hid * gates[..., None], w_down)
    shared = (jax.nn.silu(t @ sh_gate) * (t @ sh_up)) @ sh_down
    return (routed + shared).reshape(bsz, l, d)

def _mixing(h, states, prm, lb, rows):
    f32 = lambda t: t.astype(jnp.float32)
    s_gdn, s_hgrn, s_c, s_n, s_m = (f32(s) for s in states)
    proj = f32(h @ prm['w_in'])
    qa, ka, va, ga, aa, ba, qb, ib, gb, fb, qc, kc, vc, oc, ic, fc, ud = _split(proj, IN_SIZES)
    ya, st_a = _gdn_mixer(qa, ka, va, ga, aa, ba, s_gdn, f32(prm['gdn_conv']), f32(prm['gdn_a_log']),
                          f32(prm['gdn_dt_bias']), f32(prm['gdn_norm_g']))
    yb, st_b = _hgrn_mixer(qb, ib, gb, fb, s_hgrn, lb, f32(prm['hgrn_norm_g']), rows)
    yc, st_c, st_n, st_m = _mlstm_mixer(qc, kc, vc, oc, ic, fc, s_c, s_n, s_m,
                                        f32(prm['mlstm_f_bias']), f32(prm['mlstm_norm_g']))
    yd = _hyena_mixer(ud, f32(prm['hyena_conv']), f32(prm['filt_w1']), f32(prm['filt_b1']),
                      f32(prm['filt_w2']), f32(prm['filt_b2']), f32(prm['filt_w3']),
                      f32(prm['filt_freq']), f32(prm['hyena_d']))
    y = jnp.concatenate([ya, yb, yc, yd], axis=-1).astype(h.dtype) @ prm['w_out']
    return y, (st_a, st_b, st_c, st_n, st_m)

def _block(x, mod, states, prm, lb, rows):
    shift1, scale1, gate1, shift2, scale2, gate2 = (mod[:, j][:, None, :] for j in range(6))
    h = _rmsnorm(x, prm['norm1_g']) * (1 + scale1) + shift1
    y, new_states = _mixing(h, states, prm, lb, rows)
    x = x + gate1 * y
    h = _rmsnorm(x, prm['norm2_g']) * (1 + scale2) + shift2
    x = x + gate2 * _moe(h, prm['router_w'], prm['router_bias'], prm['exp_w_gate'], prm['exp_w_up'],
                         prm['exp_w_down'], prm['sh_w_gate'], prm['sh_w_up'], prm['sh_w_down'])
    return x, new_states

def setup_inputs(seed: int = 0) -> dict:
    key = jax.random.key(seed)
    k = jax.random.split(key, 40)
    f32 = jnp.float32

    def nrm(i, shape, scale):
        return scale * jax.random.normal(k[i], shape, f32)

    def gain(i, shape):
        return 1.0 + 0.02 * jax.random.normal(k[i], shape, f32)

    dt = jnp.exp(jax.random.uniform(k[16], (DEPTH, 2, H_A), f32, math.log(1e-3), math.log(1e-1)))
    return {
        'x_prompt': nrm(0, (BATCH, SEQ, D_MODEL), 1.0),
        'x_sample': nrm(1, (DEC_BATCH, DEC_SEQ, D_MODEL), 1.0),
        'c': nrm(2, (DEC_BATCH, D_MODEL), 1.0),
        'state_gdn': nrm(3, (DEC_BATCH, DEPTH, 2, H_A, DK_A, DV_A), 0.3),
        'state_hgrn': nrm(4, (DEC_BATCH, DEPTH, 2, H_B, DK_B, DV_B), 0.5),
        'state_mlstm_c': nrm(5, (DEC_BATCH, DEPTH, 2, H_C, DK_C, DV_C), 0.3),
        'state_mlstm_n': nrm(6, (DEC_BATCH, DEPTH, 2, H_C, DK_C), 0.3),
        'state_mlstm_m': nrm(7, (DEC_BATCH, DEPTH, 2, H_C), 1.0),
        'c_ctx': nrm(8, (D_MODEL,), 1.0),
        'norm1_g': gain(9, (DEPTH, D_MODEL)),
        'norm2_g': gain(10, (DEPTH, D_MODEL)),
        'w_mod': nrm(11, (DEPTH, D_MODEL, 6 * D_MODEL), 0.5 * D_MODEL ** -0.5),
        'b_mod': nrm(12, (DEPTH, 6 * D_MODEL), 0.02),
        'w_in': nrm(13, (DEPTH, D_MODEL, N_IN), D_MODEL ** -0.5),
        'gdn_conv': nrm(14, (DEPTH, GDN_CONV, 3 * W_A), GDN_CONV ** -0.5),
        'gdn_a_log': jnp.log(jax.random.uniform(k[15], (DEPTH, 2, H_A), f32, 1.0, 16.0)),
        'gdn_dt_bias': dt + jnp.log(-jnp.expm1(-dt)),
        'gdn_norm_g': gain(17, (DEPTH, DV_A)),
        'hgrn_lb_logits': nrm(18, (DEPTH, 2, W_B), 0.5),
        'hgrn_norm_g': gain(19, (DEPTH, DV_B)),
        'mlstm_f_bias': jax.random.uniform(k[20], (DEPTH, 2, H_C), f32, 3.0, 6.0),
        'mlstm_norm_g': gain(21, (DEPTH, DV_C)),
        'hyena_conv': nrm(22, (DEPTH, HYENA_CONV, 3 * W_D), HYENA_CONV ** -0.5),
        'filt_w1': nrm(23, (DEPTH, POS_DIM, FILTER_HIDDEN), POS_DIM ** -0.5),
        'filt_b1': nrm(24, (DEPTH, FILTER_HIDDEN), 0.1),
        'filt_w2': nrm(25, (DEPTH, FILTER_HIDDEN, FILTER_HIDDEN), FILTER_HIDDEN ** -0.5),
        'filt_b2': nrm(26, (DEPTH, FILTER_HIDDEN), 0.1),
        'filt_w3': nrm(27, (DEPTH, FILTER_HIDDEN, HYENA_ORDER * 2 * W_D), FILTER_HIDDEN ** -0.5),
        'filt_freq': gain(28, (DEPTH, FILTER_HIDDEN)),
        'hyena_d': nrm(29, (DEPTH, HYENA_ORDER, W_D), 0.3),
        'w_out': nrm(30, (DEPTH, D_MIX, D_MODEL), D_MIX ** -0.5),
        'router_w': nrm(31, (DEPTH, D_MODEL, N_EXPERTS), D_MODEL ** -0.5),
        'router_bias': nrm(32, (DEPTH, N_EXPERTS), 0.01),
        'exp_w_gate': nrm(33, (DEPTH, N_EXPERTS, D_MODEL, D_EXPERT), D_MODEL ** -0.5),
        'exp_w_up': nrm(34, (DEPTH, N_EXPERTS, D_MODEL, D_EXPERT), D_MODEL ** -0.5),
        'exp_w_down': nrm(35, (DEPTH, N_EXPERTS, D_EXPERT, D_MODEL), D_EXPERT ** -0.5),
        'sh_w_gate': nrm(36, (DEPTH, D_MODEL, D_SHARED), D_MODEL ** -0.5),
        'sh_w_up': nrm(37, (DEPTH, D_MODEL, D_SHARED), D_MODEL ** -0.5),
        'sh_w_down': nrm(38, (DEPTH, D_SHARED, D_MODEL), D_SHARED ** -0.5),
        'final_g': gain(39, (D_MODEL,)),
    }

def reference(x_prompt, x_sample, c, state_gdn, state_hgrn, state_mlstm_c, state_mlstm_n, state_mlstm_m,
              c_ctx, norm1_g, norm2_g, w_mod, b_mod, w_in, gdn_conv, gdn_a_log, gdn_dt_bias, gdn_norm_g,
              hgrn_lb_logits, hgrn_norm_g, mlstm_f_bias, mlstm_norm_g, hyena_conv, filt_w1, filt_b1,
              filt_w2, filt_b2, filt_w3, filt_freq, hyena_d, w_out, router_w, router_bias, exp_w_gate,
              exp_w_up, exp_w_down, sh_w_gate, sh_w_up, sh_w_down, final_g):
    lower = _hgrn_lower_bounds(hgrn_lb_logits)

    def layer_params(l):
        return {'norm1_g': norm1_g[l], 'norm2_g': norm2_g[l], 'w_in': w_in[l], 'gdn_conv': gdn_conv[l],
                'gdn_a_log': gdn_a_log[l], 'gdn_dt_bias': gdn_dt_bias[l], 'gdn_norm_g': gdn_norm_g[l],
                'hgrn_norm_g': hgrn_norm_g[l], 'mlstm_f_bias': mlstm_f_bias[l], 'mlstm_norm_g': mlstm_norm_g[l],
                'hyena_conv': hyena_conv[l], 'filt_w1': filt_w1[l], 'filt_b1': filt_b1[l],
                'filt_w2': filt_w2[l], 'filt_b2': filt_b2[l], 'filt_w3': filt_w3[l],
                'filt_freq': filt_freq[l], 'hyena_d': hyena_d[l], 'w_out': w_out[l],
                'router_w': router_w[l], 'router_bias': router_bias[l], 'exp_w_gate': exp_w_gate[l],
                'exp_w_up': exp_w_up[l], 'exp_w_down': exp_w_down[l], 'sh_w_gate': sh_w_gate[l],
                'sh_w_up': sh_w_up[l], 'sh_w_down': sh_w_down[l]}

    bsz = x_prompt.shape[0]
    zero_states = (jnp.zeros((bsz, 2, H_A, DK_A, DV_A), jnp.float32),
                   jnp.zeros((bsz, 2, H_B, DK_B, DV_B), jnp.float32),
                   jnp.zeros((bsz, 2, H_C, DK_C, DV_C), jnp.float32),
                   jnp.zeros((bsz, 2, H_C, DK_C), jnp.float32),
                   jnp.zeros((bsz, 2, H_C), jnp.float32))
    new_gdn, new_hgrn, new_c, new_n, new_m = [], [], [], [], []
    h = x_prompt
    for l in range(DEPTH):
        mod = _adaln(c_ctx[None, :], w_mod[l], b_mod[l])
        h, st = _block(h, mod, zero_states, layer_params(l), lower[l], None)
        new_gdn.append(st[0].astype(x_prompt.dtype))
        new_hgrn.append(st[1].astype(x_prompt.dtype))
        new_c.append(st[2].astype(x_prompt.dtype))
        new_n.append(st[3].astype(x_prompt.dtype))
        new_m.append(st[4].astype(x_prompt.dtype))
    y_prompt = _rmsnorm(h, final_g)

    rows = x_sample.shape[1] // GRID_W
    z = x_sample
    for l in range(DEPTH):
        mod = _adaln(c, w_mod[l], b_mod[l])
        cached = (state_gdn[:, l], state_hgrn[:, l], state_mlstm_c[:, l], state_mlstm_n[:, l],
                  state_mlstm_m[:, l])
        z, _ = _block(z, mod, cached, layer_params(l), lower[l], rows)
    y_sample = _rmsnorm(z, final_g)

    return (y_prompt, y_sample, jnp.stack(new_gdn, axis=1), jnp.stack(new_hgrn, axis=1),
            jnp.stack(new_c, axis=1), jnp.stack(new_n, axis=1), jnp.stack(new_m, axis=1))


_drawn_inputs = setup_inputs


def setup_inputs(seed=0):
    import zlib

    import numpy as np

    out = dict(_drawn_inputs(seed))
    spreads = {}
    factors = {'state_hgrn': 8.0,
     'state_mlstm_c': 5.072,
     'state_mlstm_n': 8.0,
     'state_mlstm_m': 7.545,
     'gdn_norm_g': 24.14,
     'hgrn_norm_g': 25.279,
     'mlstm_norm_g': 34.79,
     'filt_freq': 2.948,
     'final_g': 7.261,
     'norm2_g': 2.848}
    for name, (base, spread) in spreads.items():
        noise = np.random.default_rng([zlib.crc32(name.encode()), seed]).standard_normal(out[name].shape)
        drawn = base * np.exp(spread * noise) if base else spread * noise
        out[name] = jnp.asarray(drawn.astype(out[name].dtype))
    for name, factor in factors.items():
        out[name] = (out[name] * factor).astype(out[name].dtype)
    return out
```

```python
import concourse.bass as bass
from concourse import mybir
from contextlib import ExitStack
import numpy as np

P = 128
D = 1024
KT = D // P
NT = 5
TOK = NT * P
SMP = 512
GW = 64
NE = 64
TOPK = 8
HD = 64
MW = 256
LV = 7
EPS = 1e-6
BIG = 1e30
TINY = 2.0 ** -63
IN_OFF = dict(qa=0, ka=256, va=512, ga=768, ab=1024, qb=1040, ib=1296, gb=1552, fb=1808,
              qc=2320, kc=2576, vc=2832, oc=3088, fi=3344, ud=3360)
CONST = ["ident", "ones", "blk", "strict", "run", "big", "after"]
CONST_W = dict(ident=P, ones=P, blk=P, strict=2 * LV * P, run=2 * (LV + 1) * P, big=2 * P, after=2 * P)


def shape_constants():
    a = np.arange(P)
    row, col = a[:, None], a[None, :]
    strict, run = np.zeros((P, 2, LV, P)), np.zeros((P, 2, LV + 1, P))
    for l in range(LV):
        s = 64 >> l
        same = row // (2 * s) == col // (2 * s)
        m = same & (row % (2 * s) < s) & (col % (2 * s) >= s)
        strict[:, 0, l], strict[:, 1, l] = m, m.T
        mid = (col // (2 * s)) * 2 * s + s
        first = col < mid
        run[:, 0, l] = np.where(first, (row > col) & (row < mid), (row >= mid) & (row <= col))
        run[:, 1, l] = np.where(first, (row >= col) & (row < mid), (row >= mid) & (row < col))
    run[:, 0, LV], run[:, 1, LV] = row <= col, row >= col
    big = np.stack([np.where(row <= col, 0, BIG), np.where(row >= col, 0, BIG)], 1)
    after = np.stack([row > col, row < col], 1)
    parts = dict(ident=np.eye(P), ones=np.ones((P, P)), blk=row // HD == col // HD, strict=strict,
                 run=run, big=big, after=after)
    masks = np.concatenate([np.asarray(parts[n], np.float32).reshape(P, -1) for n in CONST], 1)

    def dft(length):
        n = 2 * length
        t, f = np.arange(length)[:, None], np.arange(length)[None, :]
        th = 2 * np.pi * ((t * f) % n) / n
        re, im = np.cos(th), -np.sin(th)
        im[:, 0] = (-1.0) ** np.arange(length)
        w = np.where(np.arange(length) == 0, 1.0, 2.0)[None, :] / n
        wi = w.copy()
        fwd = np.concatenate([re, im], 1)
        inv = np.concatenate([(re * w).T, (im * wi).T], 0)
        return fwd, inv
    f5, i5 = dft(SMP)
    f1, i1 = dft(P)
    fwd5 = f5.reshape(4, P, 2 * SMP).transpose(1, 0, 2).reshape(P, -1)
    inv5 = i5.reshape(8, P, SMP).transpose(1, 0, 2).reshape(P, -1)
    inv1 = i1.reshape(2, P, P).transpose(1, 0, 2).reshape(P, -1)
    dfts = np.concatenate([fwd5, inv5, f1, inv1], 1).astype(np.float32)

    def positions(length):
        t = np.arange(length, dtype=np.float64)
        tn = np.linspace(0.0, 1.0, length).astype(np.float32).astype(np.float64)
        bands = np.linspace(1e-4, 15, 16).astype(np.float32).astype(np.float64)
        ang = ((2.0 * np.pi / length) * t[:, None]).astype(np.float32) * bands[None, :].astype(np.float32)
        ang = ang.astype(np.float64)
        feats = np.concatenate([tn[:, None], np.cos(ang), -np.sin(ang)], 1)
        deltas = np.abs(np.linspace(np.log(1e-2) / 1.5, np.log(1e-2) / 0.3, MW))
        dec = np.exp(-tn[:, None] * deltas[None, :])
        dec2 = dec.copy()
        dec2[0] = 0
        return feats, np.stack([dec, dec2], 1)
    (fa, da), (fb, db) = positions(SMP), positions(P)
    feats = np.ascontiguousarray(np.concatenate([fa, fb], 0).T).astype(np.float32)
    decay = np.concatenate([da, db], 0).reshape(NT, P, 2 * MW).transpose(1, 0, 2)
    decay = np.ascontiguousarray(decay).reshape(P, -1).astype(np.float32)
    return masks, dfts, feats, decay


def trunk_program(nc, T):
    F = mybir.dt.float32
    U32 = mybir.dt.uint32
    ALU = mybir.AluOpType
    ACT = mybir.ActivationFunctionType
    AX = mybir.AxisListType

    def spread(ap, axis, n):
        shape = list(ap.shape)
        shape.insert(axis, n)
        return ap.unsqueeze(axis).to_broadcast(shape)

    ctx = ExitStack()
    with ctx:
        def sb(name, words, parts=P):
            return ctx.enter_context(nc.sbuf_tensor(name, [parts, words], F))

        stage_sems = []

        def sem(name):
            stage_sems.append(nc.alloc_semaphore(name=name))
            return stage_sems[-1]

        class Steps:

            def __init__(self, eng, name):
                self.eng, self.n = eng, 0
                self.sem = sem(name)

            def done(self, ins):
                self.n += 1
                ins.then_inc(self.sem, 1)
                self.eng.wait_ge(self.sem, self.n)

        PS = ctx.enter_context(nc.psum_tensor("PS", [P, 8, 512], F))

        cst = sb("cst", sum(CONST_W.values()))
        at, off = {}, 0
        for n in CONST:
            at[n] = cst[:, off:off + CONST_W[n]]
            off += CONST_W[n]
        ident, ones, blk = at["ident"], at["ones"], at["blk"]
        strict = at["strict"].rearrange("p (d l n) -> p d l n", d=2, l=LV)
        run = at["run"].rearrange("p (d l n) -> p d l n", d=2, l=LV + 1)
        big = at["big"].rearrange("p (d n) -> p d n", d=2)
        after = at["after"].rearrange("p (d n) -> p d n", d=2)
        ARENA = 53200 - sum(CONST_W.values())
        arena = sb("arena", ARENA)
        top = [0]

        def region(words):
            a = top[0]
            top[0] += words
            assert top[0] <= ARENA, (top[0], ARENA)
            return a

        def part(start, words):
            return arena[:, start:start + words]

        x_at, y_at, r1_at, r2_at, r3_at = region(5120), region(5120), region(15360), region(19300), region(1500)
        par_at = region(ARENA - top[0])
        par_end = [par_at]

        def small(words):
            a = par_end[0]
            par_end[0] += words
            assert par_end[0] <= ARENA, par_end[0] - ARENA
            return part(a, words)

        xt = part(x_at, 5120).rearrange("p (t d) -> p t d", t=NT)
        yT = part(y_at, 5120).rearrange("p (k n) -> p k n", k=KT)
        hT = part(r1_at, 5120).rearrange("p (k n) -> p k n", k=KT)
        hTp = part(r1_at + 5120, 4096).rearrange("p (k n) -> p k n", k=KT)
        w_slot = [part(r1_at + 9216 + 2048 * i, 2048).rearrange("p (k n) -> p k n", k=KT) for i in range(3)]
        mod_slot = [part(r2_at + 8192 * i, 8192).rearrange("p (k n) -> p k n", k=KT) for i in range(2)]

        cond = small(16).rearrange("p (c k) -> p c k", c=2)
        scond = small(16).rearrange("p (k c) -> p k c", c=2)
        g1p, g2p = small(8), small(8)
        bmod = small(48).rearrange("p (j k) -> p j k", j=6)
        modT = small(96).rearrange("p (j k c) -> p j k c", j=6, k=KT)
        scl = small(16).rearrange("p (k c) -> p k c", c=2)
        sumsq, rstd = small(8), small(8)

        consts_in, x_in, x_back = sem("consts_in"), sem("x_in"), sem("x_back")
        cond_in, params_in, cond_silu = sem("cond_in"), sem("params_in"), sem("cond_silu")
        mod_in = [sem("mod_in0"), sem("mod_in1")]
        mod_ready, mod_taken, scl_ready = sem("mod_ready"), sem("mod_taken"), sem("scl_ready")
        sq1_done, root1, xn_done, xT_ready = sem("sq1_done"), sem("root1"), sem("xn_done"), sem("xT_ready")
        mean1, hT_smp, hT_pro, hTp_done = sem("mean1"), sem("hT_smp"), sem("hT_pro"), sem("hTp_done")
        junk = part(y_at, D)
        PRE_W = SMP + P + 6
        CONV_W = PRE_W - 4
        r2 = [r2_at]

        def keep(words):
            a = r2[0]
            r2[0] += words
            assert r2[0] <= r2_at + 19300
            return part(a, words)

        pre = keep(6 * PRE_W).rearrange("p (k n) -> p k n", k=6)
        qkT = keep(4 * TOK).rearrange("p (k n) -> p k n", k=4)
        vT = keep(2 * TOK).rearrange("p (k n) -> p k n", k=2)
        hqT = keep(2 * TOK).rearrange("p (k n) -> p k n", k=2)
        fgate = keep(NT * 512).rearrange("p (t n) -> p t n", t=NT)
        hv = keep(NT * MW).rearrange("p (t n) -> p t n", t=NT)
        mqkT = keep(4 * TOK).rearrange("p (k n) -> p k n", k=4)
        mv = keep(NT * 4 * 65).rearrange("p (t h n) -> p t h n", t=NT, h=4)
        hy = keep(4 * TOK).rearrange("p (k n) -> p k n", k=4)
        w_small = small(KT * 32).rearrange("p (k n) -> p k n", k=KT)
        smt = small(NT * 32).rearrange("p (t g h) -> p t g h", t=NT, g=8)
        GROUPS = [("qa", 0, "f"), ("ka", 0, "f"), ("va", 0, "f"), ("ga", 0, "f"), ("qb", 0, "f"), ("gb", 0, "f"),
                  ("ib", 0, "t"), ("fb", 0, "t"), ("fb", MW, "t"), ("qc", 0, "f"), ("kc", 0, "f"), ("oc", 0, "f"),
                  ("vc", 0, "t"), ("small", 0, "s"), ("ud", 0, "f"), ("ud", MW, "f"), ("ud", 2 * MW, "f")]
        OUTPUTS = [(g, i) for g, (_, _, kind) in enumerate(GROUPS) for i in range(2 if kind == "f" else NT)]
        slotted = [g for g, (_, _, kind) in enumerate(GROUPS) if kind != "s"]

        def outputs_before(g):
            return sum(1 for a, _ in OUTPUTS if a < g)

        w_in_sem = [sem(f"w_in{i}") for i in range(3)]
        small_in, proj_ready, proj_taken, pads_zero = sem("small_in"), sem("proj_ready"), sem("proj_taken"), sem("pads_zero")
        gdn_conv_read = sem("gdn_conv_read")
        ones_col, dve_beg = sem("ones_col"), sem("dve_beg")
        cbuf = part(x_at, 6 * CONV_W).rearrange("p (k n) -> p k n", k=6)
        sq = part(x_at, 4 * TOK)
        rq = part(x_at + 4 * TOK, 4 * TOK)
        o_tok = part(r1_at, 3 * NT * MW).rearrange("p (m t n) -> p m t n", m=3, t=NT)
        kv_tok = part(r1_at + 3840, NT * 512).rearrange("p (t n) -> p t n", t=NT)
        mh_tok = part(r1_at + 6400, NT * 512).rearrange("p (t n) -> p t n", t=NT)
        rows_in, rows_T, rows_zero, taps_ready = sem("rows_in"), sem("rows_T"), sem("rows_zero"), sem("taps_ready")
        rows = part(r2_at + 16700, 768)
        tapsT = small(60).rearrange("p (k r) -> p k r", k=6)
        prm_raw, prm = small(24), small(24)
        lb_row = part(x_at, 512)
        lbn = small(8)
        silu_done, sq_done, l2_sum, l2_eps, l2_root, k_unit = (sem(n) for n in
            ("silu_done", "sq_done", "l2_sum", "l2_eps", "l2_root", "k_unit"))
        hy_conv, hy_out, tr_ready, tr_taken, prm_in = (sem(n) for n in
            ("hy_conv", "hy_out", "tr_ready", "tr_taken", "prm_in"))
        softin, softabs, softexp, softlog, scal_ready, scal_ps = (sem(n) for n in
            ("softin", "softabs", "softexp", "softlog", "scal_ready", "scal_ps"))
        spi = small(NT * 16).rearrange("p (t g h) -> p t g h", t=NT, g=4)
        spa = small(NT * 16).rearrange("p (t g h) -> p t g h", t=NT, g=4)
        beta = small(NT * 8).rearrange("p (t d h) -> p t d h", t=NT, d=2)
        gl = small(NT * 16).rearrange("p (d t w h) -> p d t w h", d=2, t=NT, w=2)
        cs = small(NT * 16).rearrange("p (d t w h) -> p d t w h", d=2, t=NT, w=2)
        tot = small(NT * 16).rearrange("p (d t w h) -> p d t w h", d=2, t=NT, w=2)
        egc = small(NT * 8).rearrange("p (d t h) -> p d t h", d=2, t=NT)
        beg = small(NT * 8).rearrange("p (d t h) -> p d t h", d=2, t=NT)
        cc = small(NT * 8).rearrange("p (d t h) -> p d t h", d=2, t=NT)
        nalog = small(8)
        scal_done, egc_done, alog_exp, beta_done, fo_done = (sem(n) for n in
            ("scal_done", "egc_done", "alog_exp", "beta_done", "fo_done"))
        lb_in, lb_e, lb_work = sem("lb_in"), sem("lb_e"), sem("lb_work")
        lbt = [part(r3_at, 512), part(r3_at + 512, 512)]
        UNITS = [(0, 4, 1), (1, 4, 1)] + [(d, n if d == 0 else 3 - n, 0) for n in range(4) for d in range(2)]
        seen = set()
        FIRST = []
        for _, t, _ in UNITS:
            FIRST.append(t not in seen)
            seen.add(t)

        def last_token(d):
            return P - 1 if d == 0 else 0

        pool_area = {"u1": (r1_at + 8960, 6400), "u2": (x_at, 5120), "u3": (r3_at, 1500), "s": (r2_at, 3876)}
        used = {k: 0 for k in pool_area}

        def scratch(where, words):
            a, n = pool_area[where]
            used[where] += words
            assert used[where] <= n, (where, used[where])
            return part(a + used[where] - words, words)

        def heads(ap):
            return ap.rearrange("p (h n) -> p h n", h=4)

        gS = scratch("s", 4 * 2 * P).rearrange("p (s d pt n) -> p s d pt n", s=2, d=2, pt=2)
        hS = scratch("s", 4 * 2 * P).rearrange("p (s d pt n) -> p s d pt n", s=2, d=2, pt=2)
        mS = scratch("s", 4 * 260).rearrange("p (s d pt n) -> p s d pt n", s=2, d=2, pt=2)
        states_zero, states_in = sem("states_zero"), sem("states_in")

        gDG, gEGB, gX, gDT, gMT = (heads(scratch("u1", 512)) for _ in range(5))
        gMS = [heads(scratch("u1", 512)) for _ in range(2)]
        gAT, gT, gTT, gP, gBK = (heads(scratch("u1", 512)) for _ in range(5))
        gvn, gU, gwt, gwT, gqd, gkd = (scratch("u1" if i == 0 else "u2", 256).rearrange("p (pt n) -> p pt n", pt=2)
                                       for i in range(6))
        gel = scratch("u2", 4)
        (g_diag, g_row, g_egb, g_x, g_dt, g_kq, g_mt, g_at, g_ms, g_lv1, g_p, g_lv2, g_t, g_bk, g_uw, g_wt, g_wTr,
         g_wT, g_ws, g_vn, g_qd, g_eld, g_el, g_kd, g_o, g_st, g_otaken, g_staken) = (sem("g_" + n) for n in (
         "diag row egb x dt kq mt at ms lv1 p lv2 t bk uw wt wTr wT ws vn qd eld el kd o st otaken staken").split())

        def kq_banks(b):
            return PS[:, b:b + 2, 0:256]

        def by_par(ap):
            return ap.rearrange("p (par pt) n -> p par (pt n)", par=2)
        mDC, mWD = (heads(scratch("u3", 512)) for _ in range(2))
        mWT, mX = heads(scratch("s", 512)), heads(scratch("u2", 512))
        mqd, mkw = (scratch("u2", 256).rearrange("p (pt n) -> p pt n", pt=2) for _ in range(2))
        mtmp = scratch("u3", 256)
        mst = small(16).rearrange("p (s d h) -> p s d h", s=2, d=2)
        m_raw = small(8)
        mmx, mmu, mden = small(4), small(4), small(4)
        mex = small(12).rearrange("p (k h) -> p k h", k=3)
        (m_in, m_zero, m_dc, m_cb, m_qk, m_dmu, m_mb, m_x, m_eqx, m_sm, m_wd, m_eq, m_ex, m_wt, m_qd, m_kw, m_o, m_st,
         m_otaken, m_staken) = (sem("m_" + n) for n in
         "in zero dc cb qk dmu mb x eqx sm wd eq ex wt qd kw o st otaken staken".split())
        used["u1"] = 0
        hE = scratch("u1", 2 * (LV + 1) * P).rearrange("p (pt l n) -> p pt l n", pt=2, l=LV + 1)
        hQE = scratch("u1", 2 * (LV + 1) * P).rearrange("p (pt l n) -> p pt l n", pt=2, l=LV + 1)
        hKE = scratch("u1", 2 * LV * P).rearrange("p (pt l n) -> p pt l n", pt=2, l=LV)
        hAT = heads(scratch("u1", 512))
        hlt, hkt, hkT, hkd = (scratch("u2", 256) for _ in range(4))
        (h_lt, h_kt, h_x, h_kT, h_e, h_ek, h_kTs, h_qe, h_ke, h_kd, h_lvl, h_merge, h_o, h_st, h_otaken,
         h_staken) = (sem("h_" + n) for n in "lt kt x kT e ek kTs qe ke kd lvl merge o st otaken staken".split())
        norm_row = small(3 * HD).rearrange("p (m n) -> p m n", m=3)
        ho_ss = small(3 * 20)
        (n_in, n_sq, n_ss, n_root, n_on, n_tr, n_taken) = (sem("n_" + x) for x in "in sq ss root on tr taken".split())
        MIX = [0, 1, 2]
        sq_at = x_at + 3840
        osq = part(sq_at, NT * MW)
        osq4 = osq.rearrange("p (h n) -> p h n", n=HD)
        s_out = sem("s_out")

        with nc.Block() as block:

            @block.sync
            def _(sp):
                sp.dma_start(cond[:, 0, :], T["c"].rearrange("a (p k) -> p (a k)", k=KT)).then_inc(cond_in, 16)
                sp.dma_start(cond[:, 1, :], T["c_ctx"].rearrange("(p k) -> p k", k=KT)).then_inc(cond_in, 16)
                sp.dma_start(xt[:, 0:4, :], T["x_sample"].rearrange("a (t p) d -> p (a t) d", p=P)).then_inc(x_in, 16)
                sp.dma_start(xt[:, 4, :], T["x_prompt"].rearrange("a p d -> p (a d)")).then_inc(x_in, 16)
                wm = T["w_mod"].rearrange("a (p k) (j n) -> p j (a k) n", k=KT, j=6)
                for j in range(6):
                    if j >= 2:
                        sp.wait_ge(mod_ready, j - 1)
                    sp.dma_start(mod_slot[j % 2], wm[:, j]).then_inc(mod_in[j % 2], 16)
                    if j == 0:
                        sp.dma_start(g1p, T["norm1_g"].rearrange("a (p k) -> p (a k)", k=KT)).then_inc(params_in, 16)
                        sp.dma_start(g2p, T["norm2_g"].rearrange("a (p k) -> p (a k)", k=KT)).then_inc(params_in, 16)
                        sp.dma_start(bmod, T["b_mod"].rearrange("a (j p k) -> p (a j) k", j=6, k=KT)).then_inc(params_in, 16)
                        sp.dma_start(cst[:, :], T["masks"]).then_inc(consts_in, 16)
                sp.wait_ge(rows_zero, 1)
                sp.dma_start(rows[0:5, :], T["gdn_conv"].rearrange("a t n -> (a t) n")).then_inc(rows_in, 16)
                sp.dma_start(rows[5:8, :], T["hyena_conv"].rearrange("a t n -> (a t) n")).then_inc(rows_in, 16)
                sp.dma_start(rows[8:10, 0:MW], T["hyena_d"].rearrange("a t n -> (a t) n")).then_inc(rows_in, 16)
                for i, n in enumerate(("gdn_dt_bias", "gdn_a_log", "mlstm_f_bias")):
                    sp.dma_start(prm_raw[:, 8 * i:8 * i + 8],
                                 T[n].rearrange("a d h -> a (d h)").to_broadcast([P, 8])).then_inc(prm_in, 16)
                sp.dma_start(lbt[0], T["hgrn_lb_logits"].rearrange("a d n -> a (d n)").to_broadcast([P, 512])).then_inc(lb_in, 16)

                wi = T["w_in"].rearrange("a (p k) n -> p (a k) n", k=KT)
                sp.dma_start(w_small[:, :, 0:16], wi[:, :, IN_OFF["ab"]:IN_OFF["ab"] + 16]).then_inc(small_in, 16)
                sp.dma_start(w_small[:, :, 16:32], wi[:, :, IN_OFF["fi"]:IN_OFF["fi"] + 16]).then_inc(small_in, 16)
                for n, g in enumerate(slotted):
                    name, extra, _ = GROUPS[g]
                    if n >= 3:
                        sp.wait_ge(proj_ready, outputs_before(slotted[n - 3] + 1))
                    c0 = IN_OFF[name] + extra
                    sp.dma_start(w_slot[n % 3], wi[:, :, c0:c0 + MW]).then_inc(w_in_sem[n % 3], 16)
                    if n == 5:
                        pass
                sp.wait_ge(states_zero, 1)
                for name, S, w in (("state_gdn", gS, HD), ("state_hgrn", hS, HD), ("state_mlstm_c", mS, 65)):
                    for d in range(2):
                        for h in range(4):
                            par, pt = h % 2, h // 2
                            sp.dma_start(S[HD * par:HD * par + HD, 0, d, pt, w * par:w * par + HD],
                                         T[name][0, 0, d, h]).then_inc(states_in, 16)
                            if w == 65:
                                sp.dma_start(S[HD * par:HD * par + HD, 0, d, pt, w * par + HD:w * par + HD + 1],
                                             T["state_mlstm_n"][0, 0, d, h].rearrange("(n a) -> n a", a=1),
                                             allow_slow_non_contiguous=True).then_inc(states_in, 16)
                sp.dma_start(m_raw[:, :], T["state_mlstm_m"].rearrange("a b d h -> (a b) (d h)").to_broadcast([P, 8])).then_inc(m_in, 16)
                for m, n in enumerate(("gdn_norm_g", "hgrn_norm_g", "mlstm_norm_g")):
                    sp.dma_start(norm_row[:, m, :], T[n].to_broadcast([P, HD])).then_inc(n_in, 16)
                sp.wait_ge(g_staken, 2)
                sp.wait_ge(m_staken, 2)
                sp.wait_ge(h_staken, 2)
                for name, S, w in (("new_gdn", gS, HD), ("new_hgrn", hS, HD), ("new_c", mS, 65)):
                    for d in range(2):
                        for h in range(4):
                            par, pt = h % 2, h // 2
                            sp.dma_start(T[name][0, 0, d, h],
                                         S[HD * par:HD * par + HD, 1, d, pt, w * par:w * par + HD]).then_inc(s_out, 16)
                            if w == 65:
                                sp.dma_start(T["new_n"][0, 0, d, h].rearrange("(n a) -> n a", a=1),
                                             S[HD * par:HD * par + HD, 1, d, pt, w * par + HD:w * par + HD + 1],
                                             allow_slow_non_contiguous=True).then_inc(s_out, 16)
                                sp.dma_start(T["new_m"][0, 0, d:d + 1, h:h + 1],
                                             mst[0:1, 1, d, 2 * par + pt:2 * par + pt + 1]).then_inc(s_out, 16)
                sp.wait_ge(s_out, 16 * 40)


            @block.tensor
            def _(pe):
                def mod_block(j):
                    pe.wait_ge(mod_in[j % 2], 16 * (j // 2 + 1))
                    if j >= 2:
                        pe.wait_ge(mod_taken, j - 1)
                    for m in range(KT):
                        for k in range(KT):
                            mm = pe.matmul(PS[:, 6 + j % 2, 2 * m:2 * m + 2], mod_slot[j % 2][:, k, m:D:KT],
                                           scond[:, k, :], start=(k == 0), stop=(k == KT - 1))
                    mm.then_inc(mod_ready, 1)

                pe.wait_ge(cond_silu, 1)
                mod_block(0)
                mod_block(1)
                pe.wait_ge(consts_in, 16)
                pe.wait_ge(xn_done, NT)
                for k in range(KT):
                    if k >= 2:
                        pe.wait_ge(hT_smp, k - 1)
                        pe.wait_ge(hT_pro, k - 1)
                    for t in range(NT):
                        dst = PS[:, k % 2, t * P:(t + 1) * P] if t < 4 else PS[:, 2 + k % 2, 0:P]
                        mm = pe.transpose(dst, xt[:, t, k:D:KT], ident)
                    mm.then_inc(xT_ready, 1)
                for j in range(2, 6):
                    mod_block(j)
                pe.wait_ge(rows_in, 48)
                for k in range(6):
                    mm = pe.transpose(PS[:, 5, 16 * k:16 * k + 10], rows[0:10, k * P:(k + 1) * P], ident[0:10, 0:10])
                mm.then_inc(rows_T, 1)
                for n, (g, i) in enumerate(OUTPUTS):
                    name, extra, kind = GROUPS[g]
                    b0, b1 = 2 * (n % 4), 2 * (n % 4) + 1
                    if i == 0:
                        if kind == "s":
                            pe.wait_ge(small_in, 32)
                        else:
                            s = slotted.index(g)
                            pe.wait_ge(w_in_sem[s % 3], 16 * (s // 3 + 1))
                            w = w_slot[s % 3]
                    if n == 0:
                        pe.wait_ge(hT_smp, KT)
                        pe.wait_ge(hT_pro, KT)
                    if n == 2:
                        pe.wait_ge(taps_ready, 1)
                    if n == 3:
                        pe.wait_ge(mod_taken, 6)
                    if n >= 4:
                        pe.wait_ge(proj_taken, n - 3)
                    if kind == "f":
                        for k in range(KT):
                            pe.matmul(PS[:, b0, :], w[:, k, i * P:(i + 1) * P], hT[:, k, 0:SMP], start=(k == 0), stop=(k == KT - 1))
                        for k in range(KT):
                            mm = pe.matmul(PS[:, b1, 0:P], w[:, k, i * P:(i + 1) * P], hT[:, k, SMP:TOK],
                                           start=(k == 0), stop=(k == KT - 1))
                    else:
                        src = hTp if name in ("ib", "fb") and i < 4 else hT
                        if src is hTp:
                            pe.wait_ge(hTp_done, KT)
                        rhs = w_small if kind == "s" else w
                        for k in range(KT):
                            mm = pe.matmul(PS[:, b0, 0:rhs.shape[2]], src[:, k, i * P:(i + 1) * P], rhs[:, k, :],
                                           start=(k == 0), stop=(k == KT - 1))
                    mm.then_inc(proj_ready, 1)
                pe.wait_ge(proj_taken, len(OUTPUTS))
                pe.wait_ge(scal_ready, 1)
                for d in range(2):
                    pe.matmul(PS[:, 6, 40 * d:40 * d + 40], run[:, d, LV, :], gl[:, d].rearrange("p t w h -> p (t w h)"),
                              start=True, stop=True)
                pe.matmul(PS[:, 6, 128:208], ones, gl.rearrange("p d t w h -> p (d t w h)"), start=True, stop=True).then_inc(scal_ps, 1)
                pe.wait_ge(sq_done, 1)
                for i in range(5):
                    mm = pe.matmul(PS[:, i, :], blk, sq[:, i * 512:(i + 1) * 512], start=True, stop=True)
                mm.then_inc(l2_sum, 1)
                TR = [("kv", t) for t in range(NT)] + [("mh", t) for t in range(NT)]
                for n, (what, t) in enumerate(TR):
                    if n == 0:
                        pe.wait_ge(k_unit, 1)
                        pe.wait_ge(silu_done, 4)
                    if n == NT:
                        pe.wait_ge(hy_out, 2)
                    if n >= 4:
                        pe.wait_ge(tr_taken, n - 3)
                    c = slice(t * P, (t + 1) * P)
                    four = (qkT[:, 2, c], qkT[:, 3, c], vT[:, 0, c], vT[:, 1, c]) if what == "kv" else \
                           (mqkT[:, 2, c], mqkT[:, 3, c], hy[:, 0, c], hy[:, 1, c])
                    for j, src in enumerate(four):
                        mm = pe.transpose(PS[:, n % 4, j * P:(j + 1) * P], src, ident)
                    mm.then_inc(tr_ready, 1)
                for u, (d, t, s) in enumerate(UNITS):
                    c = slice(t * P, (t + 1) * P)
                    pe.wait_ge(g_diag, u + 1)
                    if u == 0:
                        pe.wait_ge(tr_taken, 2 * NT)
                        pe.wait_ge(l2_eps, 1)
                        pe.wait_ge(scal_done, 1)
                    else:
                        pe.wait_ge(g_otaken, u)
                        pe.wait_ge(g_staken, u)
                        pe.wait_ge(g_eld, u)
                    pe.matmul(PS[:, 0, :], ones, gDG.rearrange("p h n -> p (h n)"), start=True, stop=True).then_inc(g_row, 1)
                    for b, q in ((1, 2), (3, 0)):
                        for pt in range(2):
                            for par in range(2):
                                r = slice(HD * par, HD * par + HD)
                                mm = pe.matmul(PS[:, b + par, P * pt:P * pt + P], qkT[r, 2 + pt, c], qkT[r, q + pt, c],
                                               start=True, stop=True)
                    mm.then_inc(g_kq, 1)
                    for n in range(LV):
                        pe.wait_ge(g_ms, LV * u + n + 1)
                        if n > 0:
                            pe.wait_ge(g_t, LV * u + n)
                        for h in range(4):
                            mm = pe.matmul(PS[:, 5, P * h:P * h + P], gMS[n % 2][:, h, :], gT[:, h, :] if n else ident,
                                           start=True, stop=True)
                        mm.then_inc(g_lv1, 1)
                        pe.wait_ge(g_p, LV * u + n + 1)
                        if 0 < n < LV - 1:
                            for h in range(4):
                                pe.matmul(PS[:, 6, P * h:P * h + P], gTT[:, h, :], gP[:, h, :], start=True, stop=True)
                        for h in range(4):
                            mm = pe.matmul(PS[:, 7, P * h:P * h + P], gP[:, h, :], gTT[:, h, :] if n else ident,
                                           start=True, stop=True)
                        mm.then_inc(g_lv2, 1)
                    pe.wait_ge(g_t, LV * (u + 1))
                    pe.wait_ge(g_bk, u + 1)
                    for h in range(4):
                        mm = pe.matmul(PS[:, 5, P * h:P * h + P], gTT[:, h, :], gBK[:, h, :], start=True, stop=True)
                    mm.then_inc(g_uw, 1)
                    pe.wait_ge(g_wt, u + 1)
                    for pt in range(2):
                        mm = pe.transpose(PS[:, 6, P * pt:P * pt + P], gwt[:, pt, :], ident)
                    mm.then_inc(g_wTr, 1)
                    pe.wait_ge(g_wT, u + 1)
                    if u == 0:
                        pe.wait_ge(states_zero, 1)
                    if s == 0 and u < 4:
                        pe.wait_ge(states_in, 16 * 32)
                    for pt in range(2):
                        mm = pe.matmul(PS[:, 7, P * pt:P * pt + P], gwT[:, pt, :], gS[:, s, d, pt, :], start=True, stop=True)
                    mm.then_inc(g_ws, 1)
                    pe.wait_ge(g_vn, u + 1)
                    pe.wait_ge(g_qd, u + 1)
                    pe.wait_ge(g_at, u + 1)
                    for pt in range(2):
                        pe.matmul(PS[:, 1, P * pt:P * pt + P], gqd[:, pt, :], gS[:, s, d, pt, :], start=True, stop=False)
                        for par in range(2):
                            o = P * pt + HD * par
                            mm = pe.matmul(PS[:, 1, o:o + HD], gAT[:, 2 * par + pt, :], gvn[:, pt, HD * par:HD * par + HD],
                                           start=False, stop=par == 1)
                    mm.then_inc(g_o, 1)
                    pe.wait_ge(g_kd, u + 1)
                    for pt in range(2):
                        mm = pe.matmul(PS[:, 2, P * pt:P * pt + P], gkd[:, pt, :], gvn[:, pt, :], start=True, stop=True)
                    mm.then_inc(g_st, 1)
                for u, (d, t, s) in enumerate(UNITS):
                    c = slice(t * P, (t + 1) * P)
                    pe.wait_ge(m_dc, u + 1)
                    if u == 0:
                        pe.wait_ge(g_otaken, len(UNITS))
                        pe.wait_ge(g_staken, len(UNITS))
                    else:
                        pe.wait_ge(m_otaken, u)
                        pe.wait_ge(m_staken, u)
                    pe.matmul(PS[:, 0, :], ones, mDC.rearrange("p h n -> p (h n)"), start=True, stop=True).then_inc(m_cb, 1)
                    for pt in range(2):
                        for par in range(2):
                            r = slice(HD * par, HD * par + HD)
                            mm = pe.matmul(PS[:, 2 + par, P * pt:P * pt + P], mqkT[r, 2 + pt, c], mqkT[r, pt, c],
                                           start=True, stop=True)
                    mm.then_inc(m_qk, 1)
                    pe.wait_ge(m_dmu, u + 1)
                    pe.matmul(PS[:, 1, :], ones, mDC.rearrange("p h n -> p (h n)"), start=True, stop=True).then_inc(m_mb, 1)
                    pe.wait_ge(m_qd, u + 1)
                    pe.wait_ge(m_wt, u + 1)
                    if u == 0:
                        pe.wait_ge(ones_col, 1)
                    if s == 0 and u < 4:
                        pe.wait_ge(states_in, 16 * 32)
                    for pt in range(2):
                        pe.matmul(PS[:, 4, 130 * pt:130 * pt + 130], mqd[:, pt, :], mS[:, s, d, pt, :], start=True, stop=False)
                        for par in range(2):
                            o = 130 * pt + 65 * par
                            mm = pe.matmul(PS[:, 4, o:o + 65], mWT[:, 2 * par + pt, :], mv[:, t, 2 * pt + par, :],
                                           start=False, stop=par == 1)
                    mm.then_inc(m_o, 1)
                    pe.wait_ge(m_kw, u + 1)
                    for pt in range(2):
                        mm = pe.matmul(PS[:, 5, 130 * pt:130 * pt + 130], mkw[:, pt, :],
                                       mv[:, t, 2 * pt:2 * pt + 2, :].rearrange("p h n -> p (h n)"), start=True, stop=True)
                    mm.then_inc(m_st, 1)
                for u, (d, t, s) in enumerate(UNITS):
                    c = slice(t * P, (t + 1) * P)
                    pe.wait_ge(h_lt, u + 1)
                    if u == 0:
                        pe.wait_ge(m_otaken, len(UNITS))
                        pe.wait_ge(m_staken, len(UNITS))
                        pe.wait_ge(g_staken, len(UNITS))
                    else:
                        pe.wait_ge(h_otaken, u)
                        pe.wait_ge(h_staken, u)
                    for pt in range(2):
                        for half in range(2):
                            pe.matmul(PS[:, 2 * pt + half, :], hlt[:, P * pt:P * pt + P],
                                      run[:, d, 4 * half:4 * half + 4, :].rearrange("p l n -> p (l n)"), start=True, stop=True)
                    pe.matmul(PS[:, 5, 0:256], after[:, d, :], hlt, start=True, stop=True).then_inc(h_x, 1)
                    pe.wait_ge(h_kt, u + 1)
                    for pt in range(2):
                        mm = pe.transpose(PS[:, 4, P * pt:P * pt + P], hkt[:, P * pt:P * pt + P], ident)
                    mm.then_inc(h_kT, 1)
                    for r in range(LV + 1):
                        if r == 0:
                            pe.wait_ge(h_kTs, u + 1)
                            pe.wait_ge(h_ek, u + 1)
                        if r == 1:
                            pe.wait_ge(h_ke, u + 1)
                            pe.wait_ge(h_qe, u + 1)
                        if r >= 2:
                            pe.wait_ge(h_merge, (LV + 1) * u + r - 1)
                        for pt in range(2):
                            for par in range(2):
                                q = slice(HD * par, HD * par + HD)
                                k_, q_ = (hkT[q, P * pt:P * pt + P], hqT[q, pt, c]) if r == 0 else \
                                         (hKE[q, pt, r - 1, :], hQE[q, pt, r - 1, :])
                                mm = pe.matmul(PS[:, 4 + 2 * (r % 2) + par, P * pt:P * pt + P], k_, q_, start=True, stop=True)
                        mm.then_inc(h_lvl, 1)
                    pe.wait_ge(h_merge, (LV + 1) * (u + 1))
                    for pt in range(2):
                        pe.matmul(PS[:, 6, P * pt:P * pt + P], hQE[:, pt, LV, :], hS[:, s, d, pt, :], start=True, stop=False)
                        for par in range(2):
                            o = P * pt + HD * par
                            mm = pe.matmul(PS[:, 6, o:o + HD], hAT[:, 2 * par + pt, :], hv[:, t, o:o + HD],
                                           start=False, stop=par == 1)
                    mm.then_inc(h_o, 1)
                    pe.wait_ge(h_kd, u + 1)
                    for pt in range(2):
                        mm = pe.matmul(PS[:, 7, P * pt:P * pt + P], hkd[:, P * pt:P * pt + P], hv[:, t, P * pt:P * pt + P],
                                       start=True, stop=True)
                    mm.then_inc(h_st, 1)
                for i, m in enumerate(MIX):
                    pe.wait_ge(n_on, i + 1)
                    for pt in range(2):
                        if i > 0:
                            pe.wait_ge(n_taken, 2 * (i - 1) + pt + 1)
                        for t in range(NT):
                            dst = PS[:, 2 * pt, t * P:(t + 1) * P] if t < 4 else PS[:, 2 * pt + 1, 0:P]
                            mm = pe.transpose(dst, o_tok[:, m, t, P * pt:P * pt + P], ident)
                        mm.then_inc(n_tr, 1)


            @block.vector
            def _(dve):
                dve_order = Steps(dve, "dve_order1")
                def mod_take(j):
                    dve.wait_ge(mod_ready, j + 1)
                    dve.tensor_tensor(modT[:, j], PS[:, 6 + j % 2, 0:16].rearrange("p (k c) -> p k c", c=2),
                                      spread(bmod[:, j], 2, 2), ALU.add).then_inc(mod_taken, 1)

                dve.wait_ge(sq1_done, 1)
                dve.tensor_scalar(sumsq[:, 0:NT], sumsq[:, 0:NT], 1.0 / D, EPS, ALU.mult, ALU.add).then_inc(mean1, 1)
                dve.wait_ge(root1, 1)
                dve_order.done(dve.reciprocal(rstd[:, 0:NT], rstd[:, 0:NT]))
                for t in range(NT):
                    dve.tensor_scalar(xt[:, t, :], xt[:, t, :], rstd[:, t:t + 1], None, ALU.mult).then_inc(xn_done, 1)
                dve.wait_ge(params_in, 48)
                mod_take(0)
                mod_take(1)
                dve.wait_ge(mod_taken, 2)
                dve_order.done(dve.tensor_scalar(scl[:, :, :], modT[:, 1], 1.0, None, ALU.add))
                dve.tensor_tensor(scl[:, :, :], scl[:, :, :], spread(g1p, 2, 2), ALU.mult).then_inc(scl_ready, 1)
                dve.wait_ge(scl_ready, 1)
                for k in range(KT):
                    dve.wait_ge(xT_ready, k + 1)
                    dve.tensor_scalar(hT[:, k, 0:SMP], PS[:, k % 2, :], scl[:, k, 0:1], modT[:, 0, k, 0:1], ALU.mult,
                                      ALU.add).then_inc(hT_smp, 1)
                for j in range(2, 6):
                    mod_take(j)
                dve.wait_ge(rows_T, 1)
                dve.tensor_copy(tapsT[:, :, :], PS[:, 5, 0:96].rearrange("p (k r) -> p k r", k=6)[:, :, 0:10]).then_inc(taps_ready, 1)
                dve.wait_ge(prm_in, 48)
                dve_order.done(dve.tensor_copy(prm.rearrange("p (g par pt) -> p g par pt", g=6, par=2),
                                               prm_raw.rearrange("p (g pt par) -> p g par pt", g=6, par=2)))
                dve.wait_ge(lb_in, 16)
                dve.tensor_tensor(lbt[1], lbt[0], lbt[0], ALU.subtract).then_inc(lb_work, 1)
                dve.wait_ge(lb_e, 1)
                dve_order.done(dve.reciprocal(lbt[1], lbt[0]))
                dve_order.done(dve.tensor_tensor(lbt[0], lbt[0], lbt[1], ALU.mult))
                dve_order.done(dve.tensor_tensor(lbt[0], lbt[0], lbt[0], ALU.subtract))
                dve_order.done(dve.tensor_scalar(lbt[1], lbt[0], -1.0, 1.0, ALU.mult, ALU.add))

                dve.wait_ge(proj_taken, 6)
                dve.wait_ge(taps_ready, 1)
                for tap in range(5):
                    for k in range(6):
                        src = pre[:, k, tap:tap + CONV_W]
                        if tap == 0:
                            i = dve.tensor_scalar(cbuf[:, k, :], src, tapsT[:, k, 0:1], None, ALU.mult)
                        else:
                            i = dve.scalar_tensor_tensor(out=cbuf[:, k, :], in0=src, scalar=tapsT[:, k, tap:tap + 1],
                                                         in1=cbuf[:, k, :], op0=ALU.mult, op1=ALU.add)
                    if tap < 4:
                        dve_order.done(i)
                i.then_inc(gdn_conv_read, 1)

                dve.wait_ge(proj_taken, outputs_before(14))
                for g in range(2):
                    dve.tensor_tensor(spi[:, :, g, :], smt[:, :, g, :], spread(prm[:, 4 * g:4 * g + 4], 1, NT), ALU.add)
                    i = dve.tensor_tensor(spi[:, :, 2 + g, :], smt[:, :, 6 + g, :], spread(prm[:, 16 + 4 * g:20 + 4 * g], 1, NT), ALU.add)
                dve_order.done(i)
                dve.tensor_scalar(spi[:, :, 2:4, :], spi[:, :, 2:4, :], -1.0, None, ALU.mult).then_inc(softin, 1)
                for t in range(NT):
                    i = dve.scalar_tensor_tensor(out=fgate[:, t, :], in0=fgate[:, t, :], scalar=TINY, in1=lbt[1],
                                                 op0=ALU.max, op1=ALU.mult)
                dve_order.done(i)
                for t in range(NT):
                    i = dve.tensor_tensor(fgate[:, t, :], fgate[:, t, :], lbt[0], ALU.add)
                i.then_inc(fo_done, 1)
                dve.wait_ge(softlog, 1)
                for d in range(2):
                    for w in range(2):
                        i = dve.scalar_tensor_tensor(out=gl[:, d, :, w, :], in0=spi[:, :, 2 * w + d, :], scalar=0.0,
                                                     in1=spa[:, :, 2 * w + d, :], op0=ALU.max, op1=ALU.add)
                dve_order.done(i)
                dve.wait_ge(alog_exp, 1)
                for d in range(2):
                    dve.tensor_scalar(gl[:, d, :, 1, :], gl[:, d, :, 1, :], -1.0, None, ALU.mult)
                    i = dve.scalar_tensor_tensor(out=gl[:, d, :, 0, :], in0=gl[:, d, :, 0, :], scalar=-1.0,
                                                 in1=spread(nalog[:, 4 * d:4 * d + 4], 1, NT), op0=ALU.mult, op1=ALU.mult)
                i.then_inc(scal_ready, 1)
                dve.wait_ge(scal_ps, 1)
                dve.tensor_copy(cs.rearrange("p d t w h -> p (d t w h)"), PS[:, 6, 0:80])
                dve.tensor_copy(tot.rearrange("p d t w h -> p (d t w h)"), PS[:, 6, 128:208]).then_inc(scal_done, 1)
                dve.wait_ge(scal_done, 1)
                dve.wait_ge(egc_done, 1)
                dve.wait_ge(beta_done, 1)
                for d in range(2):
                    dve.tensor_tensor(beg[:, d], egc[:, d], beta[:, :, d, :], ALU.mult)
                    i = dve.tensor_tensor(cc[:, d], smt[:, :, 4 + d, :], cs[:, d, :, 1, :], ALU.subtract)
                i.then_inc(dve_beg, 1)

                dve.wait_ge(l2_sum, 1)
                for i5 in range(5):
                    i = dve.tensor_scalar(rq[:, i5 * 512:(i5 + 1) * 512], PS[:, i5, :], EPS, None, ALU.add)
                i.then_inc(l2_eps, 1)
                dve.wait_ge(l2_root, 1)
                dve_order.done(dve.reciprocal(rq, rq))
                qk_flat = qkT.rearrange("p k n -> p (k n)")
                dve.scalar_tensor_tensor(out=qk_flat[:, 0:2 * TOK], in0=qk_flat[:, 0:2 * TOK], scalar=HD ** -0.5,
                                         in1=rq[:, 0:2 * TOK], op0=ALU.mult, op1=ALU.mult)
                dve.tensor_tensor(qk_flat[:, 2 * TOK:], qk_flat[:, 2 * TOK:], rq[:, 2 * TOK:], ALU.mult).then_inc(k_unit, 1)

                dve.wait_ge(proj_taken, len(OUTPUTS))
                dve.wait_ge(k_unit, 1)
                for tap in range(3):
                    for k in range(6):
                        src = pre[:, k, tap + 1:tap + 1 + CONV_W]
                        if tap == 0:
                            i = dve.tensor_scalar(cbuf[:, k, :], src, tapsT[:, k, 5:6], None, ALU.mult)
                        else:
                            i = dve.scalar_tensor_tensor(out=cbuf[:, k, :], in0=src, scalar=tapsT[:, k, 5 + tap:6 + tap],
                                                         in1=cbuf[:, k, :], op0=ALU.mult, op1=ALU.add)
                    if tap < 2:
                        dve_order.done(i)
                i.then_inc(hy_conv, 1)
                for u, (d, t, s) in enumerate(UNITS):
                    c = slice(t * P, (t + 1) * P)
                    gc = cs[:, d, t, 0, :]
                    end = last_token(d)
                    if u == 0:
                        dve.wait_ge(hy_out, 2)
                        dve.wait_ge(proj_ready, len(OUTPUTS))
                    dve.tensor_tensor(gDG, spread(ident, 1, 4), spread(gc, 2, P), ALU.mult).then_inc(g_diag, 1)
                    dve.wait_ge(g_row, u + 1)
                    row = heads(PS[:, 0, :])
                    dve.tensor_tensor(gel, row[:, :, end:end + 1].rearrange("p h a -> p (h a)"), gc, ALU.subtract).then_inc(g_eld, 1)
                    dve_order.done(dve.tensor_tensor(gX, spread(gc, 2, P), row, ALU.subtract))
                    dve.scalar_tensor_tensor(out=gX, in0=gX, scalar=0.0, in1=spread(big[:, d, :], 1, 4),
                                             op0=ALU.max, op1=ALU.add).then_inc(g_x, 1)
                    dve.wait_ge(g_dt, u + 1)
                    dve.wait_ge(g_kq, u + 1)
                    dve.tensor_tensor(by_par(gMT), kq_banks(1), by_par(gDT), ALU.mult).then_inc(g_mt, 1)
                    dve.tensor_tensor(by_par(gAT), kq_banks(3), by_par(gDT), ALU.mult).then_inc(g_at, 1)
                    dve.wait_ge(g_egb, u + 1)
                    for par in range(2):
                        r = slice(HD * par, HD * par + HD)
                        i = dve.tensor_tensor(gqd[r], qkT[r, 0:2, c], gEGB[r, 2 * par:2 * par + 2, :], ALU.mult)
                    i.then_inc(g_qd, 1)
                    for n in range(LV):
                        dve.wait_ge(g_lv1, LV * u + n + 1)
                        dve.tensor_tensor(gP, heads(PS[:, 5, :]), spread(beta[:, t, d, :], 2, P), ALU.mult).then_inc(g_p, 1)
                        dve.wait_ge(g_lv2, LV * u + n + 1)
                        if n == 0:
                            dve.wait_ge(g_p, LV * u + 1)
                            dve.tensor_tensor(gT, spread(ident, 1, 4), gP, ALU.subtract)
                            dve.tensor_tensor(gTT, spread(ident, 1, 4), heads(PS[:, 7, :]), ALU.subtract).then_inc(g_t, 1)
                        else:
                            dve.wait_ge(g_t, LV * u + n)
                            if n < LV - 1:
                                dve.tensor_tensor(gT, gT, heads(PS[:, 6, :]), ALU.subtract)
                            dve.tensor_tensor(gTT, gTT, heads(PS[:, 7, :]), ALU.subtract).then_inc(g_t, 1)
                    dve.wait_ge(g_ws, u + 1)
                    dve.tensor_tensor(gvn.rearrange("p pt n -> p (pt n)"), gU.rearrange("p pt n -> p (pt n)"), PS[:, 7, 0:256],
                                      ALU.add).then_inc(g_vn, 1)
                    dve.wait_ge(g_o, u + 1)
                    if FIRST[u]:
                        dve.tensor_copy(o_tok[:, 0, t, :], PS[:, 1, 0:256]).then_inc(g_otaken, 1)
                    else:
                        dve.tensor_tensor(o_tok[:, 0, t, :], o_tok[:, 0, t, :], PS[:, 1, 0:256], ALU.add).then_inc(g_otaken, 1)
                    dve.wait_ge(g_st, u + 1)
                    for pt in range(2):
                        for par in range(2):
                            r, n = slice(HD * par, HD * par + HD), HD * par
                            i = dve.scalar_tensor_tensor(out=gS[r, s, d, pt, n:n + HD], in0=gS[r, s, d, pt, n:n + HD],
                                                         scalar=gEGB[r, 2 * par + pt, end:end + 1],
                                                         in1=PS[r, 2, P * pt + n:P * pt + n + HD], op0=ALU.mult, op1=ALU.add)
                    i.then_inc(g_staken, 1)
                dve.wait_ge(m_in, 16)
                dve_order.done(dve.tensor_copy(mst[:, 0].rearrange("p d (par pt) -> p d par pt", par=2),
                                               m_raw.rearrange("p (d pt par) -> p d par pt", d=2, pt=2)))
                dve.wait_ge(m_zero, 1)
                for u, (d, t, s) in enumerate(UNITS):
                    c = slice(t * P, (t + 1) * P)
                    cj, m0, end = cc[:, d, t, :], mst[:, s, d, :], last_token(d)
                    dve.tensor_tensor(mDC, spread(ident, 1, 4), spread(cj, 2, P), ALU.mult).then_inc(m_dc, 1)
                    dve.wait_ge(m_cb, u + 1)
                    dve_order.done(dve.tensor_tensor(mX, heads(PS[:, 0, :]), spread(big[:, 1 - d, :], 1, 4), ALU.subtract))
                    dve_order.done(dve.tensor_reduce(mmx, mX, AX.X, ALU.max))
                    dve_order.done(dve.tensor_tensor(mmu, mmx, m0, ALU.max))
                    dve.tensor_tensor(mDC, spread(ident, 1, 4), spread(mmu, 2, P), ALU.mult).then_inc(m_dmu, 1)
                    dve.wait_ge(m_mb, u + 1)
                    row = heads(PS[:, 1, :])
                    row_end = row[:, :, end:end + 1].rearrange("p h a -> p (h a)")
                    dve.tensor_tensor(mex[:, 0, :], cj, row_end, ALU.subtract)
                    dve.tensor_tensor(mex[:, 1, :], m0, row_end, ALU.subtract)
                    dve.scalar_tensor_tensor(out=mex[:, 2, :], in0=cs[:, d, t, 1, :], scalar=-1.0, in1=mmu, op0=ALU.mult,
                                             op1=ALU.subtract).then_inc(m_sm, 1)
                    dve_order.done(dve.tensor_tensor(mX, row, spread(cj, 2, P), ALU.subtract))
                    dve.scalar_tensor_tensor(out=mX, in0=mX, scalar=0.0, in1=spread(big[:, d, :], 1, 4),
                                             op0=ALU.max, op1=ALU.add).then_inc(m_x, 1)
                    dve.tensor_tensor(mDC, row, spread(m0, 2, P), ALU.subtract).then_inc(m_eqx, 1)
                    dve.wait_ge(m_eq, u + 1)
                    dve.tensor_tensor(m0, tot[:, d, t, 1, :], row_end, ALU.add)
                    for par in range(2):
                        r = slice(HD * par, HD * par + HD)
                        i = dve.tensor_tensor(mqd[r], mqkT[r, 0:2, c], mDC[r, 2 * par:2 * par + 2, :], ALU.mult)
                    i.then_inc(m_qd, 1)
                    dve.wait_ge(m_wd, u + 1)
                    dve.wait_ge(m_qk, u + 1)
                    dve.tensor_tensor(by_par(mWT), kq_banks(2), by_par(mWD), ALU.mult).then_inc(m_wt, 1)
                    dve.wait_ge(m_ex, u + 1)
                    dve.wait_ge(m_o, u + 1)
                    num = PS[:, 4, 0:260].rearrange("p (h n) -> p h n", h=4)
                    den = num[:, :, HD:HD + 1].rearrange("p h a -> p (h a)")
                    dve_order.done(dve.tensor_scalar(mden, den, -1.0, None, ALU.mult))
                    dve_order.done(dve.tensor_tensor(mden, mden, den, ALU.max))
                    dve_order.done(dve.tensor_tensor(mden.rearrange("p (pt par) -> p pt par", pt=2),
                                                     mden.rearrange("p (pt par) -> p pt par", pt=2),
                                                     mex[:, 2, :].rearrange("p (par pt) -> p pt par", par=2), ALU.max))
                    dve_order.done(dve.reciprocal(mden, mden))
                    out = heads(o_tok[:, 2, t, :])
                    if FIRST[u]:
                        dve.tensor_tensor(out, num[:, :, 0:HD], spread(mden, 2, HD), ALU.mult).then_inc(m_otaken, 1)
                    else:
                        dve.tensor_tensor(heads(mtmp), num[:, :, 0:HD], spread(mden, 2, HD), ALU.mult).then_inc(m_otaken, 1)
                        dve.wait_ge(m_otaken, u + 1)
                        dve.tensor_tensor(out, out, heads(mtmp), ALU.add)
                    dve.wait_ge(m_st, u + 1)
                    for pt in range(2):
                        for par in range(2):
                            r, n = slice(HD * par, HD * par + HD), 65 * par
                            i = dve.scalar_tensor_tensor(out=mS[r, s, d, pt, n:n + 65], in0=mS[r, s, d, pt, n:n + 65],
                                                         scalar=mex[r, 1, 2 * par + pt:2 * par + pt + 1],
                                                         in1=PS[r, 5, 130 * pt + n:130 * pt + n + 65], op0=ALU.mult, op1=ALU.add)
                    i.then_inc(m_staken, 1)
                    dve.wait_ge(m_staken, u + 1)
                for u, (d, t, s) in enumerate(UNITS):
                    c = slice(t * P, (t + 1) * P)
                    end = last_token(d)
                    dve.wait_ge(h_e, u + 1)
                    for pt in range(2):
                        i = dve.tensor_tensor(hQE[:, pt], spread(hqT[:, pt, c], 1, LV + 1), hE[:, pt], ALU.mult)
                    i.then_inc(h_qe, 1)
                    A4 = hAT.rearrange("p (par pt) n -> p par pt n", par=2)
                    for r in range(LV + 1):
                        dve.wait_ge(h_lvl, (LV + 1) * u + r + 1)
                        b = 4 + 2 * (r % 2)
                        src = PS[:, b:b + 2, 0:256].rearrange("p par (pt n) -> p par pt n", pt=2)
                        if r == 0:
                            dve.tensor_tensor(A4, src, spread(spread(ident, 1, 2), 1, 2), ALU.mult).then_inc(h_merge, 1)
                        else:
                            dve.wait_ge(h_merge, (LV + 1) * u + r)
                            mask = strict[:, d, r - 1, :].bitcast(U32)
                            dve.copy_predicated(A4, spread(spread(mask, 1, 2), 1, 2), src).then_inc(h_merge, 1)
                    dve.wait_ge(h_o, u + 1)
                    if FIRST[u]:
                        dve.tensor_copy(o_tok[:, 1, t, :], PS[:, 6, 0:256]).then_inc(h_otaken, 1)
                    else:
                        dve.tensor_tensor(o_tok[:, 1, t, :], o_tok[:, 1, t, :], PS[:, 6, 0:256], ALU.add).then_inc(h_otaken, 1)
                    dve.wait_ge(h_st, u + 1)
                    for pt in range(2):
                        for par in range(2):
                            r, n = slice(HD * par, HD * par + HD), HD * par
                            i = dve.scalar_tensor_tensor(out=hS[r, s, d, pt, n:n + HD], in0=hS[r, s, d, pt, n:n + HD],
                                                         scalar=hE[r, pt, LV, end:end + 1],
                                                         in1=PS[r, 7, P * pt + n:P * pt + n + HD], op0=ALU.mult, op1=ALU.add)
                    i.then_inc(h_staken, 1)

                for i, m in enumerate(MIX):
                    o = o_tok[:, m].rearrange("p t n -> p (t n)")
                    o4 = o.rearrange("p (h n) -> p h n", n=HD)
                    ss = ho_ss[:, 20 * m:20 * m + 20]
                    dve.wait_ge((g_otaken, h_otaken, m_otaken)[m], len(UNITS))
                    if i == 0:
                        dve.wait_ge(n_in, 48)
                    dve_order.done(dve.tensor_tensor(osq, o, o, ALU.mult))
                    dve_order.done(dve.tensor_reduce(ss, osq4, AX.X, ALU.add))
                    dve.tensor_scalar(ss, ss, 1.0 / HD, EPS, ALU.mult, ALU.add).then_inc(n_ss, 1)
                    dve.wait_ge(n_root, i + 1)
                    dve_order.done(dve.reciprocal(ss, ss))
                    dve_order.done(dve.tensor_tensor(o4, o4, spread(ss, 2, HD), ALU.mult))
                    dve.tensor_tensor(o4, o4, spread(norm_row[:, m, :], 1, 20), ALU.mult).then_inc(n_on, 1)
                    for pt in range(2):
                        dve.wait_ge(n_tr, 2 * i + pt + 1)
                        y = yT[:, 2 * m + pt, :]
                        b = 2 * pt
                        if m == 1:
                            dst = y[:, 0:SMP].rearrange("p (r w) -> p w r", w=GW)
                            src = PS[:, b, :].rearrange("p (w r) -> p w r", r=SMP // GW)
                        else:
                            dst, src = y[:, 0:SMP], PS[:, b, :]
                        dve.tensor_tensor(dst, dst, src, ALU.mult)
                        dve.tensor_tensor(y[:, SMP:TOK], y[:, SMP:TOK], PS[:, b + 1, 0:P], ALU.mult).then_inc(n_taken, 1)

            @block.scalar
            def _(act):
                act_order = Steps(act, "act_order1")
                act.wait_ge(cond_in, 32)
                act.activation(scond[:, :, :].rearrange("p k c -> p c k"), cond[:, :, :], ACT.Silu).then_inc(cond_silu, 1)
                act.wait_ge(x_in, 32)
                for t in range(NT):
                    i = act.activation(junk, xt[:, t, :], ACT.Square, accum_out=sumsq[:, t:t + 1])
                    if t < NT - 1:
                        act_order.done(i)
                i.then_inc(sq1_done, 1)
                act.wait_ge(mean1, 1)
                act.activation(rstd[:, 0:NT], sumsq[:, 0:NT], ACT.Sqrt).then_inc(root1, 1)
                for k in range(KT):
                    act.wait_ge(xT_ready, k + 1)
                    act.wait_ge(scl_ready, 1)
                    act.activation(hT[:, k, SMP:TOK], PS[:, 2 + k % 2, 0:P], ACT.Identity, scale=scl[:, k, 1:2],
                                   bias=modT[:, 0, k, 1:2]).then_inc(hT_pro, 1)
                act.wait_ge(lb_work, 1)
                act.activation(lbt[0], lbt[1], ACT.Exp).then_inc(lb_e, 1)
                def leave(dst_s, dst_p, b0, func, scale=1.0):
                    act.activation(dst_s, PS[:, b0, :], func, scale=scale)
                    act.activation(dst_p, PS[:, b0 + 1, 0:P], func, scale=scale).then_inc(proj_taken, 1)

                PRO = slice(SMP + 2, SMP + 2 + P)

                def silu_qkv():
                    act.wait_ge(gdn_conv_read, 1)
                    act.activation(qkT[:, :, 0:SMP], cbuf[:, 0:4, 0:SMP], ACT.Silu).then_inc(silu_done, 1)
                    act.activation(qkT[:, :, SMP:TOK], cbuf[:, 0:4, PRO], ACT.Silu).then_inc(silu_done, 1)
                    act.activation(vT[:, :, 0:SMP], cbuf[:, 4:6, 0:SMP], ACT.Silu).then_inc(silu_done, 1)
                    act.activation(vT[:, :, SMP:TOK], cbuf[:, 4:6, PRO], ACT.Silu).then_inc(silu_done, 1)

                GATE_AT = dict(ga=0, gb=2, oc=4)
                for n, (g, i) in enumerate(OUTPUTS):
                    name, extra, kind = GROUPS[g]
                    b0 = 2 * (n % 4)
                    act.wait_ge(proj_ready, n + 1)
                    if name in ("qa", "ka", "va", "ud"):
                        j = {"qa": 0, "ka": 2, "va": 4, "ud": 2 * (extra // MW)}[name] + i
                        if n == 0:
                            act.wait_ge(pads_zero, 3)
                        if name == "ud" and extra == 0 and i == 0:
                            silu_qkv()
                        leave(pre[:, j, 2:2 + SMP], pre[:, j, SMP + 4:SMP + 4 + P], b0, ACT.Copy)
                    elif name in GATE_AT:
                        j = GATE_AT[name] + i
                        leave(yT[:, j, 0:SMP], yT[:, j, SMP:TOK], b0, ACT.Silu if name == "ga" else ACT.Sigmoid)
                    elif name == "qb":
                        act.activation(hqT[:, i, 0:SMP].rearrange("p (w r) -> p w r", r=SMP // GW),
                                       PS[:, b0, :].rearrange("p (r w) -> p w r", w=GW), ACT.Copy)
                        act.activation(hqT[:, i, SMP:TOK], PS[:, b0 + 1, 0:P], ACT.Copy).then_inc(proj_taken, 1)
                    elif name in ("qc", "kc"):
                        j = i if name == "qc" else 2 + i
                        leave(mqkT[:, j, 0:SMP], mqkT[:, j, SMP:TOK], b0, ACT.Copy, 1.0 if name == "qc" else HD ** -0.5)
                    elif name == "ib":
                        act.activation(hv[:, i, :], PS[:, b0, 0:MW], ACT.Copy).then_inc(proj_taken, 1)
                    elif name == "fb":
                        act.activation(fgate[:, i, extra:extra + MW], PS[:, b0, 0:MW], ACT.Sigmoid).then_inc(proj_taken, 1)
                    elif name == "vc":
                        act.activation(mv[:, i, :, 0:HD], PS[:, b0, 0:MW].rearrange("p (h n) -> p h n", h=4),
                                       ACT.Copy).then_inc(proj_taken, 1)
                    else:
                        act.activation(smt[:, i].rearrange("p g (par pt) -> p g par pt", par=2),
                                       PS[:, b0, 0:32].rearrange("p (g pt par) -> p g par pt", pt=2, par=2),
                                       ACT.Copy).then_inc(proj_taken, 1)
                act.activation(beta[:, :, :, :], smt[:, :, 2:4, :], ACT.Sigmoid).then_inc(beta_done, 1)
                act.wait_ge(softin, 1)
                act_order.done(act.activation(spa[:, :, :, :], spi[:, :, :, :], ACT.Abs))
                act_order.done(act.activation(spa[:, :, :, :], spa[:, :, :, :], ACT.Exp, scale=-1.0))
                act.activation(nalog[:, :], prm[:, 8:16], ACT.Exp).then_inc(alog_exp, 1)
                act.activation(spa[:, :, :, :], spa[:, :, :, :], ACT.Ln, bias=1.0).then_inc(softlog, 1)
                act.wait_ge(scal_done, 1)
                act.activation(egc[:, :, :, :], cs[:, :, :, 0, :], ACT.Exp).then_inc(egc_done, 1)
                act.wait_ge(l2_eps, 1)
                act.activation(rq, rq, ACT.Sqrt).then_inc(l2_root, 1)
                act.wait_ge(hy_conv, 1)
                act.activation(hy[:, :, 0:SMP], cbuf[:, 0:4, 0:SMP], ACT.Copy)
                act.activation(hy[:, :, SMP:TOK], cbuf[:, 0:4, PRO], ACT.Copy).then_inc(hy_out, 1)
                act.activation(yT[:, 6:8, 0:SMP], cbuf[:, 4:6, 0:SMP], ACT.Copy)
                act.activation(yT[:, 6:8, SMP:TOK], cbuf[:, 4:6, PRO], ACT.Copy).then_inc(hy_out, 1)
                for n in range(2 * NT):
                    dst = kv_tok[:, n, :] if n < NT else mh_tok[:, n - NT, :]
                    act.wait_ge(tr_ready, n + 1)
                    act.activation(dst, PS[:, n % 4, :], ACT.Copy).then_inc(tr_taken, 1)

                for u, (d, t, s) in enumerate(UNITS):
                    act.wait_ge(g_x, u + 1)
                    act.activation(gDT, gX, ACT.Exp, scale=-1.0).then_inc(g_dt, 1)
                    act.activation(gEGB, heads(PS[:, 0, :]), ACT.Exp).then_inc(g_egb, 1)
                    act.activation(gel, gel, ACT.Exp).then_inc(g_el, 1)
                    act.wait_ge(g_uw, u + 1)
                    uw = PS[:, 5, :].rearrange("p (par pt n) -> p pt par n", par=2, pt=2)
                    act.activation(gU.rearrange("p pt (par n) -> p pt par n", par=2), uw[:, :, :, 0:HD], ACT.Copy)
                    act.activation(gwt.rearrange("p pt (par n) -> p pt par n", par=2), uw[:, :, :, HD:P], ACT.Copy,
                                   scale=-1.0).then_inc(g_wt, 1)
                    act.wait_ge(g_wTr, u + 1)
                    act.activation(gwT.rearrange("p pt n -> p (pt n)"), PS[:, 6, 0:256], ACT.Copy).then_inc(g_wT, 1)

                for u, (d, t, s) in enumerate(UNITS):
                    act.wait_ge(m_sm, u + 1)
                    if u > 0:
                        act.wait_ge(m_kw, u)
                    act.activation(mex[:, :, :], mex[:, :, :], ACT.Exp).then_inc(m_ex, 1)
                    act.wait_ge(m_x, u + 1)
                    act.activation(mWD, mX, ACT.Exp, scale=-1.0).then_inc(m_wd, 1)
                    act.wait_ge(m_eqx, u + 1)
                    act.activation(mDC, mDC, ACT.Exp, scale=-1.0).then_inc(m_eq, 1)

                for u, (d, t, s) in enumerate(UNITS):
                    if u == 0:
                        act.wait_ge(fo_done, 1)
                    else:
                        act.wait_ge(h_x, u)
                    act.activation(hlt, fgate[:, t, MW * d:MW * d + MW], ACT.Ln).then_inc(h_lt, 1)
                    act.wait_ge(h_x, u + 1)
                    if u == 0:
                        act.wait_ge(g_staken, len(UNITS))
                    else:
                        act.wait_ge(h_staken, u)
                    act.activation(hE.rearrange("p pt l n -> p (pt l n)"), PS[:, 0:4, :].rearrange("p b n -> p (b n)"),
                                   ACT.Exp).then_inc(h_e, 1)
                    act.activation(hkd, PS[:, 5, 0:256], ACT.Exp).then_inc(h_ek, 1)
                    act.wait_ge(h_kT, u + 1)
                    act.activation(hkT, PS[:, 4, 0:256], ACT.Copy).then_inc(h_kTs, 1)
                for i, m in enumerate(MIX):
                    ss = ho_ss[:, 20 * m:20 * m + 20]
                    act.wait_ge(n_ss, i + 1)
                    act.activation(ss, ss, ACT.Sqrt).then_inc(n_root, 1)

            @block.gpsimd
            def _(pool):
                pool_order = Steps(pool, "pool_order1")
                pool.memset(rows[:, :], 0.0).then_inc(rows_zero, 1)

                for k in range(KT):
                    pool.wait_ge(hT_smp, k + 1)
                    pool.tensor_copy(hTp[:, k].rearrange("p (w r) -> p w r", r=SMP // GW),
                                     hT[:, k, 0:SMP].rearrange("p (r w) -> p w r", w=GW)).then_inc(hTp_done, 1)

                pool.wait_ge(mod_ready, 6)
                pool.memset(pre[:, :, 0:2], 0.0).then_inc(pads_zero, 1)
                pool.memset(pre[:, :, SMP + 2:SMP + 4], 0.0).then_inc(pads_zero, 1)
                pool.memset(pre[:, :, PRE_W - 2:PRE_W], 0.0).then_inc(pads_zero, 1)

                pool.memset(mv[:, :, :, HD:HD + 1], 1.0).then_inc(ones_col, 1)
                pool.wait_ge(silu_done, 2)
                pool.tensor_tensor(sq, qkT.rearrange("p k n -> p (k n)"), qkT.rearrange("p k n -> p (k n)"), ALU.mult).then_inc(sq_done, 1)
                pool.wait_ge(hy_conv, 1)
                pool.memset(part(r2_at, 3088), 0.0).then_inc(states_zero, 1)
                for u, (d, t, s) in enumerate(UNITS):
                    if u == 0:
                        pool.wait_ge(tr_taken, 5)
                        pool.wait_ge(scal_done, 1)
                        pool.wait_ge(dve_beg, 1)
                    else:
                        pool.wait_ge(g_uw, u)
                    kh = kv_tok[:, t, 0:MW].rearrange("p (pt par n) -> p par pt n", pt=2, par=2)
                    vh = kv_tok[:, t, MW:512].rearrange("p (pt par n) -> p par pt n", pt=2, par=2)
                    bkv = gBK.rearrange("p (par pt) n -> p par pt n", par=2)
                    bt = beta[:, t, d, :].rearrange("p (par pt) -> p par pt", par=2)
                    bg = beg[:, d, t, :].rearrange("p (par pt) -> p par pt", par=2)
                    for par in range(2):
                        pool.tensor_tensor(bkv[:, par, :, 0:HD], vh[:, par], spread(bt[:, par], 2, HD), ALU.mult)
                        i = pool.tensor_tensor(bkv[:, par, :, HD:P], kh[:, par], spread(bg[:, par], 2, HD), ALU.mult)
                    i.then_inc(g_bk, 1)
                    pool.wait_ge(g_mt, u + 1)
                    for n in range(LV):
                        if LV * u + n >= 2:
                            pool.wait_ge(g_lv1, LV * u + n - 1)
                        pool.tensor_tensor(gMS[n % 2], gMT, spread(strict[:, d, LV - 1 - n, :], 1, 4), ALU.mult).then_inc(g_ms, 1)
                    pool.wait_ge(g_el, u + 1)
                    el = gel.rearrange("p (par pt) -> p par pt", par=2)
                    for par in range(2):
                        i = pool.tensor_tensor(gkd.rearrange("p pt (par n) -> p par pt n", par=2)[:, par], kh[:, par],
                                               spread(el[:, par], 2, HD), ALU.mult)
                    i.then_inc(g_kd, 1)
                pool.memset(mst[:, 1], 0.0).then_inc(m_zero, 1)
                for u, (d, t, s) in enumerate(UNITS):
                    pool.wait_ge(m_ex, u + 1)
                    if u == 0:
                        pool.wait_ge(tr_taken, 2 * NT)
                    else:
                        pool.wait_ge(m_st, u)
                    kh = mh_tok[:, t, 0:MW].rearrange("p (pt par n) -> p par pt n", pt=2, par=2)
                    wk = mex[:, 0, :].rearrange("p (par pt) -> p par pt", par=2)
                    for par in range(2):
                        i = pool.tensor_tensor(mkw.rearrange("p pt (par n) -> p par pt n", par=2)[:, par], kh[:, par],
                                               spread(wk[:, par], 2, HD), ALU.mult)
                    i.then_inc(m_kw, 1)
                for u, (d, t, s) in enumerate(UNITS):
                    if u == 0:
                        pool.wait_ge(fo_done, 1)
                    else:
                        pool.wait_ge(h_kT, u)
                        pool.wait_ge(h_kd, u)
                    pool.tensor_scalar(hkt, fgate[:, t, MW * d:MW * d + MW], -1.0, 1.0, ALU.mult, ALU.add).then_inc(h_kt, 1)
                    pool.wait_ge(h_e, u + 1)
                    pool.wait_ge(h_kTs, u + 1)
                    for pt in range(2):
                        i = pool.tensor_tensor(hKE[:, pt], spread(hkT[:, P * pt:P * pt + P], 1, LV), hE[:, pt, 0:LV, :], ALU.mult)
                    i.then_inc(h_ke, 1)
                    pool.wait_ge(h_ek, u + 1)
                    pool.wait_ge(h_kt, u + 1)
                    pool.tensor_tensor(hkd, hkd, hkt, ALU.mult).then_inc(h_kd, 1)

        nc.all_engine_barrier()
        nc.clear_and_free_semaphores(stage_sems)
        stage_sems.clear()
        nc.all_engine_barrier()

        dft_at = r2_at + 3900
        fwd5 = part(dft_at, 4096).rearrange("p (t n) -> p t n", t=4)
        inv5 = part(dft_at + 4096, 4096).rearrange("p (t n) -> p t n", t=8)
        fwd1 = part(dft_at + 8192, 256).rearrange("p (t n) -> p t n", t=1)
        inv1 = part(dft_at + 8448, 256).rearrange("p (t n) -> p t n", t=2)
        dec_at = dft_at + 8704
        decay = part(dec_at, NT * 512).rearrange("p (t n) -> p t n", t=NT)
        feats = part(dec_at + 2560, TOK)[0:33]
        fw1, fw2, fw3 = part(r3_at, HD)[0:33], part(r3_at + 64, HD)[0:HD], part(r3_at + 128, 1024)[0:HD]
        fcol = small(3)[0:HD]
        fz, fn, hid1, hid2 = (part(x_at + TOK * i, TOK)[0:HD] for i in range(4))
        hf = part(r1_at, NT * 1024).rearrange("p (t o s n) -> p t o s n", t=NT, o=2, s=2)
        hsum = part(r1_at + 8960, NT * 512).rearrange("p (t o n) -> p t o n", t=NT, o=2)
        hdif = part(r1_at + 11520, NT * 512).rearrange("p (t o n) -> p t o n", t=NT, o=2)
        hsq = [part(x_at + 2560 + 1024 * i, 1024).rearrange("p (o s n) -> p o s n", o=2, s=2) for i in range(2)]
        rn = part(x_at, 1024).rearrange("p (s n) -> p s n", s=2)
        HA = part(r1_at, 2560).rearrange("p (f n) -> p f n", f=5)
        HB = part(r1_at + 2560, 2560).rearrange("p (f n) -> p f n", f=5)
        HC = part(r1_at + 5120, 1024).rearrange("p (s n) -> p s n", s=2)
        spec = part(x_at + 1024, 2560).rearrange("p (f n) -> p f n", f=10)
        z1 = part(dec_at, 2 * TOK).rearrange("p (k n) -> p k n", k=2)
        ctmp = part(dec_at + 1300, TOK)
        z1_tok = part(r1_at + 14080, NT * MW).rearrange("p (t n) -> p t n", t=NT)
        pr = [part(x_at + 3584, 1024).rearrange("p (k n) -> p k n", k=4), part(r3_at, 1024).rearrange("p (k n) -> p k n", k=4)]
        FT = [(0, f) for f in range(4)] + [(1, 0)]
        (f_in, f_dft, f_1, f_z, f_s, f_h, f_hf, f_sq, f_nrm, f_ne, f_nr, f_rn, f_sd, f_H, f_Ht, f_HC, c_Z, c_pr, c_Y, c_y,
         c_out, c_z1, c_tr, c_trt, f_row) = (sem("f_" + n) for n in
         "in dft 1 z s h hf sq nrm ne nr rn sd H Ht HC cZ cpr cY cy cout cz1 ctr ctrt row".split())
        w_out = part(r1_at, 8192).rearrange("p (k n) -> p k n", k=8)
        xn = part(r1_at + 8192, 5120).rearrange("p (t n) -> p t n", t=NT)
        gate_row = part(r2_at, 4096).rearrange("p (g c n) -> p g c n", g=2, c=2)
        gdiag = [part(r2_at + 4096 + 1024 * i, 1024).rearrange("p (k n) -> p k n", k=8) for i in range(2)]
        acc = part(r2_at + 6144, 5120).rearrange("p (t n) -> p t n", t=NT)
        otmp = [part(r1_at + 13312 + 512 * i, 512) for i in range(2)]
        h2T = part(y_at, 5120).rearrange("p (k n) -> p k n", k=KT)
        rw = part(r3_at, 512).rearrange("p (k n) -> p k n", k=KT)
        rb = part(r3_at + 512, NE)
        score = part(r3_at + 576, NT * NE).rearrange("p (t n) -> p t n", t=NT)
        gate = part(r3_at + 896, NT * NE).rearrange("p (t n) -> p t n", t=NT)
        biased = small(NE)
        top8, gsum = small(8), small(8)
        fin_row = part(r1_at + 14336, 1024)
        scl2 = small(16).rearrange("p (k c) -> p k c", c=2)
        (o_w, o_x, o_rw, o_rb, o_fg, o_scl, o_gd, o_gr, o_gt, o_ps, o_mul, o_x1, n2_sq, n2_mean, n2_root, n2_xn, n2_tr, n2_s,
         n2_p, r_ps, r_sig, r_g) = (sem("o_" + n) for n in
         "w x rw rb fg scl gd gr gt ps mul x1 sq mean root xn tr s p rps rsig rg".split())
        ew = [part(r2_at + 11264 + 3072 * i, 3072) for i in range(2)]
        eg = [w[:, 0:1024].rearrange("p (k f) -> p k f", k=KT) for w in ew]
        eu = [w[:, 1024:2048].rearrange("p (k f) -> p k f", k=KT) for w in ew]
        ed = [w[:, 2048:3072] for w in ew]
        gact = part(r1_at, TOK)
        hid = [part(r1_at + TOK * (i + 1), TOK) for i in range(2)]
        e_w = [sem("e_w0"), sem("e_w1")]
        e_gu, e_silu, e_hid, e_ps, e_acc = sem("e_gu"), sem("e_silu"), sem("e_hid"), sem("e_ps"), sem("e_acc")
        f_x2, f_sq2, f_mn, f_rt, f_y, y_out = (sem("f2_" + n) for n in "x2 sq mn rt y out".split())
        fmul = part(r1_at + 2048, 1024)
        fjunk = part(r1_at + 3072, 1024)
        NQ = NE + 1
        DN = 2 * NT

        with nc.Block() as block:

            @block.sync
            def _(sp):
                sp.dma_start(feats, T["feats"]).then_inc(f_in, 16)
                sp.dma_start(fw1, T["filt_w1"].rearrange("a k n -> (a k) n")).then_inc(f_in, 16)
                sp.dma_start(fw2, T["filt_w2"].rearrange("a k n -> (a k) n")).then_inc(f_in, 16)
                sp.dma_start(fw3, T["filt_w3"].rearrange("a k n -> (a k) n")).then_inc(f_in, 16)
                for i, n in enumerate(("filt_b1", "filt_freq", "filt_b2")):
                    sp.dma_start(fcol[:, i:i + 1], T[n].rearrange("a n -> n a"), allow_slow_non_contiguous=True).then_inc(f_in, 16)
                sp.dma_start(decay.rearrange("p t n -> p (t n)"), T["decay"]).then_inc(f_in, 16)
                sp.dma_start(part(dft_at, 8704), T["dfts"]).then_inc(f_dft, 16)
                sp.wait_ge(c_z1, 8)
                sp.wait_ge(c_trt, NT)
                sp.dma_start(w_out[:, :, :], T["w_out"].rearrange("a (k p) n -> p (a k) n", p=P)).then_inc(o_w, 16)
                sp.dma_start(xt[:, 0:4, :], T["x_sample"].rearrange("a (t p) d -> p (a t) d", p=P)).then_inc(o_x, 16)
                sp.dma_start(xt[:, 4, :], T["x_prompt"].rearrange("a p d -> p (a d)")).then_inc(o_x, 16)
                sp.dma_start(rw[:, :, :], T["router_w"].rearrange("a (p k) n -> p (a k) n", k=KT)).then_inc(o_rw, 16)
                sp.dma_start(rb, T["router_bias"].to_broadcast([P, NE])).then_inc(o_rb, 16)
                sp.dma_start(fin_row, T["final_g"].rearrange("(a n) -> a n", a=1).to_broadcast([P, D])).then_inc(o_fg, 16)
                wg = T["exp_w_gate"].rearrange("a e (p k) f -> p (a e) k f", k=KT)
                wu = T["exp_w_up"].rearrange("a e (p k) f -> p (a e) k f", k=KT)
                wd = T["exp_w_down"].rearrange("a e f d -> f (a e) d")

                def load_expert(e, slot):
                    sp.dma_start(eg[slot], wg[:, bass.ds(e, 1)].rearrange("p a k f -> p (a k) f")).then_inc(e_w[slot], 16)
                    sp.dma_start(eu[slot], wu[:, bass.ds(e, 1)].rearrange("p a k f -> p (a k) f")).then_inc(e_w[slot], 16)
                    sp.dma_start(ed[slot], wd[:, bass.ds(e, 1)].rearrange("p a d -> p (a d)")).then_inc(e_w[slot], 16)

                sp.dma_start(eg[0], T["sh_w_gate"].rearrange("a (p k) f -> p (a k) f", k=KT)).then_inc(e_w[0], 16)
                sp.dma_start(eu[0], T["sh_w_up"].rearrange("a (p k) f -> p (a k) f", k=KT)).then_inc(e_w[0], 16)
                sp.dma_start(ed[0], T["sh_w_down"].rearrange("a f d -> f (a d)")).then_inc(e_w[0], 16)
                load_expert(0, 1)
                with sp.Fori(0, NE // 2 - 1) as i:
                    sp.wait_ge(e_ps, DN * (2 * i + 1))
                    load_expert(2 * i + 1, 0)
                    sp.wait_ge(e_ps, DN * (2 * i + 2))
                    load_expert(2 * i + 2, 1)
                sp.wait_ge(e_ps, DN * (NE - 1))
                load_expert(NE - 1, 0)
                for t in range(NT):
                    sp.wait_ge(f_y, t + 1)
                    dst = T["y_sample"].rearrange("a (t p) d -> p (a t) d", p=P)[:, t] if t < 4 else T["y_prompt"][0]
                    sp.dma_start(dst, acc[:, t, :]).then_inc(y_out, 16)
                sp.wait_ge(y_out, 16 * NT)

            @block.tensor
            def _(pe):
                pe.wait_ge(f_in, 16 * 8)
                for i, (w, src, b) in enumerate(((fw1, feats, 0), (fw2, hid1, 2))):
                    if i:
                        pe.wait_ge(f_s, 1)
                    pe.matmul(PS[0:HD, b, :], w, src[:, 0:SMP], start=True, stop=True)
                    pe.matmul(PS[0:HD, b + 1, 0:P], w, src[:, SMP:TOK], start=True, stop=True).then_inc(f_1, 1)
                pe.wait_ge(f_s, 2)
                for t in range(NT):
                    if t >= 2:
                        pe.wait_ge(f_hf, t - 1)
                    for o in range(2):
                        mm = pe.matmul(PS[:, 4 + 2 * (t % 2) + o, :], hid2[:, t * P:(t + 1) * P], fw3[:, 512 * o:512 * o + 512],
                                       start=True, stop=True)
                    mm.then_inc(f_h, 1)
                for t in range(NT):
                    pe.wait_ge(f_sq, t + 1)
                    for side in range(2):
                        mm = pe.matmul(PS[:, t // 4, :], ones, hsq[t % 2][:, :, side, :],
                                       start=t in (0, 4) and side == 0, stop=t in (3, 4) and side == 1)
                    mm.then_inc(f_nrm, 1)
                pe.wait_ge(f_sd, NT)
                pe.wait_ge(f_dft, 16)
                for i, (s, f) in enumerate(FT):
                    m, t0, nt = (fwd1, 4, 1) if s else (fwd5, 0, 4)
                    n = P if s else SMP
                    if i == 0:
                        pe.wait_ge(f_rn, 1)
                        pe.wait_ge(f_hf, NT)
                    if i >= 1:
                        pe.wait_ge(f_Ht, i)
                    for b, base, h in ((2, 0, hsum), (3, n, hdif)) + (((4, n, hsum),) if f == 0 else ()):
                        for t in range(nt):
                            mm = pe.matmul(PS[:, b, :], m[:, t, base + f * P:base + f * P + P],
                                           h[:, t0 + t].rearrange("p o n -> p (o n)"), start=t == 0, stop=t == nt - 1)
                    mm.then_inc(f_H, 1)
                for o in range(2):
                    if o == 1:
                        for t in range(NT):
                            pe.wait_ge(c_z1, 2 if t < 4 else 4)
                            if t >= 2:
                                pe.wait_ge(c_trt, t - 1)
                            for pt in range(2):
                                mm = pe.transpose(PS[:, t % 2, P * pt:P * pt + P], z1[:, pt, t * P:(t + 1) * P], ident)
                            mm.then_inc(c_tr, 1)
                        pe.wait_ge(c_trt, NT)
                    for i, (s, f) in enumerate(FT):
                        m, t0, nt = (fwd1, 4, 1) if s else (fwd5, 0, 4)
                        n = P if s else SMP
                        if o == 0 and i < 2:
                            pe.wait_ge(f_Ht, len(FT))
                        if len(FT) * o + i >= 2:
                            pe.wait_ge(c_pr, len(FT) * o + i - 1)
                        for part_, base in ((0, 0), (1, n)):
                            for t in range(nt):
                                z = z1_tok[:, t0 + t, :] if o else mh_tok[:, t0 + t, MW:512]
                                mm = pe.matmul(PS[:, 2 + (len(FT) * o + i) % 2, MW * part_:MW * part_ + MW],
                                               m[:, t, base + f * P:base + f * P + P], z, start=t == 0, stop=t == nt - 1)
                        mm.then_inc(c_Z, 1)
                    pe.wait_ge(c_Y, len(FT) * (o + 1))
                    if o == 1:
                        pe.wait_ge(c_out, 4)
                    for pt in range(2):
                        for k in range(8):
                            mm = pe.matmul(PS[:, 4 + pt, :], spec[:, k, P * pt:P * pt + P], inv5[:, k, :], start=k == 0, stop=k == 7)
                    mm.then_inc(c_y, 1)
                    for pt in range(2):
                        for k in range(2):
                            mm = pe.matmul(PS[:, 6, P * pt:P * pt + P], spec[:, 8 + k, P * pt:P * pt + P], inv1[:, k, :],
                                           start=k == 0, stop=k == 1)
                    mm.then_inc(c_y, 1)
                for n, (g, c) in enumerate([(g, c) for g in range(2) for c in range(2)]):
                    pe.wait_ge(o_gd, n + 1)
                    if n >= 2:
                        pe.wait_ge(o_gt, n - 1)
                    for half in range(2):
                        mm = pe.matmul(PS[:, 2 * (n % 2) + half, :], ones,
                                       gdiag[n % 2][:, 4 * half:4 * half + 4, :].rearrange("p k n -> p (k n)"), start=True, stop=True)
                    mm.then_inc(o_gr, 1)
                pe.wait_ge(o_w, 16)
                pe.wait_ge(c_z1, 8)
                for n in range(2 * NT):
                    t, half = n // 2, n % 2
                    if n >= 4:
                        pe.wait_ge(o_mul, n - 3)
                    for k in range(8):
                        mm = pe.matmul(PS[:, 4 + n % 4, :], yT[:, k, t * P:(t + 1) * P], w_out[:, k, 512 * half:512 * half + 512],
                                       start=k == 0, stop=k == 7)
                    mm.then_inc(o_ps, 1)
                pe.wait_ge(o_gt, 4)
                pe.wait_ge(n2_xn, NT)
                for k in range(KT):
                    if k >= 2:
                        pe.wait_ge(n2_s, k - 1)
                        pe.wait_ge(n2_p, k - 1)
                    for t in range(NT):
                        dst = PS[:, k % 2, t * P:(t + 1) * P] if t < 4 else PS[:, 2 + k % 2, 0:P]
                        mm = pe.transpose(dst, xn[:, t, k:D:KT], ident)
                    mm.then_inc(n2_tr, 1)
                pe.wait_ge(o_rw, 16)
                pe.wait_ge(n2_s, KT)
                pe.wait_ge(n2_p, KT)
                pe.wait_ge(o_mul, 2 * NT)
                for t in range(NT):
                    if t == 4:
                        pe.wait_ge(r_sig, 1)
                    for k in range(KT):
                        mm = pe.matmul(PS[:, 4 + t % 4, 0:NE], h2T[:, k, t * P:(t + 1) * P], rw[:, k, :], start=k == 0, stop=k == KT - 1)
                    mm.then_inc(r_ps, 1)

                def gate_up(slot, loads, before):
                    pe.wait_ge(e_w[slot], loads)
                    if before is not None:
                        pe.wait_ge(e_hid, before)
                    for w, b in ((eg[slot], 0), (eu[slot], 2)):
                        for half in range(2):
                            for k in range(KT):
                                mm = pe.matmul(PS[:, b + half, 0:320], w[:, k, :], h2T[:, k, 320 * half:320 * half + 320],
                                               start=k == 0, stop=k == KT - 1)
                    mm.then_inc(e_gu, 1)

                def down(slot, q, first=False):
                    pe.wait_ge(e_hid, q + 1)
                    for j in range(DN):
                        t, half = j // 2, j % 2
                        if not (first and j < 4):
                            pe.wait_ge(e_acc, DN * q + j - 3)
                        b = 4 + (j + (2 if slot else 0)) % 4
                        pe.matmul(PS[:, b, :], hid[slot][:, t * P:(t + 1) * P], ed[slot][:, 512 * half:512 * half + 512],
                                  start=True, stop=True).then_inc(e_ps, 1)

                pe.wait_ge(r_sig, NT)
                gate_up(0, 48, None)
                gate_up(1, 48, 1)
                down(0, 0, True)
                with pe.Fori(0, NE // 2 - 1) as i:
                    gate_up(0, 48 * i + 96, 2 * i + 2)
                    down(1, 2 * i + 1)
                    gate_up(1, 48 * i + 96, 2 * i + 3)
                    down(0, 2 * i + 2)
                gate_up(0, 48 * (NE // 2) + 48, NE)
                down(1, NE - 1)
                down(0, NE)

            @block.vector
            def _(dve):
                dve_order = Steps(dve, "dve_order2")
                TWO_PI = 2 * np.pi
                HI = 6.28125
                LO = float(TWO_PI - HI)
                MAGIC = 12582912.0
                for i in range(2):
                    b = 2 * i
                    dve.wait_ge(f_1, i + 1)
                    dve.tensor_scalar(fz[:, 0:SMP], PS[0:HD, b, :], fcol[:, 2 * i:2 * i + 1], fcol[:, 1:2], ALU.add, ALU.mult)
                    dve_order.done(dve.tensor_scalar(fz[:, SMP:TOK], PS[0:HD, b + 1, 0:P], fcol[:, 2 * i:2 * i + 1], fcol[:, 1:2],
                                                     ALU.add, ALU.mult))
                    dve_order.done(dve.tensor_scalar(fn, fz, 1.0 / TWO_PI, MAGIC, ALU.mult, ALU.add))
                    dve_order.done(dve.tensor_scalar(fn, fn, MAGIC, None, ALU.subtract))
                    dve_order.done(dve.scalar_tensor_tensor(out=fz, in0=fn, scalar=-HI, in1=fz, op0=ALU.mult, op1=ALU.add))
                    dve_order.done(dve.scalar_tensor_tensor(out=fz, in0=fn, scalar=-LO, in1=fz, op0=ALU.mult, op1=ALU.add))
                    dve.tensor_scalar(fz, fz, 3.1415925, -3.1415925, ALU.min, ALU.max).then_inc(f_z, 1)
                    dve.wait_ge(f_s, i + 1)
                for t in range(NT):
                    dve.wait_ge(f_h, t + 1)
                    for o in range(2):
                        i = dve.tensor_tensor(hf[:, t, o].rearrange("p s n -> p (s n)"), PS[:, 4 + 2 * (t % 2) + o, :],
                                              decay[:, t, :], ALU.mult)
                    i.then_inc(f_hf, 1)
                dve.wait_ge(f_nrm, NT)
                for s in range(2):
                    i = dve.tensor_scalar(rn[:, s, :], PS[:, s, :], EPS, None, ALU.add)
                i.then_inc(f_ne, 1)
                dve.wait_ge(f_nr, 1)
                dve.reciprocal(rn, rn).then_inc(f_rn, 1)
                dve.wait_ge(f_rn, 1)
                dve.wait_ge(f_sd, NT)
                for i, (s, f) in enumerate(FT):
                    dve.wait_ge(f_H, i + 1)
                    dve.tensor_tensor(HA[:, i, :], PS[:, 2, :], rn[:, s, :], ALU.mult)
                    j = dve.tensor_tensor(HB[:, i, :], PS[:, 3, :], rn[:, s, :], ALU.mult)
                    if f == 0:
                        dve_order.done(j)
                        dve.memset(HB[0:1, i, :], 0.0)
                        dve_order.done(dve.tensor_copy(HC[:, s, :], HA[:, i, :]))
                        j = dve.tensor_tensor(HC[0:1, s, :], PS[0:1, 4, :], rn[0:1, s, :], ALU.mult)
                    j.then_inc(f_Ht, 1)
                dve.wait_ge(f_Ht, len(FT))
                for o in range(2):
                    for i, (s, f) in enumerate(FT):
                        n = len(FT) * o + i
                        dve.wait_ge(c_Z, n + 1)
                        if n >= 2:
                            dve.wait_ge(c_Y, n - 1)
                        b, q = 2 + n % 2, pr[n % 2]
                        w = slice(MW * o, MW * o + MW)
                        hc = HC[:, s, w] if f == 0 else HA[:, i, w]
                        dve.tensor_tensor(q[:, 0, :], PS[:, b, 0:MW], HA[:, i, w], ALU.mult)
                        dve.tensor_tensor(q[:, 1, :], PS[:, b, MW:512], HB[:, i, w], ALU.mult)
                        dve.tensor_tensor(q[:, 2, :], PS[:, b, 0:MW], HB[:, i, w], ALU.mult)
                        dve.tensor_tensor(q[:, 3, :], PS[:, b, MW:512], hc, ALU.mult).then_inc(c_pr, 1)
                    for s in range(2):
                        dve.wait_ge(c_y, 2 * o + s + 1)
                        for pt in range(2):
                            cols = slice(0, SMP) if s == 0 else slice(SMP, TOK)
                            ps = PS[:, 4 + pt, :] if s == 0 else PS[:, 6, P * pt:P * pt + P]
                            z = z1[:, pt, cols] if o else hy[:, pt, cols]
                            dve.scalar_tensor_tensor(out=ctmp[:, cols], in0=z, scalar=tapsT[:, pt, 8 + o:9 + o], in1=ps,
                                                     op0=ALU.mult, op1=ALU.add).then_inc(c_out, 1)
                            dve.wait_ge(c_out, 4 * o + 2 * s + pt + 1)
                            dst, x = (yT[:, 6 + pt, cols], yT[:, 6 + pt, cols]) if o else (z1[:, pt, cols], hy[:, 2 + pt, cols])
                            dve.tensor_tensor(dst, x, ctmp[:, cols], ALU.mult).then_inc(c_z1, 1)
                            dve.wait_ge(c_z1, 4 * o + 2 * s + pt + 1)
                dve.wait_ge(c_z1, 8)
                dve_order.done(dve.tensor_scalar(scl2[:, :, :], modT[:, 4], 1.0, None, ALU.add))
                dve.tensor_tensor(scl2[:, :, :], scl2[:, :, :], spread(g2p, 2, 2), ALU.mult).then_inc(o_scl, 1)
                GR = [(g, c) for g in range(2) for c in range(2)]
                def gate_diag(n):
                    g, c = GR[n]
                    if n >= 2:
                        dve.wait_ge(o_gr, n - 1)
                    dve.tensor_tensor(gdiag[n % 2], spread(ident, 1, KT), spread(modT[:, 2 + 3 * g, :, c], 2, P),
                                      ALU.mult).then_inc(o_gd, 1)
                gate_diag(0)
                for n, (g, c) in enumerate(GR):
                    if n + 1 < 4:
                        gate_diag(n + 1)
                    dve.wait_ge(o_gr, n + 1)
                    dst = gate_row[:, g, c, :].rearrange("p (q k) -> p k q", k=KT)
                    b = 2 * (n % 2)
                    for half in range(2):
                        i = dve.tensor_copy(dst[:, 4 * half:4 * half + 4, :], PS[:, b + half, :].rearrange("p (k q) -> p k q", k=4))
                    i.then_inc(o_gt, 1)
                dve.wait_ge(o_gt, 4)
                dve.wait_ge(o_x, 32)
                for t in range(NT):
                    for half in range(2):
                        n = 2 * t + half
                        w = slice(512 * half, 512 * half + 512)
                        dve.wait_ge(o_ps, n + 1)
                        if n >= 2:
                            dve.wait_ge(o_x1, n - 1)
                        dve.tensor_tensor(otmp[half], PS[:, 4 + n % 4, :], gate_row[:, 0, t // 4, w], ALU.mult).then_inc(o_mul, 1)
                dve.wait_ge(n2_sq, NT)
                dve.tensor_scalar(sumsq[:, 0:NT], sumsq[:, 0:NT], 1.0 / D, EPS, ALU.mult, ALU.add).then_inc(n2_mean, 1)
                dve.wait_ge(n2_root, 1)
                dve_order.done(dve.reciprocal(rstd[:, 0:NT], rstd[:, 0:NT]))
                for t in range(NT):
                    dve.tensor_scalar(xn[:, t, :], xt[:, t, :], rstd[:, t:t + 1], None, ALU.mult).then_inc(n2_xn, 1)
                for k in range(KT):
                    dve.wait_ge(n2_tr, k + 1)
                    dve.tensor_scalar(h2T[:, k, 0:SMP], PS[:, k % 2, :], scl2[:, k, 0:1], modT[:, 3, k, 0:1], ALU.mult,
                                      ALU.add).then_inc(n2_s, 1)
                dve.wait_ge(r_sig, NT)
                dve.wait_ge(o_rb, 16)
                for t in range(NT):
                    dve_order.done(dve.tensor_tensor(biased[:, :], score[:, t, :], rb, ALU.add))
                    dve_order.done(dve.max(top8[:, :], biased[:, :]))
                    dve_order.done(dve.match_replace(gate[:, t, :], top8[:, :], biased[:, :], -BIG))
                    dve_order.done(dve.tensor_tensor(gate[:, t, :], gate[:, t, :], biased[:, :], ALU.not_equal))
                    dve_order.done(dve.tensor_tensor(gate[:, t, :], gate[:, t, :], score[:, t, :], ALU.mult))
                    dve_order.done(dve.tensor_reduce(gsum[:, 0:1], gate[:, t, :], AX.X, ALU.add))
                    dve_order.done(dve.reciprocal(gsum[:, 0:1], gsum[:, 0:1]))
                    dve.tensor_scalar(gate[:, t, :], gate[:, t, :], gsum[:, 0:1], 2.5, ALU.mult, ALU.mult).then_inc(r_g, 1)
                    dve.wait_ge(r_g, t + 1)
                def hidden(slot, q):
                    dve.wait_ge(e_silu, q + 1)
                    dve.tensor_tensor(hid[slot].rearrange("p (b n) -> p b n", b=2), gact.rearrange("p (b n) -> p b n", b=2),
                                      PS[:, 2:4, 0:320], ALU.mult).then_inc(e_hid, 1)

                def accumulate(slot, q, e=None):
                    for j in range(DN):
                        t, half = j // 2, j % 2
                        b = 4 + (j + (2 if slot else 0)) % 4
                        a = acc[:, t, 512 * half:512 * half + 512]
                        dve.wait_ge(e_ps, DN * q + j + 1)
                        if e is None:
                            dve.tensor_copy(a, PS[:, b, :]).then_inc(e_acc, 1)
                        else:
                            dve.wait_ge(e_acc, DN * (q - 1) + j + 1)
                            dve.scalar_tensor_tensor(out=a, in0=PS[:, b, :], scalar=gate[:, t, bass.ds(e, 1)], in1=a,
                                                     op0=ALU.mult, op1=ALU.add).then_inc(e_acc, 1)

                hidden(0, 0)
                hidden(1, 1)
                accumulate(0, 0)
                with dve.Fori(0, NE // 2 - 1) as i:
                    hidden(0, 2 * i + 2)
                    accumulate(1, 2 * i + 1, 2 * i)
                    hidden(1, 2 * i + 3)
                    accumulate(0, 2 * i + 2, 2 * i + 1)
                hidden(0, NE)
                accumulate(1, NE - 1, NE - 2)
                accumulate(0, NE, NE - 1)
                dve.wait_ge(e_acc, DN * NQ)
                for t in range(NT):
                    dve_order.done(dve.tensor_tensor(fmul, acc[:, t, :], gate_row[:, 1, t // 4, :], ALU.mult))
                    dve.tensor_tensor(xt[:, t, :], xt[:, t, :], fmul, ALU.add).then_inc(f_x2, 1)
                    dve.wait_ge(f_x2, t + 1)
                dve.wait_ge(f_sq2, NT)
                dve.tensor_scalar(sumsq[:, 0:NT], sumsq[:, 0:NT], 1.0 / D, EPS, ALU.mult, ALU.add).then_inc(f_mn, 1)
                dve.wait_ge(f_rt, 1)
                dve_order.done(dve.reciprocal(rstd[:, 0:NT], rstd[:, 0:NT]))
                dve.wait_ge(o_fg, 16)
                for t in range(NT):
                    dve.scalar_tensor_tensor(out=acc[:, t, :], in0=xt[:, t, :], scalar=rstd[:, t:t + 1], in1=fin_row,
                                             op0=ALU.mult, op1=ALU.mult).then_inc(f_y, 1)


            @block.scalar
            def _(act):
                act_order = Steps(act, "act_order2")
                for i in range(2):
                    act.wait_ge(f_z, i + 1)
                    act.activation(hid1 if i == 0 else hid2, fz, ACT.Sin).then_inc(f_s, 1)
                act.wait_ge(f_ne, 1)
                act.activation(rn, rn, ACT.Sqrt).then_inc(f_nr, 1)
                for t in range(NT):
                    act.wait_ge(c_tr, t + 1)
                    act.activation(z1_tok[:, t, :], PS[:, t % 2, 0:256], ACT.Copy).then_inc(c_trt, 1)

                for t in range(NT):
                    act.wait_ge(o_x1, 2 * t + 2)
                    i = act.activation(part(r1_at + 8192, D), xt[:, t, :], ACT.Square, accum_out=sumsq[:, t:t + 1])
                    i.then_inc(n2_sq, 1)
                    act.wait_ge(n2_sq, t + 1)
                act.wait_ge(n2_mean, 1)
                act.activation(rstd[:, 0:NT], sumsq[:, 0:NT], ACT.Sqrt).then_inc(n2_root, 1)
                act.wait_ge(o_scl, 1)
                for k in range(KT):
                    act.wait_ge(n2_tr, k + 1)
                    act.activation(h2T[:, k, SMP:TOK], PS[:, 2 + k % 2, 0:P], ACT.Identity, scale=scl2[:, k, 1:2],
                                   bias=modT[:, 3, k, 1:2]).then_inc(n2_p, 1)
                for t in range(NT):
                    act.wait_ge(r_ps, t + 1)
                    act.activation(score[:, t, :], PS[:, 4 + t % 4, 0:NE], ACT.Sigmoid).then_inc(r_sig, 1)
                def silu(q, first=False):
                    act.wait_ge(e_gu, q + 1)
                    if not first:
                        act.wait_ge(e_hid, q)
                    act.activation(gact.rearrange("p (b n) -> p b n", b=2), PS[:, 0:2, 0:320], ACT.Silu).then_inc(e_silu, 1)

                silu(0, True)
                with act.Fori(0, NE) as i:
                    silu(i + 1)
                for t in range(NT):
                    act.wait_ge(f_x2, t + 1)
                    act.activation(fjunk, xt[:, t, :], ACT.Square, accum_out=sumsq[:, t:t + 1]).then_inc(f_sq2, 1)
                    act.wait_ge(f_sq2, t + 1)
                act.wait_ge(f_mn, 1)
                act.activation(rstd[:, 0:NT], sumsq[:, 0:NT], ACT.Sqrt).then_inc(f_rt, 1)

            @block.gpsimd
            def _(pool):
                pool_order = Steps(pool, "pool_order2")
                for t in range(NT):
                    pool.wait_ge(f_hf, t + 1)
                    if t >= 2:
                        pool.wait_ge(f_nrm, t - 1)
                    h = hf[:, t]
                    pool.tensor_tensor(hsq[t % 2].rearrange("p o s n -> p (o s n)"), h.rearrange("p o s n -> p (o s n)"),
                                       h.rearrange("p o s n -> p (o s n)"), ALU.mult).then_inc(f_sq, 1)
                    pool.tensor_tensor(hsum[:, t], h[:, :, 0, :], h[:, :, 1, :], ALU.add)
                    pool.tensor_tensor(hdif[:, t], h[:, :, 0, :], h[:, :, 1, :], ALU.subtract).then_inc(f_sd, 1)
                for o in range(2):
                    for i, (s, f) in enumerate(FT):
                        n = len(FT) * o + i
                        pool.wait_ge(c_pr, n + 1)
                        if o == 1 and i == 0:
                            pool.wait_ge(c_y, 2)
                        q = pr[n % 2]
                        re, im = (8, 9) if s else (f, 4 + f)
                        pool.tensor_tensor(spec[:, re, :], q[:, 0, :], q[:, 1, :], ALU.subtract)
                        pool.tensor_tensor(spec[:, im, :], q[:, 2, :], q[:, 3, :], ALU.add).then_inc(c_Y, 1)
                pool.wait_ge(o_x, 32)
                for n in range(2 * NT):
                    t, half = n // 2, n % 2
                    w = slice(512 * half, 512 * half + 512)
                    pool.wait_ge(o_mul, n + 1)
                    pool.tensor_tensor(xt[:, t, w], xt[:, t, w], otmp[half], ALU.add).then_inc(o_x1, 1)


_IN = ['x_prompt', 'x_sample', 'c', 'state_gdn', 'state_hgrn', 'state_mlstm_c', 'state_mlstm_n',
       'state_mlstm_m', 'c_ctx', 'norm1_g', 'norm2_g', 'w_mod', 'b_mod', 'w_in', 'gdn_conv', 'gdn_a_log',
       'gdn_dt_bias', 'gdn_norm_g', 'hgrn_lb_logits', 'hgrn_norm_g', 'mlstm_f_bias', 'mlstm_norm_g',
       'hyena_conv', 'filt_w1', 'filt_b1', 'filt_w2', 'filt_b2', 'filt_w3', 'filt_freq', 'hyena_d',
       'w_out', 'router_w', 'router_bias', 'exp_w_gate', 'exp_w_up', 'exp_w_down', 'sh_w_gate',
       'sh_w_up', 'sh_w_down', 'final_g']
_OUT = [("y_prompt", (1, P, D)), ("y_sample", (1, SMP, D)), ("new_gdn", (1, 1, 2, 4, HD, HD)),
        ("new_hgrn", (1, 1, 2, 4, HD, HD)), ("new_c", (1, 1, 2, 4, HD, HD)), ("new_n", (1, 1, 2, 4, HD)),
        ("new_m", (1, 1, 2, 4))]


def kernel(**inputs):
    import concourse.bacc as bacc
    from concourse.bass_utils import run_bass_kernel_spmd

    nc = bacc.Bacc("TRN2", target_bir_lowering=False, num_devices=1)
    arrays, T = {}, {}
    for name in _IN:
        a = np.ascontiguousarray(inputs[name])
        arrays["in_" + name] = a
        T[name] = nc.dram_tensor("in_" + name, a.shape, mybir.dt.float32, kind="ExternalInput").ap()
    for name, a in zip(("masks", "dfts", "feats", "decay"), shape_constants()):
        arrays["const_" + name] = a
        T[name] = nc.dram_tensor("const_" + name, a.shape, mybir.dt.float32, kind="ExternalInput").ap()
    for name, shape in _OUT:
        T[name] = nc.dram_tensor("out_" + name, shape, mybir.dt.float32, kind="ExternalOutput").ap()
    trunk_program(nc, T)
    r = run_bass_kernel_spmd(nc, [arrays], core_ids=[0])
    return tuple(r.results[0]["out_" + name] for name, _ in _OUT)
```

```python
import concourse.bass as bass
from concourse import mybir
from contextlib import ExitStack
import numpy as np

P = 128
D = 1024
KT = D // P
NT = 5
TOK = NT * P
SMP = 512
GW = 64
NE = 64
TOPK = 8
HD = 64
MW = 256
LV = 7
EPS = 1e-6
BIG = 1e30
TINY = 2.0 ** -63
IN_OFF = dict(qa=0, ka=256, va=512, ga=768, ab=1024, qb=1040, ib=1296, gb=1552, fb=1808,
              qc=2320, kc=2576, vc=2832, oc=3088, fi=3344, ud=3360)
CONST = ["ident", "ones", "blk", "strict", "run", "big", "after"]
CONST_W = dict(ident=P, ones=P, blk=P, strict=2 * LV * P, run=2 * (LV + 1) * P, big=2 * P, after=2 * P)


def shape_constants():
    a = np.arange(P)
    row, col = a[:, None], a[None, :]
    strict, run = np.zeros((P, 2, LV, P)), np.zeros((P, 2, LV + 1, P))
    for l in range(LV):
        s = 64 >> l
        same = row // (2 * s) == col // (2 * s)
        m = same & (row % (2 * s) < s) & (col % (2 * s) >= s)
        strict[:, 0, l], strict[:, 1, l] = m, m.T
        mid = (col // (2 * s)) * 2 * s + s
        first = col < mid
        run[:, 0, l] = np.where(first, (row > col) & (row < mid), (row >= mid) & (row <= col))
        run[:, 1, l] = np.where(first, (row >= col) & (row < mid), (row >= mid) & (row < col))
    run[:, 0, LV], run[:, 1, LV] = row <= col, row >= col
    big = np.stack([np.where(row <= col, 0, BIG), np.where(row >= col, 0, BIG)], 1)
    after = np.stack([row > col, row < col], 1)
    parts = dict(ident=np.eye(P), ones=np.ones((P, P)), blk=row // HD == col // HD, strict=strict,
                 run=run, big=big, after=after)
    masks = np.concatenate([np.asarray(parts[n], np.float32).reshape(P, -1) for n in CONST], 1)

    def dft(length):
        n = 2 * length
        t, f = np.arange(length)[:, None], np.arange(length)[None, :]
        th = 2 * np.pi * ((t * f) % n) / n
        re, im = np.cos(th), -np.sin(th)
        im[:, 0] = (-1.0) ** np.arange(length)
        w = np.where(np.arange(length) == 0, 1.0, 2.0)[None, :] / n
        wi = w.copy()
        fwd = np.concatenate([re, im], 1)
        inv = np.concatenate([(re * w).T, (im * wi).T], 0)
        return fwd, inv
    f5, i5 = dft(SMP)
    f1, i1 = dft(P)
    fwd5 = f5.reshape(4, P, 2 * SMP).transpose(1, 0, 2).reshape(P, -1)
    inv5 = i5.reshape(8, P, SMP).transpose(1, 0, 2).reshape(P, -1)
    inv1 = i1.reshape(2, P, P).transpose(1, 0, 2).reshape(P, -1)
    dfts = np.concatenate([fwd5, inv5, f1, inv1], 1).astype(np.float32)

    def positions(length):
        t = np.arange(length, dtype=np.float64)
        tn = np.linspace(0.0, 1.0, length).astype(np.float32).astype(np.float64)
        bands = np.linspace(1e-4, 15, 16).astype(np.float32).astype(np.float64)
        ang = ((2.0 * np.pi / length) * t[:, None]).astype(np.float32) * bands[None, :].astype(np.float32)
        ang = ang.astype(np.float64)
        feats = np.concatenate([tn[:, None], np.cos(ang), -np.sin(ang)], 1)
        deltas = np.abs(np.linspace(np.log(1e-2) / 1.5, np.log(1e-2) / 0.3, MW))
        dec = np.exp(-tn[:, None] * deltas[None, :])
        dec2 = dec.copy()
        dec2[0] = 0
        return feats, np.stack([dec, dec2], 1)
    (fa, da), (fb, db) = positions(SMP), positions(P)
    feats = np.ascontiguousarray(np.concatenate([fa, fb], 0).T).astype(np.float32)
    decay = np.concatenate([da, db], 0).reshape(NT, P, 2 * MW).transpose(1, 0, 2)
    decay = np.ascontiguousarray(decay).reshape(P, -1).astype(np.float32)
    return masks, dfts, feats, decay


def token_numbers():
    a = np.arange(P)
    return np.concatenate([np.tile(a, (P, 1)), a[:, None] + P * np.arange(NT)[None, :]], 1).astype(np.float32)


def trunk_program(nc, T):
    F = mybir.dt.float32
    U32 = mybir.dt.uint32
    ALU = mybir.AluOpType
    ACT = mybir.ActivationFunctionType
    AX = mybir.AxisListType

    def spread(ap, axis, n):
        shape = list(ap.shape)
        shape.insert(axis, n)
        return ap.unsqueeze(axis).to_broadcast(shape)

    ctx = ExitStack()
    with ctx:
        def sb(name, words, parts=P):
            return ctx.enter_context(nc.sbuf_tensor(name, [parts, words], F))

        stage_sems = []

        def sem(name):
            stage_sems.append(nc.alloc_semaphore(name=name))
            return stage_sems[-1]

        class Steps:

            def __init__(self, eng, name):
                self.eng, self.n = eng, 0
                self.sem = sem(name)

            def done(self, ins):
                self.n += 1
                ins.then_inc(self.sem, 1)
                self.eng.wait_ge(self.sem, self.n)

        PS = ctx.enter_context(nc.psum_tensor("PS", [P, 8, 512], F))

        cst = sb("cst", sum(CONST_W.values()))
        at, off = {}, 0
        for n in CONST:
            at[n] = cst[:, off:off + CONST_W[n]]
            off += CONST_W[n]
        ident, ones, blk = at["ident"], at["ones"], at["blk"]
        strict = at["strict"].rearrange("p (d l n) -> p d l n", d=2, l=LV)
        run = at["run"].rearrange("p (d l n) -> p d l n", d=2, l=LV + 1)
        big = at["big"].rearrange("p (d n) -> p d n", d=2)
        after = at["after"].rearrange("p (d n) -> p d n", d=2)
        ARENA = 53200 - sum(CONST_W.values())
        arena = sb("arena", ARENA)
        top = [0]

        def region(words):
            a = top[0]
            top[0] += words
            assert top[0] <= ARENA, (top[0], ARENA)
            return a

        def part(start, words):
            return arena[:, start:start + words]

        x_at, y_at, r1_at, r2_at, r3_at = region(5120), region(5120), region(15360), region(19300), region(1500)
        par_at = region(ARENA - top[0])
        par_end = [par_at]

        def small(words):
            a = par_end[0]
            par_end[0] += words
            assert par_end[0] <= ARENA, par_end[0] - ARENA
            return part(a, words)

        xt = part(x_at, 5120).rearrange("p (t d) -> p t d", t=NT)
        yT = part(y_at, 5120).rearrange("p (k n) -> p k n", k=KT)
        hT = part(r1_at, 5120).rearrange("p (k n) -> p k n", k=KT)
        hTp = part(r1_at + 5120, 4096).rearrange("p (k n) -> p k n", k=KT)
        w_slot = [part(r1_at + 9216 + 2048 * i, 2048).rearrange("p (k n) -> p k n", k=KT) for i in range(3)]
        mod_slot = [part(r2_at + 8192 * i, 8192).rearrange("p (k n) -> p k n", k=KT) for i in range(2)]

        cond = small(16).rearrange("p (c k) -> p c k", c=2)
        scond = small(16).rearrange("p (k c) -> p k c", c=2)
        g1p, g2p = small(8), small(8)
        bmod = small(48).rearrange("p (j k) -> p j k", j=6)
        modT = small(96).rearrange("p (j k c) -> p j k c", j=6, k=KT)
        scl = small(16).rearrange("p (k c) -> p k c", c=2)
        sumsq, rstd = small(8), small(8)

        consts_in, x_in, x_back = sem("consts_in"), sem("x_in"), sem("x_back")
        cond_in, params_in, cond_silu = sem("cond_in"), sem("params_in"), sem("cond_silu")
        mod_in = [sem("mod_in0"), sem("mod_in1")]
        mod_ready, mod_taken, scl_ready = sem("mod_ready"), sem("mod_taken"), sem("scl_ready")
        sq1_done, root1, xn_done, xT_ready = sem("sq1_done"), sem("root1"), sem("xn_done"), sem("xT_ready")
        mean1, hT_smp, hT_pro, hTp_done = sem("mean1"), sem("hT_smp"), sem("hT_pro"), sem("hTp_done")
        junk = part(y_at, D)
        PRE_W = SMP + P + 6
        CONV_W = PRE_W - 4
        r2 = [r2_at]

        def keep(words):
            a = r2[0]
            r2[0] += words
            assert r2[0] <= r2_at + 19300
            return part(a, words)

        pre = keep(6 * PRE_W).rearrange("p (k n) -> p k n", k=6)
        qkT = keep(4 * TOK).rearrange("p (k n) -> p k n", k=4)
        vT = keep(2 * TOK).rearrange("p (k n) -> p k n", k=2)
        hqT = keep(2 * TOK).rearrange("p (k n) -> p k n", k=2)
        fgate = keep(NT * 512).rearrange("p (t n) -> p t n", t=NT)
        hv = keep(NT * MW).rearrange("p (t n) -> p t n", t=NT)
        mqkT = keep(4 * TOK).rearrange("p (k n) -> p k n", k=4)
        mv = keep(NT * 4 * 65).rearrange("p (t h n) -> p t h n", t=NT, h=4)
        hy = keep(4 * TOK).rearrange("p (k n) -> p k n", k=4)
        w_small = small(KT * 32).rearrange("p (k n) -> p k n", k=KT)
        smt = small(NT * 32).rearrange("p (t g h) -> p t g h", t=NT, g=8)
        GROUPS = [("qa", 0, "f"), ("ka", 0, "f"), ("va", 0, "f"), ("ga", 0, "f"), ("qb", 0, "f"), ("gb", 0, "f"),
                  ("ib", 0, "t"), ("fb", 0, "t"), ("fb", MW, "t"), ("qc", 0, "f"), ("kc", 0, "f"), ("oc", 0, "f"),
                  ("vc", 0, "t"), ("small", 0, "s"), ("ud", 0, "f"), ("ud", MW, "f"), ("ud", 2 * MW, "f")]
        OUTPUTS = [(g, i) for g, (_, _, kind) in enumerate(GROUPS) for i in range(2 if kind == "f" else NT)]
        slotted = [g for g, (_, _, kind) in enumerate(GROUPS) if kind != "s"]

        def outputs_before(g):
            return sum(1 for a, _ in OUTPUTS if a < g)

        w_in_sem = [sem(f"w_in{i}") for i in range(3)]
        small_in, proj_ready, proj_taken, pads_zero = sem("small_in"), sem("proj_ready"), sem("proj_taken"), sem("pads_zero")
        gdn_conv_read = sem("gdn_conv_read")
        ones_col, dve_beg = sem("ones_col"), sem("dve_beg")
        cbuf = part(x_at, 6 * CONV_W).rearrange("p (k n) -> p k n", k=6)
        sq = part(x_at, 4 * TOK)
        rq = part(x_at + 4 * TOK, 4 * TOK)
        o_tok = part(r1_at, 3 * NT * MW).rearrange("p (m t n) -> p m t n", m=3, t=NT)
        kv_tok = part(r1_at + 3840, NT * 512).rearrange("p (t n) -> p t n", t=NT)
        mh_tok = part(r1_at + 6400, NT * 512).rearrange("p (t n) -> p t n", t=NT)
        rows_in, rows_T, rows_zero, taps_ready = sem("rows_in"), sem("rows_T"), sem("rows_zero"), sem("taps_ready")
        rows = part(r2_at + 16700, 768)
        tapsT = small(60).rearrange("p (k r) -> p k r", k=6)
        prm_raw, prm = small(24), small(24)
        lb_row = part(x_at, 512)
        lbn = small(8)
        silu_done, sq_done, l2_sum, l2_eps, l2_root, k_unit = (sem(n) for n in
            ("silu_done", "sq_done", "l2_sum", "l2_eps", "l2_root", "k_unit"))
        hy_conv, hy_out, tr_ready, tr_taken, prm_in = (sem(n) for n in
            ("hy_conv", "hy_out", "tr_ready", "tr_taken", "prm_in"))
        softin, softabs, softexp, softlog, scal_ready, scal_ps = (sem(n) for n in
            ("softin", "softabs", "softexp", "softlog", "scal_ready", "scal_ps"))
        spi = small(NT * 16).rearrange("p (t g h) -> p t g h", t=NT, g=4)
        spa = small(NT * 16).rearrange("p (t g h) -> p t g h", t=NT, g=4)
        beta = small(NT * 8).rearrange("p (t d h) -> p t d h", t=NT, d=2)
        gl = small(NT * 16).rearrange("p (d t w h) -> p d t w h", d=2, t=NT, w=2)
        cs = small(NT * 16).rearrange("p (d t w h) -> p d t w h", d=2, t=NT, w=2)
        tot = small(NT * 16).rearrange("p (d t w h) -> p d t w h", d=2, t=NT, w=2)
        egc = small(NT * 8).rearrange("p (d t h) -> p d t h", d=2, t=NT)
        beg = small(NT * 8).rearrange("p (d t h) -> p d t h", d=2, t=NT)
        cc = small(NT * 8).rearrange("p (d t h) -> p d t h", d=2, t=NT)
        nalog = small(8)
        scal_done, egc_done, alog_exp, beta_done, fo_done = (sem(n) for n in
            ("scal_done", "egc_done", "alog_exp", "beta_done", "fo_done"))
        lb_in, lb_e, lb_work = sem("lb_in"), sem("lb_e"), sem("lb_work")
        lbt = [part(r3_at, 512), part(r3_at + 512, 512)]
        UNITS = [(0, 4, 1), (1, 4, 1)] + [(d, n if d == 0 else 3 - n, 0) for n in range(4) for d in range(2)]
        seen = set()
        FIRST = []
        for _, t, _ in UNITS:
            FIRST.append(t not in seen)
            seen.add(t)

        def last_token(d):
            return P - 1 if d == 0 else 0

        pool_area = {"u1": (r1_at + 8960, 6400), "u2": (x_at, 5120), "u3": (r3_at, 1500), "s": (r2_at, 3876)}
        used = {k: 0 for k in pool_area}

        def scratch(where, words):
            a, n = pool_area[where]
            used[where] += words
            assert used[where] <= n, (where, used[where])
            return part(a + used[where] - words, words)

        def heads(ap):
            return ap.rearrange("p (h n) -> p h n", h=4)

        gS = scratch("s", 4 * 2 * P).rearrange("p (s d pt n) -> p s d pt n", s=2, d=2, pt=2)
        hS = scratch("s", 4 * 2 * P).rearrange("p (s d pt n) -> p s d pt n", s=2, d=2, pt=2)
        mS = scratch("s", 4 * 260).rearrange("p (s d pt n) -> p s d pt n", s=2, d=2, pt=2)
        states_zero, states_in = sem("states_zero"), sem("states_in")

        gDG, gEGB, gX, gDT, gMT = (heads(scratch("u1", 512)) for _ in range(5))
        gMS = [heads(scratch("u1", 512)) for _ in range(2)]
        gAT, gT, gTT, gP, gBK = (heads(scratch("u1", 512)) for _ in range(5))
        gvn, gU, gwt, gwT, gqd, gkd = (scratch("u1" if i == 0 else "u2", 256).rearrange("p (pt n) -> p pt n", pt=2)
                                       for i in range(6))
        gel = scratch("u2", 4)
        (g_diag, g_row, g_egb, g_x, g_dt, g_kq, g_mt, g_at, g_ms, g_lv1, g_p, g_lv2, g_t, g_bk, g_uw, g_wt, g_wTr,
         g_wT, g_ws, g_vn, g_qd, g_eld, g_el, g_kd, g_o, g_st, g_otaken, g_staken) = (sem("g_" + n) for n in (
         "diag row egb x dt kq mt at ms lv1 p lv2 t bk uw wt wTr wT ws vn qd eld el kd o st otaken staken").split())

        def kq_banks(b):
            return PS[:, b:b + 2, 0:256]

        def by_par(ap):
            return ap.rearrange("p (par pt) n -> p par (pt n)", par=2)
        mDC, mWD = (heads(scratch("u3", 512)) for _ in range(2))
        mWT, mX = heads(scratch("s", 512)), heads(scratch("u2", 512))
        mqd, mkw = (scratch("u2", 256).rearrange("p (pt n) -> p pt n", pt=2) for _ in range(2))
        mtmp = scratch("u3", 256)
        mst = small(16).rearrange("p (s d h) -> p s d h", s=2, d=2)
        m_raw = small(8)
        mmx, mmu, mden = small(4), small(4), small(4)
        mex = small(12).rearrange("p (k h) -> p k h", k=3)
        (m_in, m_zero, m_dc, m_cb, m_qk, m_dmu, m_mb, m_x, m_eqx, m_sm, m_wd, m_eq, m_ex, m_wt, m_qd, m_kw, m_o, m_st,
         m_otaken, m_staken) = (sem("m_" + n) for n in
         "in zero dc cb qk dmu mb x eqx sm wd eq ex wt qd kw o st otaken staken".split())
        used["u1"] = 0
        hE = scratch("u1", 2 * (LV + 1) * P).rearrange("p (pt l n) -> p pt l n", pt=2, l=LV + 1)
        hQE = scratch("u1", 2 * (LV + 1) * P).rearrange("p (pt l n) -> p pt l n", pt=2, l=LV + 1)
        hKE = scratch("u1", 2 * LV * P).rearrange("p (pt l n) -> p pt l n", pt=2, l=LV)
        hAT = heads(scratch("u1", 512))
        hlt, hkt, hkT, hkd = (scratch("u2", 256) for _ in range(4))
        (h_lt, h_kt, h_x, h_kT, h_e, h_ek, h_kTs, h_qe, h_ke, h_kd, h_lvl, h_merge, h_o, h_st, h_otaken,
         h_staken) = (sem("h_" + n) for n in "lt kt x kT e ek kTs qe ke kd lvl merge o st otaken staken".split())
        norm_row = small(3 * HD).rearrange("p (m n) -> p m n", m=3)
        ho_ss = small(3 * 20)
        (n_in, n_sq, n_ss, n_root, n_on, n_tr, n_taken) = (sem("n_" + x) for x in "in sq ss root on tr taken".split())
        MIX = [0, 1, 2]
        sq_at = x_at + 3840
        osq = part(sq_at, NT * MW)
        osq4 = osq.rearrange("p (h n) -> p h n", n=HD)
        tail_out = sem("tail_out")
        s_out = sem("s_out")

        with nc.Block() as block:

            @block.sync
            def _(sp):
                sp.dma_start(cond[:, 0, :], T["c"].rearrange("a (p k) -> p (a k)", k=KT)).then_inc(cond_in, 16)
                sp.dma_start(cond[:, 1, :], T["c_ctx"].rearrange("(p k) -> p k", k=KT)).then_inc(cond_in, 16)
                sp.dma_start(xt[:, 0:4, :], T["x_sample"].rearrange("a (t p) d -> p (a t) d", p=P)).then_inc(x_in, 16)
                sp.dma_start(xt[:, 4, :], T["x_prompt"].rearrange("a p d -> p (a d)")).then_inc(x_in, 16)
                wm = T["w_mod"].rearrange("a (p k) (j n) -> p j (a k) n", k=KT, j=6)
                for j in range(6):
                    if j >= 2:
                        sp.wait_ge(mod_ready, j - 1)
                    sp.dma_start(mod_slot[j % 2], wm[:, j]).then_inc(mod_in[j % 2], 16)
                    if j == 0:
                        sp.dma_start(g1p, T["norm1_g"].rearrange("a (p k) -> p (a k)", k=KT)).then_inc(params_in, 16)
                        sp.dma_start(g2p, T["norm2_g"].rearrange("a (p k) -> p (a k)", k=KT)).then_inc(params_in, 16)
                        sp.dma_start(bmod, T["b_mod"].rearrange("a (j p k) -> p (a j) k", j=6, k=KT)).then_inc(params_in, 16)
                        sp.dma_start(cst[:, :], T["masks"]).then_inc(consts_in, 16)
                sp.wait_ge(rows_zero, 1)
                sp.dma_start(rows[0:5, :], T["gdn_conv"].rearrange("a t n -> (a t) n")).then_inc(rows_in, 16)
                sp.dma_start(rows[5:8, :], T["hyena_conv"].rearrange("a t n -> (a t) n")).then_inc(rows_in, 16)
                sp.dma_start(rows[8:10, 0:MW], T["hyena_d"].rearrange("a t n -> (a t) n")).then_inc(rows_in, 16)
                for i, n in enumerate(("gdn_dt_bias", "gdn_a_log", "mlstm_f_bias")):
                    sp.dma_start(prm_raw[:, 8 * i:8 * i + 8],
                                 T[n].rearrange("a d h -> a (d h)").to_broadcast([P, 8])).then_inc(prm_in, 16)
                sp.dma_start(lbt[0], T["hgrn_lb_logits"].rearrange("a d n -> a (d n)").to_broadcast([P, 512])).then_inc(lb_in, 16)

                wi = T["w_in"].rearrange("a (p k) n -> p (a k) n", k=KT)
                sp.dma_start(w_small[:, :, 0:16], wi[:, :, IN_OFF["ab"]:IN_OFF["ab"] + 16]).then_inc(small_in, 16)
                sp.dma_start(w_small[:, :, 16:32], wi[:, :, IN_OFF["fi"]:IN_OFF["fi"] + 16]).then_inc(small_in, 16)
                for n, g in enumerate(slotted):
                    name, extra, _ = GROUPS[g]
                    if n >= 3:
                        sp.wait_ge(proj_ready, outputs_before(slotted[n - 3] + 1))
                    c0 = IN_OFF[name] + extra
                    sp.dma_start(w_slot[n % 3], wi[:, :, c0:c0 + MW]).then_inc(w_in_sem[n % 3], 16)
                    if n == 5:
                        pass
                sp.wait_ge(states_zero, 1)
                for name, S, w in (("state_gdn", gS, HD), ("state_hgrn", hS, HD), ("state_mlstm_c", mS, 65)):
                    for d in range(2):
                        for h in range(4):
                            par, pt = h % 2, h // 2
                            sp.dma_start(S[HD * par:HD * par + HD, 0, d, pt, w * par:w * par + HD],
                                         T[name][0, 0, d, h]).then_inc(states_in, 16)
                            if w == 65:
                                sp.dma_start(S[HD * par:HD * par + HD, 0, d, pt, w * par + HD:w * par + HD + 1],
                                             T["state_mlstm_n"][0, 0, d, h].rearrange("(n a) -> n a", a=1),
                                             allow_slow_non_contiguous=True).then_inc(states_in, 16)
                sp.dma_start(m_raw[:, :], T["state_mlstm_m"].rearrange("a b d h -> (a b) (d h)").to_broadcast([P, 8])).then_inc(m_in, 16)
                for m, n in enumerate(("gdn_norm_g", "hgrn_norm_g", "mlstm_norm_g")):
                    sp.dma_start(norm_row[:, m, :], T[n].to_broadcast([P, HD])).then_inc(n_in, 16)
                y_tail = T["y_rows"].rearrange("(b p) d -> p b d", p=P)[:, TOK * TOPK // P:, :]
                sp.dma_start(y_tail, spread(at["strict"][:, 0:D], 1, NE)).then_inc(tail_out, 16)
                sp.wait_ge(g_staken, 2)
                sp.wait_ge(m_staken, 2)
                sp.wait_ge(h_staken, 2)
                for name, S, w in (("new_gdn", gS, HD), ("new_hgrn", hS, HD), ("new_c", mS, 65)):
                    for d in range(2):
                        for h in range(4):
                            par, pt = h % 2, h // 2
                            sp.dma_start(T[name][0, 0, d, h],
                                         S[HD * par:HD * par + HD, 1, d, pt, w * par:w * par + HD]).then_inc(s_out, 16)
                            if w == 65:
                                sp.dma_start(T["new_n"][0, 0, d, h].rearrange("(n a) -> n a", a=1),
                                             S[HD * par:HD * par + HD, 1, d, pt, w * par + HD:w * par + HD + 1],
                                             allow_slow_non_contiguous=True).then_inc(s_out, 16)
                                sp.dma_start(T["new_m"][0, 0, d:d + 1, h:h + 1],
                                             mst[0:1, 1, d, 2 * par + pt:2 * par + pt + 1]).then_inc(s_out, 16)
                sp.wait_ge(s_out, 16 * 40)
                sp.wait_ge(tail_out, 16)


            @block.tensor
            def _(pe):
                def mod_block(j):
                    pe.wait_ge(mod_in[j % 2], 16 * (j // 2 + 1))
                    if j >= 2:
                        pe.wait_ge(mod_taken, j - 1)
                    for m in range(KT):
                        for k in range(KT):
                            mm = pe.matmul(PS[:, 6 + j % 2, 2 * m:2 * m + 2], mod_slot[j % 2][:, k, m:D:KT],
                                           scond[:, k, :], start=(k == 0), stop=(k == KT - 1))
                    mm.then_inc(mod_ready, 1)

                pe.wait_ge(cond_silu, 1)
                mod_block(0)
                mod_block(1)
                pe.wait_ge(consts_in, 16)
                pe.wait_ge(xn_done, NT)
                for k in range(KT):
                    if k >= 2:
                        pe.wait_ge(hT_smp, k - 1)
                        pe.wait_ge(hT_pro, k - 1)
                    for t in range(NT):
                        dst = PS[:, k % 2, t * P:(t + 1) * P] if t < 4 else PS[:, 2 + k % 2, 0:P]
                        mm = pe.transpose(dst, xt[:, t, k:D:KT], ident)
                    mm.then_inc(xT_ready, 1)
                for j in range(2, 6):
                    mod_block(j)
                pe.wait_ge(rows_in, 48)
                for k in range(6):
                    mm = pe.transpose(PS[:, 5, 16 * k:16 * k + 10], rows[0:10, k * P:(k + 1) * P], ident[0:10, 0:10])
                mm.then_inc(rows_T, 1)
                for n, (g, i) in enumerate(OUTPUTS):
                    name, extra, kind = GROUPS[g]
                    b0, b1 = 2 * (n % 4), 2 * (n % 4) + 1
                    if i == 0:
                        if kind == "s":
                            pe.wait_ge(small_in, 32)
                        else:
                            s = slotted.index(g)
                            pe.wait_ge(w_in_sem[s % 3], 16 * (s // 3 + 1))
                            w = w_slot[s % 3]
                    if n == 0:
                        pe.wait_ge(hT_smp, KT)
                        pe.wait_ge(hT_pro, KT)
                    if n == 2:
                        pe.wait_ge(taps_ready, 1)
                    if n == 3:
                        pe.wait_ge(mod_taken, 6)
                    if n >= 4:
                        pe.wait_ge(proj_taken, n - 3)
                    if kind == "f":
                        for k in range(KT):
                            pe.matmul(PS[:, b0, :], w[:, k, i * P:(i + 1) * P], hT[:, k, 0:SMP], start=(k == 0), stop=(k == KT - 1))
                        for k in range(KT):
                            mm = pe.matmul(PS[:, b1, 0:P], w[:, k, i * P:(i + 1) * P], hT[:, k, SMP:TOK],
                                           start=(k == 0), stop=(k == KT - 1))
                    else:
                        src = hTp if name in ("ib", "fb") and i < 4 else hT
                        if src is hTp:
                            pe.wait_ge(hTp_done, KT)
                        rhs = w_small if kind == "s" else w
                        for k in range(KT):
                            mm = pe.matmul(PS[:, b0, 0:rhs.shape[2]], src[:, k, i * P:(i + 1) * P], rhs[:, k, :],
                                           start=(k == 0), stop=(k == KT - 1))
                    mm.then_inc(proj_ready, 1)
                pe.wait_ge(proj_taken, len(OUTPUTS))
                pe.wait_ge(scal_ready, 1)
                for d in range(2):
                    pe.matmul(PS[:, 6, 40 * d:40 * d + 40], run[:, d, LV, :], gl[:, d].rearrange("p t w h -> p (t w h)"),
                              start=True, stop=True)
                pe.matmul(PS[:, 6, 128:208], ones, gl.rearrange("p d t w h -> p (d t w h)"), start=True, stop=True).then_inc(scal_ps, 1)
                pe.wait_ge(sq_done, 1)
                for i in range(5):
                    mm = pe.matmul(PS[:, i, :], blk, sq[:, i * 512:(i + 1) * 512], start=True, stop=True)
                mm.then_inc(l2_sum, 1)
                TR = [("kv", t) for t in range(NT)] + [("mh", t) for t in range(NT)]
                for n, (what, t) in enumerate(TR):
                    if n == 0:
                        pe.wait_ge(k_unit, 1)
                        pe.wait_ge(silu_done, 4)
                    if n == NT:
                        pe.wait_ge(hy_out, 2)
                    if n >= 4:
                        pe.wait_ge(tr_taken, n - 3)
                    c = slice(t * P, (t + 1) * P)
                    four = (qkT[:, 2, c], qkT[:, 3, c], vT[:, 0, c], vT[:, 1, c]) if what == "kv" else \
                           (mqkT[:, 2, c], mqkT[:, 3, c], hy[:, 0, c], hy[:, 1, c])
                    for j, src in enumerate(four):
                        mm = pe.transpose(PS[:, n % 4, j * P:(j + 1) * P], src, ident)
                    mm.then_inc(tr_ready, 1)
                for u, (d, t, s) in enumerate(UNITS):
                    c = slice(t * P, (t + 1) * P)
                    pe.wait_ge(g_diag, u + 1)
                    if u == 0:
                        pe.wait_ge(tr_taken, 2 * NT)
                        pe.wait_ge(l2_eps, 1)
                        pe.wait_ge(scal_done, 1)
                    else:
                        pe.wait_ge(g_otaken, u)
                        pe.wait_ge(g_staken, u)
                        pe.wait_ge(g_eld, u)
                    pe.matmul(PS[:, 0, :], ones, gDG.rearrange("p h n -> p (h n)"), start=True, stop=True).then_inc(g_row, 1)
                    for b, q in ((1, 2), (3, 0)):
                        for pt in range(2):
                            for par in range(2):
                                r = slice(HD * par, HD * par + HD)
                                mm = pe.matmul(PS[:, b + par, P * pt:P * pt + P], qkT[r, 2 + pt, c], qkT[r, q + pt, c],
                                               start=True, stop=True)
                    mm.then_inc(g_kq, 1)
                    for n in range(LV):
                        pe.wait_ge(g_ms, LV * u + n + 1)
                        if n > 0:
                            pe.wait_ge(g_t, LV * u + n)
                        for h in range(4):
                            mm = pe.matmul(PS[:, 5, P * h:P * h + P], gMS[n % 2][:, h, :], gT[:, h, :] if n else ident,
                                           start=True, stop=True)
                        mm.then_inc(g_lv1, 1)
                        pe.wait_ge(g_p, LV * u + n + 1)
                        if 0 < n < LV - 1:
                            for h in range(4):
                                pe.matmul(PS[:, 6, P * h:P * h + P], gTT[:, h, :], gP[:, h, :], start=True, stop=True)
                        for h in range(4):
                            mm = pe.matmul(PS[:, 7, P * h:P * h + P], gP[:, h, :], gTT[:, h, :] if n else ident,
                                           start=True, stop=True)
                        mm.then_inc(g_lv2, 1)
                    pe.wait_ge(g_t, LV * (u + 1))
                    pe.wait_ge(g_bk, u + 1)
                    for h in range(4):
                        mm = pe.matmul(PS[:, 5, P * h:P * h + P], gTT[:, h, :], gBK[:, h, :], start=True, stop=True)
                    mm.then_inc(g_uw, 1)
                    pe.wait_ge(g_wt, u + 1)
                    for pt in range(2):
                        mm = pe.transpose(PS[:, 6, P * pt:P * pt + P], gwt[:, pt, :], ident)
                    mm.then_inc(g_wTr, 1)
                    pe.wait_ge(g_wT, u + 1)
                    if u == 0:
                        pe.wait_ge(states_zero, 1)
                    if s == 0 and u < 4:
                        pe.wait_ge(states_in, 16 * 32)
                    for pt in range(2):
                        mm = pe.matmul(PS[:, 7, P * pt:P * pt + P], gwT[:, pt, :], gS[:, s, d, pt, :], start=True, stop=True)
                    mm.then_inc(g_ws, 1)
                    pe.wait_ge(g_vn, u + 1)
                    pe.wait_ge(g_qd, u + 1)
                    pe.wait_ge(g_at, u + 1)
                    for pt in range(2):
                        pe.matmul(PS[:, 1, P * pt:P * pt + P], gqd[:, pt, :], gS[:, s, d, pt, :], start=True, stop=False)
                        for par in range(2):
                            o = P * pt + HD * par
                            mm = pe.matmul(PS[:, 1, o:o + HD], gAT[:, 2 * par + pt, :], gvn[:, pt, HD * par:HD * par + HD],
                                           start=False, stop=par == 1)
                    mm.then_inc(g_o, 1)
                    pe.wait_ge(g_kd, u + 1)
                    for pt in range(2):
                        mm = pe.matmul(PS[:, 2, P * pt:P * pt + P], gkd[:, pt, :], gvn[:, pt, :], start=True, stop=True)
                    mm.then_inc(g_st, 1)
                for u, (d, t, s) in enumerate(UNITS):
                    c = slice(t * P, (t + 1) * P)
                    pe.wait_ge(m_dc, u + 1)
                    if u == 0:
                        pe.wait_ge(g_otaken, len(UNITS))
                        pe.wait_ge(g_staken, len(UNITS))
                    else:
                        pe.wait_ge(m_otaken, u)
                        pe.wait_ge(m_staken, u)
                    pe.matmul(PS[:, 0, :], ones, mDC.rearrange("p h n -> p (h n)"), start=True, stop=True).then_inc(m_cb, 1)
                    for pt in range(2):
                        for par in range(2):
                            r = slice(HD * par, HD * par + HD)
                            mm = pe.matmul(PS[:, 2 + par, P * pt:P * pt + P], mqkT[r, 2 + pt, c], mqkT[r, pt, c],
                                           start=True, stop=True)
                    mm.then_inc(m_qk, 1)
                    pe.wait_ge(m_dmu, u + 1)
                    pe.matmul(PS[:, 1, :], ones, mDC.rearrange("p h n -> p (h n)"), start=True, stop=True).then_inc(m_mb, 1)
                    pe.wait_ge(m_qd, u + 1)
                    pe.wait_ge(m_wt, u + 1)
                    if u == 0:
                        pe.wait_ge(ones_col, 1)
                    if s == 0 and u < 4:
                        pe.wait_ge(states_in, 16 * 32)
                    for pt in range(2):
                        pe.matmul(PS[:, 4, 130 * pt:130 * pt + 130], mqd[:, pt, :], mS[:, s, d, pt, :], start=True, stop=False)
                        for par in range(2):
                            o = 130 * pt + 65 * par
                            mm = pe.matmul(PS[:, 4, o:o + 65], mWT[:, 2 * par + pt, :], mv[:, t, 2 * pt + par, :],
                                           start=False, stop=par == 1)
                    mm.then_inc(m_o, 1)
                    pe.wait_ge(m_kw, u + 1)
                    for pt in range(2):
                        mm = pe.matmul(PS[:, 5, 130 * pt:130 * pt + 130], mkw[:, pt, :],
                                       mv[:, t, 2 * pt:2 * pt + 2, :].rearrange("p h n -> p (h n)"), start=True, stop=True)
                    mm.then_inc(m_st, 1)
                for u, (d, t, s) in enumerate(UNITS):
                    c = slice(t * P, (t + 1) * P)
                    pe.wait_ge(h_lt, u + 1)
                    if u == 0:
                        pe.wait_ge(m_otaken, len(UNITS))
                        pe.wait_ge(m_staken, len(UNITS))
                        pe.wait_ge(g_staken, len(UNITS))
                    else:
                        pe.wait_ge(h_otaken, u)
                        pe.wait_ge(h_staken, u)
                    for pt in range(2):
                        for half in range(2):
                            pe.matmul(PS[:, 2 * pt + half, :], hlt[:, P * pt:P * pt + P],
                                      run[:, d, 4 * half:4 * half + 4, :].rearrange("p l n -> p (l n)"), start=True, stop=True)
                    pe.matmul(PS[:, 5, 0:256], after[:, d, :], hlt, start=True, stop=True).then_inc(h_x, 1)
                    pe.wait_ge(h_kt, u + 1)
                    for pt in range(2):
                        mm = pe.transpose(PS[:, 4, P * pt:P * pt + P], hkt[:, P * pt:P * pt + P], ident)
                    mm.then_inc(h_kT, 1)
                    for r in range(LV + 1):
                        if r == 0:
                            pe.wait_ge(h_kTs, u + 1)
                            pe.wait_ge(h_ek, u + 1)
                        if r == 1:
                            pe.wait_ge(h_ke, u + 1)
                            pe.wait_ge(h_qe, u + 1)
                        if r >= 2:
                            pe.wait_ge(h_merge, (LV + 1) * u + r - 1)
                        for pt in range(2):
                            for par in range(2):
                                q = slice(HD * par, HD * par + HD)
                                k_, q_ = (hkT[q, P * pt:P * pt + P], hqT[q, pt, c]) if r == 0 else \
                                         (hKE[q, pt, r - 1, :], hQE[q, pt, r - 1, :])
                                mm = pe.matmul(PS[:, 4 + 2 * (r % 2) + par, P * pt:P * pt + P], k_, q_, start=True, stop=True)
                        mm.then_inc(h_lvl, 1)
                    pe.wait_ge(h_merge, (LV + 1) * (u + 1))
                    for pt in range(2):
                        pe.matmul(PS[:, 6, P * pt:P * pt + P], hQE[:, pt, LV, :], hS[:, s, d, pt, :], start=True, stop=False)
                        for par in range(2):
                            o = P * pt + HD * par
                            mm = pe.matmul(PS[:, 6, o:o + HD], hAT[:, 2 * par + pt, :], hv[:, t, o:o + HD],
                                           start=False, stop=par == 1)
                    mm.then_inc(h_o, 1)
                    pe.wait_ge(h_kd, u + 1)
                    for pt in range(2):
                        mm = pe.matmul(PS[:, 7, P * pt:P * pt + P], hkd[:, P * pt:P * pt + P], hv[:, t, P * pt:P * pt + P],
                                       start=True, stop=True)
                    mm.then_inc(h_st, 1)
                for i, m in enumerate(MIX):
                    pe.wait_ge(n_on, i + 1)
                    for pt in range(2):
                        if i > 0:
                            pe.wait_ge(n_taken, 2 * (i - 1) + pt + 1)
                        for t in range(NT):
                            dst = PS[:, 2 * pt, t * P:(t + 1) * P] if t < 4 else PS[:, 2 * pt + 1, 0:P]
                            mm = pe.transpose(dst, o_tok[:, m, t, P * pt:P * pt + P], ident)
                        mm.then_inc(n_tr, 1)


            @block.vector
            def _(dve):
                dve_order = Steps(dve, "dve_order1")
                def mod_take(j):
                    dve.wait_ge(mod_ready, j + 1)
                    dve.tensor_tensor(modT[:, j], PS[:, 6 + j % 2, 0:16].rearrange("p (k c) -> p k c", c=2),
                                      spread(bmod[:, j], 2, 2), ALU.add).then_inc(mod_taken, 1)

                dve.wait_ge(sq1_done, 1)
                dve.tensor_scalar(sumsq[:, 0:NT], sumsq[:, 0:NT], 1.0 / D, EPS, ALU.mult, ALU.add).then_inc(mean1, 1)
                dve.wait_ge(root1, 1)
                dve_order.done(dve.reciprocal(rstd[:, 0:NT], rstd[:, 0:NT]))
                for t in range(NT):
                    dve.tensor_scalar(xt[:, t, :], xt[:, t, :], rstd[:, t:t + 1], None, ALU.mult).then_inc(xn_done, 1)
                dve.wait_ge(params_in, 48)
                mod_take(0)
                mod_take(1)
                dve.wait_ge(mod_taken, 2)
                dve_order.done(dve.tensor_scalar(scl[:, :, :], modT[:, 1], 1.0, None, ALU.add))
                dve.tensor_tensor(scl[:, :, :], scl[:, :, :], spread(g1p, 2, 2), ALU.mult).then_inc(scl_ready, 1)
                dve.wait_ge(scl_ready, 1)
                for k in range(KT):
                    dve.wait_ge(xT_ready, k + 1)
                    dve.tensor_scalar(hT[:, k, 0:SMP], PS[:, k % 2, :], scl[:, k, 0:1], modT[:, 0, k, 0:1], ALU.mult,
                                      ALU.add).then_inc(hT_smp, 1)
                for j in range(2, 6):
                    mod_take(j)
                dve.wait_ge(rows_T, 1)
                dve.tensor_copy(tapsT[:, :, :], PS[:, 5, 0:96].rearrange("p (k r) -> p k r", k=6)[:, :, 0:10]).then_inc(taps_ready, 1)
                dve.wait_ge(prm_in, 48)
                dve_order.done(dve.tensor_copy(prm.rearrange("p (g par pt) -> p g par pt", g=6, par=2),
                                               prm_raw.rearrange("p (g pt par) -> p g par pt", g=6, par=2)))
                dve.wait_ge(lb_in, 16)
                dve.tensor_tensor(lbt[1], lbt[0], lbt[0], ALU.subtract).then_inc(lb_work, 1)
                dve.wait_ge(lb_e, 1)
                dve_order.done(dve.reciprocal(lbt[1], lbt[0]))
                dve_order.done(dve.tensor_tensor(lbt[0], lbt[0], lbt[1], ALU.mult))
                dve_order.done(dve.tensor_tensor(lbt[0], lbt[0], lbt[0], ALU.subtract))
                dve_order.done(dve.tensor_scalar(lbt[1], lbt[0], -1.0, 1.0, ALU.mult, ALU.add))

                dve.wait_ge(proj_taken, 6)
                dve.wait_ge(taps_ready, 1)
                for tap in range(5):
                    for k in range(6):
                        src = pre[:, k, tap:tap + CONV_W]
                        if tap == 0:
                            i = dve.tensor_scalar(cbuf[:, k, :], src, tapsT[:, k, 0:1], None, ALU.mult)
                        else:
                            i = dve.scalar_tensor_tensor(out=cbuf[:, k, :], in0=src, scalar=tapsT[:, k, tap:tap + 1],
                                                         in1=cbuf[:, k, :], op0=ALU.mult, op1=ALU.add)
                    if tap < 4:
                        dve_order.done(i)
                i.then_inc(gdn_conv_read, 1)

                dve.wait_ge(proj_taken, outputs_before(14))
                for g in range(2):
                    dve.tensor_tensor(spi[:, :, g, :], smt[:, :, g, :], spread(prm[:, 4 * g:4 * g + 4], 1, NT), ALU.add)
                    i = dve.tensor_tensor(spi[:, :, 2 + g, :], smt[:, :, 6 + g, :], spread(prm[:, 16 + 4 * g:20 + 4 * g], 1, NT), ALU.add)
                dve_order.done(i)
                dve.tensor_scalar(spi[:, :, 2:4, :], spi[:, :, 2:4, :], -1.0, None, ALU.mult).then_inc(softin, 1)
                for t in range(NT):
                    i = dve.scalar_tensor_tensor(out=fgate[:, t, :], in0=fgate[:, t, :], scalar=TINY, in1=lbt[1],
                                                 op0=ALU.max, op1=ALU.mult)
                dve_order.done(i)
                for t in range(NT):
                    i = dve.tensor_tensor(fgate[:, t, :], fgate[:, t, :], lbt[0], ALU.add)
                i.then_inc(fo_done, 1)
                dve.wait_ge(softlog, 1)
                for d in range(2):
                    for w in range(2):
                        i = dve.scalar_tensor_tensor(out=gl[:, d, :, w, :], in0=spi[:, :, 2 * w + d, :], scalar=0.0,
                                                     in1=spa[:, :, 2 * w + d, :], op0=ALU.max, op1=ALU.add)
                dve_order.done(i)
                dve.wait_ge(alog_exp, 1)
                for d in range(2):
                    dve.tensor_scalar(gl[:, d, :, 1, :], gl[:, d, :, 1, :], -1.0, None, ALU.mult)
                    i = dve.scalar_tensor_tensor(out=gl[:, d, :, 0, :], in0=gl[:, d, :, 0, :], scalar=-1.0,
                                                 in1=spread(nalog[:, 4 * d:4 * d + 4], 1, NT), op0=ALU.mult, op1=ALU.mult)
                i.then_inc(scal_ready, 1)
                dve.wait_ge(scal_ps, 1)
                dve.tensor_copy(cs.rearrange("p d t w h -> p (d t w h)"), PS[:, 6, 0:80])
                dve.tensor_copy(tot.rearrange("p d t w h -> p (d t w h)"), PS[:, 6, 128:208]).then_inc(scal_done, 1)
                dve.wait_ge(scal_done, 1)
                dve.wait_ge(egc_done, 1)
                dve.wait_ge(beta_done, 1)
                for d in range(2):
                    dve.tensor_tensor(beg[:, d], egc[:, d], beta[:, :, d, :], ALU.mult)
                    i = dve.tensor_tensor(cc[:, d], smt[:, :, 4 + d, :], cs[:, d, :, 1, :], ALU.subtract)
                i.then_inc(dve_beg, 1)

                dve.wait_ge(l2_sum, 1)
                for i5 in range(5):
                    i = dve.tensor_scalar(rq[:, i5 * 512:(i5 + 1) * 512], PS[:, i5, :], EPS, None, ALU.add)
                i.then_inc(l2_eps, 1)
                dve.wait_ge(l2_root, 1)
                dve_order.done(dve.reciprocal(rq, rq))
                qk_flat = qkT.rearrange("p k n -> p (k n)")
                dve.scalar_tensor_tensor(out=qk_flat[:, 0:2 * TOK], in0=qk_flat[:, 0:2 * TOK], scalar=HD ** -0.5,
                                         in1=rq[:, 0:2 * TOK], op0=ALU.mult, op1=ALU.mult)
                dve.tensor_tensor(qk_flat[:, 2 * TOK:], qk_flat[:, 2 * TOK:], rq[:, 2 * TOK:], ALU.mult).then_inc(k_unit, 1)

                dve.wait_ge(proj_taken, len(OUTPUTS))
                dve.wait_ge(k_unit, 1)
                for tap in range(3):
                    for k in range(6):
                        src = pre[:, k, tap + 1:tap + 1 + CONV_W]
                        if tap == 0:
                            i = dve.tensor_scalar(cbuf[:, k, :], src, tapsT[:, k, 5:6], None, ALU.mult)
                        else:
                            i = dve.scalar_tensor_tensor(out=cbuf[:, k, :], in0=src, scalar=tapsT[:, k, 5 + tap:6 + tap],
                                                         in1=cbuf[:, k, :], op0=ALU.mult, op1=ALU.add)
                    if tap < 2:
                        dve_order.done(i)
                i.then_inc(hy_conv, 1)
                for u, (d, t, s) in enumerate(UNITS):
                    c = slice(t * P, (t + 1) * P)
                    gc = cs[:, d, t, 0, :]
                    end = last_token(d)
                    if u == 0:
                        dve.wait_ge(hy_out, 2)
                        dve.wait_ge(proj_ready, len(OUTPUTS))
                    dve.tensor_tensor(gDG, spread(ident, 1, 4), spread(gc, 2, P), ALU.mult).then_inc(g_diag, 1)
                    dve.wait_ge(g_row, u + 1)
                    row = heads(PS[:, 0, :])
                    dve.tensor_tensor(gel, row[:, :, end:end + 1].rearrange("p h a -> p (h a)"), gc, ALU.subtract).then_inc(g_eld, 1)
                    dve_order.done(dve.tensor_tensor(gX, spread(gc, 2, P), row, ALU.subtract))
                    dve.scalar_tensor_tensor(out=gX, in0=gX, scalar=0.0, in1=spread(big[:, d, :], 1, 4),
                                             op0=ALU.max, op1=ALU.add).then_inc(g_x, 1)
                    dve.wait_ge(g_dt, u + 1)
                    dve.wait_ge(g_kq, u + 1)
                    dve.tensor_tensor(by_par(gMT), kq_banks(1), by_par(gDT), ALU.mult).then_inc(g_mt, 1)
                    dve.tensor_tensor(by_par(gAT), kq_banks(3), by_par(gDT), ALU.mult).then_inc(g_at, 1)
                    dve.wait_ge(g_egb, u + 1)
                    for par in range(2):
                        r = slice(HD * par, HD * par + HD)
                        i = dve.tensor_tensor(gqd[r], qkT[r, 0:2, c], gEGB[r, 2 * par:2 * par + 2, :], ALU.mult)
                    i.then_inc(g_qd, 1)
                    for n in range(LV):
                        dve.wait_ge(g_lv1, LV * u + n + 1)
                        dve.tensor_tensor(gP, heads(PS[:, 5, :]), spread(beta[:, t, d, :], 2, P), ALU.mult).then_inc(g_p, 1)
                        dve.wait_ge(g_lv2, LV * u + n + 1)
                        if n == 0:
                            dve.wait_ge(g_p, LV * u + 1)
                            dve.tensor_tensor(gT, spread(ident, 1, 4), gP, ALU.subtract)
                            dve.tensor_tensor(gTT, spread(ident, 1, 4), heads(PS[:, 7, :]), ALU.subtract).then_inc(g_t, 1)
                        else:
                            dve.wait_ge(g_t, LV * u + n)
                            if n < LV - 1:
                                dve.tensor_tensor(gT, gT, heads(PS[:, 6, :]), ALU.subtract)
                            dve.tensor_tensor(gTT, gTT, heads(PS[:, 7, :]), ALU.subtract).then_inc(g_t, 1)
                    dve.wait_ge(g_ws, u + 1)
                    dve.tensor_tensor(gvn.rearrange("p pt n -> p (pt n)"), gU.rearrange("p pt n -> p (pt n)"), PS[:, 7, 0:256],
                                      ALU.add).then_inc(g_vn, 1)
                    dve.wait_ge(g_o, u + 1)
                    if FIRST[u]:
                        dve.tensor_copy(o_tok[:, 0, t, :], PS[:, 1, 0:256]).then_inc(g_otaken, 1)
                    else:
                        dve.tensor_tensor(o_tok[:, 0, t, :], o_tok[:, 0, t, :], PS[:, 1, 0:256], ALU.add).then_inc(g_otaken, 1)
                    dve.wait_ge(g_st, u + 1)
                    for pt in range(2):
                        for par in range(2):
                            r, n = slice(HD * par, HD * par + HD), HD * par
                            i = dve.scalar_tensor_tensor(out=gS[r, s, d, pt, n:n + HD], in0=gS[r, s, d, pt, n:n + HD],
                                                         scalar=gEGB[r, 2 * par + pt, end:end + 1],
                                                         in1=PS[r, 2, P * pt + n:P * pt + n + HD], op0=ALU.mult, op1=ALU.add)
                    i.then_inc(g_staken, 1)
                dve.wait_ge(m_in, 16)
                dve_order.done(dve.tensor_copy(mst[:, 0].rearrange("p d (par pt) -> p d par pt", par=2),
                                               m_raw.rearrange("p (d pt par) -> p d par pt", d=2, pt=2)))
                dve.wait_ge(m_zero, 1)
                for u, (d, t, s) in enumerate(UNITS):
                    c = slice(t * P, (t + 1) * P)
                    cj, m0, end = cc[:, d, t, :], mst[:, s, d, :], last_token(d)
                    dve.tensor_tensor(mDC, spread(ident, 1, 4), spread(cj, 2, P), ALU.mult).then_inc(m_dc, 1)
                    dve.wait_ge(m_cb, u + 1)
                    dve_order.done(dve.tensor_tensor(mX, heads(PS[:, 0, :]), spread(big[:, 1 - d, :], 1, 4), ALU.subtract))
                    dve_order.done(dve.tensor_reduce(mmx, mX, AX.X, ALU.max))
                    dve_order.done(dve.tensor_tensor(mmu, mmx, m0, ALU.max))
                    dve.tensor_tensor(mDC, spread(ident, 1, 4), spread(mmu, 2, P), ALU.mult).then_inc(m_dmu, 1)
                    dve.wait_ge(m_mb, u + 1)
                    row = heads(PS[:, 1, :])
                    row_end = row[:, :, end:end + 1].rearrange("p h a -> p (h a)")
                    dve.tensor_tensor(mex[:, 0, :], cj, row_end, ALU.subtract)
                    dve.tensor_tensor(mex[:, 1, :], m0, row_end, ALU.subtract)
                    dve.scalar_tensor_tensor(out=mex[:, 2, :], in0=cs[:, d, t, 1, :], scalar=-1.0, in1=mmu, op0=ALU.mult,
                                             op1=ALU.subtract).then_inc(m_sm, 1)
                    dve_order.done(dve.tensor_tensor(mX, row, spread(cj, 2, P), ALU.subtract))
                    dve.scalar_tensor_tensor(out=mX, in0=mX, scalar=0.0, in1=spread(big[:, d, :], 1, 4),
                                             op0=ALU.max, op1=ALU.add).then_inc(m_x, 1)
                    dve.tensor_tensor(mDC, row, spread(m0, 2, P), ALU.subtract).then_inc(m_eqx, 1)
                    dve.wait_ge(m_eq, u + 1)
                    dve.tensor_tensor(m0, tot[:, d, t, 1, :], row_end, ALU.add)
                    for par in range(2):
                        r = slice(HD * par, HD * par + HD)
                        i = dve.tensor_tensor(mqd[r], mqkT[r, 0:2, c], mDC[r, 2 * par:2 * par + 2, :], ALU.mult)
                    i.then_inc(m_qd, 1)
                    dve.wait_ge(m_wd, u + 1)
                    dve.wait_ge(m_qk, u + 1)
                    dve.tensor_tensor(by_par(mWT), kq_banks(2), by_par(mWD), ALU.mult).then_inc(m_wt, 1)
                    dve.wait_ge(m_ex, u + 1)
                    dve.wait_ge(m_o, u + 1)
                    num = PS[:, 4, 0:260].rearrange("p (h n) -> p h n", h=4)
                    den = num[:, :, HD:HD + 1].rearrange("p h a -> p (h a)")
                    dve_order.done(dve.tensor_scalar(mden, den, -1.0, None, ALU.mult))
                    dve_order.done(dve.tensor_tensor(mden, mden, den, ALU.max))
                    dve_order.done(dve.tensor_tensor(mden.rearrange("p (pt par) -> p pt par", pt=2),
                                                     mden.rearrange("p (pt par) -> p pt par", pt=2),
                                                     mex[:, 2, :].rearrange("p (par pt) -> p pt par", par=2), ALU.max))
                    dve_order.done(dve.reciprocal(mden, mden))
                    out = heads(o_tok[:, 2, t, :])
                    if FIRST[u]:
                        dve.tensor_tensor(out, num[:, :, 0:HD], spread(mden, 2, HD), ALU.mult).then_inc(m_otaken, 1)
                    else:
                        dve.tensor_tensor(heads(mtmp), num[:, :, 0:HD], spread(mden, 2, HD), ALU.mult).then_inc(m_otaken, 1)
                        dve.wait_ge(m_otaken, u + 1)
                        dve.tensor_tensor(out, out, heads(mtmp), ALU.add)
                    dve.wait_ge(m_st, u + 1)
                    for pt in range(2):
                        for par in range(2):
                            r, n = slice(HD * par, HD * par + HD), 65 * par
                            i = dve.scalar_tensor_tensor(out=mS[r, s, d, pt, n:n + 65], in0=mS[r, s, d, pt, n:n + 65],
                                                         scalar=mex[r, 1, 2 * par + pt:2 * par + pt + 1],
                                                         in1=PS[r, 5, 130 * pt + n:130 * pt + n + 65], op0=ALU.mult, op1=ALU.add)
                    i.then_inc(m_staken, 1)
                    dve.wait_ge(m_staken, u + 1)
                for u, (d, t, s) in enumerate(UNITS):
                    c = slice(t * P, (t + 1) * P)
                    end = last_token(d)
                    dve.wait_ge(h_e, u + 1)
                    for pt in range(2):
                        i = dve.tensor_tensor(hQE[:, pt], spread(hqT[:, pt, c], 1, LV + 1), hE[:, pt], ALU.mult)
                    i.then_inc(h_qe, 1)
                    A4 = hAT.rearrange("p (par pt) n -> p par pt n", par=2)
                    for r in range(LV + 1):
                        dve.wait_ge(h_lvl, (LV + 1) * u + r + 1)
                        b = 4 + 2 * (r % 2)
                        src = PS[:, b:b + 2, 0:256].rearrange("p par (pt n) -> p par pt n", pt=2)
                        if r == 0:
                            dve.tensor_tensor(A4, src, spread(spread(ident, 1, 2), 1, 2), ALU.mult).then_inc(h_merge, 1)
                        else:
                            dve.wait_ge(h_merge, (LV + 1) * u + r)
                            mask = strict[:, d, r - 1, :].bitcast(U32)
                            dve.copy_predicated(A4, spread(spread(mask, 1, 2), 1, 2), src).then_inc(h_merge, 1)
                    dve.wait_ge(h_o, u + 1)
                    if FIRST[u]:
                        dve.tensor_copy(o_tok[:, 1, t, :], PS[:, 6, 0:256]).then_inc(h_otaken, 1)
                    else:
                        dve.tensor_tensor(o_tok[:, 1, t, :], o_tok[:, 1, t, :], PS[:, 6, 0:256], ALU.add).then_inc(h_otaken, 1)
                    dve.wait_ge(h_st, u + 1)
                    for pt in range(2):
                        for par in range(2):
                            r, n = slice(HD * par, HD * par + HD), HD * par
                            i = dve.scalar_tensor_tensor(out=hS[r, s, d, pt, n:n + HD], in0=hS[r, s, d, pt, n:n + HD],
                                                         scalar=hE[r, pt, LV, end:end + 1],
                                                         in1=PS[r, 7, P * pt + n:P * pt + n + HD], op0=ALU.mult, op1=ALU.add)
                    i.then_inc(h_staken, 1)

                for i, m in enumerate(MIX):
                    o = o_tok[:, m].rearrange("p t n -> p (t n)")
                    o4 = o.rearrange("p (h n) -> p h n", n=HD)
                    ss = ho_ss[:, 20 * m:20 * m + 20]
                    dve.wait_ge((g_otaken, h_otaken, m_otaken)[m], len(UNITS))
                    if i == 0:
                        dve.wait_ge(n_in, 48)
                    dve_order.done(dve.tensor_tensor(osq, o, o, ALU.mult))
                    dve_order.done(dve.tensor_reduce(ss, osq4, AX.X, ALU.add))
                    dve.tensor_scalar(ss, ss, 1.0 / HD, EPS, ALU.mult, ALU.add).then_inc(n_ss, 1)
                    dve.wait_ge(n_root, i + 1)
                    dve_order.done(dve.reciprocal(ss, ss))
                    dve_order.done(dve.tensor_tensor(o4, o4, spread(ss, 2, HD), ALU.mult))
                    dve.tensor_tensor(o4, o4, spread(norm_row[:, m, :], 1, 20), ALU.mult).then_inc(n_on, 1)
                    for pt in range(2):
                        dve.wait_ge(n_tr, 2 * i + pt + 1)
                        y = yT[:, 2 * m + pt, :]
                        b = 2 * pt
                        if m == 1:
                            dst = y[:, 0:SMP].rearrange("p (r w) -> p w r", w=GW)
                            src = PS[:, b, :].rearrange("p (w r) -> p w r", r=SMP // GW)
                        else:
                            dst, src = y[:, 0:SMP], PS[:, b, :]
                        dve.tensor_tensor(dst, dst, src, ALU.mult)
                        dve.tensor_tensor(y[:, SMP:TOK], y[:, SMP:TOK], PS[:, b + 1, 0:P], ALU.mult).then_inc(n_taken, 1)

            @block.scalar
            def _(act):
                act_order = Steps(act, "act_order1")
                act.wait_ge(cond_in, 32)
                act.activation(scond[:, :, :].rearrange("p k c -> p c k"), cond[:, :, :], ACT.Silu).then_inc(cond_silu, 1)
                act.wait_ge(x_in, 32)
                for t in range(NT):
                    i = act.activation(junk, xt[:, t, :], ACT.Square, accum_out=sumsq[:, t:t + 1])
                    if t < NT - 1:
                        act_order.done(i)
                i.then_inc(sq1_done, 1)
                act.wait_ge(mean1, 1)
                act.activation(rstd[:, 0:NT], sumsq[:, 0:NT], ACT.Sqrt).then_inc(root1, 1)
                for k in range(KT):
                    act.wait_ge(xT_ready, k + 1)
                    act.wait_ge(scl_ready, 1)
                    act.activation(hT[:, k, SMP:TOK], PS[:, 2 + k % 2, 0:P], ACT.Identity, scale=scl[:, k, 1:2],
                                   bias=modT[:, 0, k, 1:2]).then_inc(hT_pro, 1)
                act.wait_ge(lb_work, 1)
                act.activation(lbt[0], lbt[1], ACT.Exp).then_inc(lb_e, 1)
                def leave(dst_s, dst_p, b0, func, scale=1.0):
                    act.activation(dst_s, PS[:, b0, :], func, scale=scale)
                    act.activation(dst_p, PS[:, b0 + 1, 0:P], func, scale=scale).then_inc(proj_taken, 1)

                PRO = slice(SMP + 2, SMP + 2 + P)

                def silu_qkv():
                    act.wait_ge(gdn_conv_read, 1)
                    act.activation(qkT[:, :, 0:SMP], cbuf[:, 0:4, 0:SMP], ACT.Silu).then_inc(silu_done, 1)
                    act.activation(qkT[:, :, SMP:TOK], cbuf[:, 0:4, PRO], ACT.Silu).then_inc(silu_done, 1)
                    act.activation(vT[:, :, 0:SMP], cbuf[:, 4:6, 0:SMP], ACT.Silu).then_inc(silu_done, 1)
                    act.activation(vT[:, :, SMP:TOK], cbuf[:, 4:6, PRO], ACT.Silu).then_inc(silu_done, 1)

                GATE_AT = dict(ga=0, gb=2, oc=4)
                for n, (g, i) in enumerate(OUTPUTS):
                    name, extra, kind = GROUPS[g]
                    b0 = 2 * (n % 4)
                    act.wait_ge(proj_ready, n + 1)
                    if name in ("qa", "ka", "va", "ud"):
                        j = {"qa": 0, "ka": 2, "va": 4, "ud": 2 * (extra // MW)}[name] + i
                        if n == 0:
                            act.wait_ge(pads_zero, 3)
                        if name == "ud" and extra == 0 and i == 0:
                            silu_qkv()
                        leave(pre[:, j, 2:2 + SMP], pre[:, j, SMP + 4:SMP + 4 + P], b0, ACT.Copy)
                    elif name in GATE_AT:
                        j = GATE_AT[name] + i
                        leave(yT[:, j, 0:SMP], yT[:, j, SMP:TOK], b0, ACT.Silu if name == "ga" else ACT.Sigmoid)
                    elif name == "qb":
                        act.activation(hqT[:, i, 0:SMP].rearrange("p (w r) -> p w r", r=SMP // GW),
                                       PS[:, b0, :].rearrange("p (r w) -> p w r", w=GW), ACT.Copy)
                        act.activation(hqT[:, i, SMP:TOK], PS[:, b0 + 1, 0:P], ACT.Copy).then_inc(proj_taken, 1)
                    elif name in ("qc", "kc"):
                        j = i if name == "qc" else 2 + i
                        leave(mqkT[:, j, 0:SMP], mqkT[:, j, SMP:TOK], b0, ACT.Copy, 1.0 if name == "qc" else HD ** -0.5)
                    elif name == "ib":
                        act.activation(hv[:, i, :], PS[:, b0, 0:MW], ACT.Copy).then_inc(proj_taken, 1)
                    elif name == "fb":
                        act.activation(fgate[:, i, extra:extra + MW], PS[:, b0, 0:MW], ACT.Sigmoid).then_inc(proj_taken, 1)
                    elif name == "vc":
                        act.activation(mv[:, i, :, 0:HD], PS[:, b0, 0:MW].rearrange("p (h n) -> p h n", h=4),
                                       ACT.Copy).then_inc(proj_taken, 1)
                    else:
                        act.activation(smt[:, i].rearrange("p g (par pt) -> p g par pt", par=2),
                                       PS[:, b0, 0:32].rearrange("p (g pt par) -> p g par pt", pt=2, par=2),
                                       ACT.Copy).then_inc(proj_taken, 1)
                act.activation(beta[:, :, :, :], smt[:, :, 2:4, :], ACT.Sigmoid).then_inc(beta_done, 1)
                act.wait_ge(softin, 1)
                act_order.done(act.activation(spa[:, :, :, :], spi[:, :, :, :], ACT.Abs))
                act_order.done(act.activation(spa[:, :, :, :], spa[:, :, :, :], ACT.Exp, scale=-1.0))
                act.activation(nalog[:, :], prm[:, 8:16], ACT.Exp).then_inc(alog_exp, 1)
                act.activation(spa[:, :, :, :], spa[:, :, :, :], ACT.Ln, bias=1.0).then_inc(softlog, 1)
                act.wait_ge(scal_done, 1)
                act.activation(egc[:, :, :, :], cs[:, :, :, 0, :], ACT.Exp).then_inc(egc_done, 1)
                act.wait_ge(l2_eps, 1)
                act.activation(rq, rq, ACT.Sqrt).then_inc(l2_root, 1)
                act.wait_ge(hy_conv, 1)
                act.activation(hy[:, :, 0:SMP], cbuf[:, 0:4, 0:SMP], ACT.Copy)
                act.activation(hy[:, :, SMP:TOK], cbuf[:, 0:4, PRO], ACT.Copy).then_inc(hy_out, 1)
                act.activation(yT[:, 6:8, 0:SMP], cbuf[:, 4:6, 0:SMP], ACT.Copy)
                act.activation(yT[:, 6:8, SMP:TOK], cbuf[:, 4:6, PRO], ACT.Copy).then_inc(hy_out, 1)
                for n in range(2 * NT):
                    dst = kv_tok[:, n, :] if n < NT else mh_tok[:, n - NT, :]
                    act.wait_ge(tr_ready, n + 1)
                    act.activation(dst, PS[:, n % 4, :], ACT.Copy).then_inc(tr_taken, 1)

                for u, (d, t, s) in enumerate(UNITS):
                    act.wait_ge(g_x, u + 1)
                    act.activation(gDT, gX, ACT.Exp, scale=-1.0).then_inc(g_dt, 1)
                    act.activation(gEGB, heads(PS[:, 0, :]), ACT.Exp).then_inc(g_egb, 1)
                    act.activation(gel, gel, ACT.Exp).then_inc(g_el, 1)
                    act.wait_ge(g_uw, u + 1)
                    uw = PS[:, 5, :].rearrange("p (par pt n) -> p pt par n", par=2, pt=2)
                    act.activation(gU.rearrange("p pt (par n) -> p pt par n", par=2), uw[:, :, :, 0:HD], ACT.Copy)
                    act.activation(gwt.rearrange("p pt (par n) -> p pt par n", par=2), uw[:, :, :, HD:P], ACT.Copy,
                                   scale=-1.0).then_inc(g_wt, 1)
                    act.wait_ge(g_wTr, u + 1)
                    act.activation(gwT.rearrange("p pt n -> p (pt n)"), PS[:, 6, 0:256], ACT.Copy).then_inc(g_wT, 1)

                for u, (d, t, s) in enumerate(UNITS):
                    act.wait_ge(m_sm, u + 1)
                    if u > 0:
                        act.wait_ge(m_kw, u)
                    act.activation(mex[:, :, :], mex[:, :, :], ACT.Exp).then_inc(m_ex, 1)
                    act.wait_ge(m_x, u + 1)
                    act.activation(mWD, mX, ACT.Exp, scale=-1.0).then_inc(m_wd, 1)
                    act.wait_ge(m_eqx, u + 1)
                    act.activation(mDC, mDC, ACT.Exp, scale=-1.0).then_inc(m_eq, 1)

                for u, (d, t, s) in enumerate(UNITS):
                    if u == 0:
                        act.wait_ge(fo_done, 1)
                    else:
                        act.wait_ge(h_x, u)
                    act.activation(hlt, fgate[:, t, MW * d:MW * d + MW], ACT.Ln).then_inc(h_lt, 1)
                    act.wait_ge(h_x, u + 1)
                    if u == 0:
                        act.wait_ge(g_staken, len(UNITS))
                    else:
                        act.wait_ge(h_staken, u)
                    act.activation(hE.rearrange("p pt l n -> p (pt l n)"), PS[:, 0:4, :].rearrange("p b n -> p (b n)"),
                                   ACT.Exp).then_inc(h_e, 1)
                    act.activation(hkd, PS[:, 5, 0:256], ACT.Exp).then_inc(h_ek, 1)
                    act.wait_ge(h_kT, u + 1)
                    act.activation(hkT, PS[:, 4, 0:256], ACT.Copy).then_inc(h_kTs, 1)
                for i, m in enumerate(MIX):
                    ss = ho_ss[:, 20 * m:20 * m + 20]
                    act.wait_ge(n_ss, i + 1)
                    act.activation(ss, ss, ACT.Sqrt).then_inc(n_root, 1)

            @block.gpsimd
            def _(pool):
                pool_order = Steps(pool, "pool_order1")
                pool.memset(rows[:, :], 0.0).then_inc(rows_zero, 1)

                for k in range(KT):
                    pool.wait_ge(hT_smp, k + 1)
                    pool.tensor_copy(hTp[:, k].rearrange("p (w r) -> p w r", r=SMP // GW),
                                     hT[:, k, 0:SMP].rearrange("p (r w) -> p w r", w=GW)).then_inc(hTp_done, 1)

                pool.wait_ge(mod_ready, 6)
                pool.memset(pre[:, :, 0:2], 0.0).then_inc(pads_zero, 1)
                pool.memset(pre[:, :, SMP + 2:SMP + 4], 0.0).then_inc(pads_zero, 1)
                pool.memset(pre[:, :, PRE_W - 2:PRE_W], 0.0).then_inc(pads_zero, 1)

                pool.memset(mv[:, :, :, HD:HD + 1], 1.0).then_inc(ones_col, 1)
                pool.wait_ge(silu_done, 2)
                pool.tensor_tensor(sq, qkT.rearrange("p k n -> p (k n)"), qkT.rearrange("p k n -> p (k n)"), ALU.mult).then_inc(sq_done, 1)
                pool.wait_ge(hy_conv, 1)
                pool.memset(part(r2_at, 3088), 0.0).then_inc(states_zero, 1)
                for u, (d, t, s) in enumerate(UNITS):
                    if u == 0:
                        pool.wait_ge(tr_taken, 5)
                        pool.wait_ge(scal_done, 1)
                        pool.wait_ge(dve_beg, 1)
                    else:
                        pool.wait_ge(g_uw, u)
                    kh = kv_tok[:, t, 0:MW].rearrange("p (pt par n) -> p par pt n", pt=2, par=2)
                    vh = kv_tok[:, t, MW:512].rearrange("p (pt par n) -> p par pt n", pt=2, par=2)
                    bkv = gBK.rearrange("p (par pt) n -> p par pt n", par=2)
                    bt = beta[:, t, d, :].rearrange("p (par pt) -> p par pt", par=2)
                    bg = beg[:, d, t, :].rearrange("p (par pt) -> p par pt", par=2)
                    for par in range(2):
                        pool.tensor_tensor(bkv[:, par, :, 0:HD], vh[:, par], spread(bt[:, par], 2, HD), ALU.mult)
                        i = pool.tensor_tensor(bkv[:, par, :, HD:P], kh[:, par], spread(bg[:, par], 2, HD), ALU.mult)
                    i.then_inc(g_bk, 1)
                    pool.wait_ge(g_mt, u + 1)
                    for n in range(LV):
                        if LV * u + n >= 2:
                            pool.wait_ge(g_lv1, LV * u + n - 1)
                        pool.tensor_tensor(gMS[n % 2], gMT, spread(strict[:, d, LV - 1 - n, :], 1, 4), ALU.mult).then_inc(g_ms, 1)
                    pool.wait_ge(g_el, u + 1)
                    el = gel.rearrange("p (par pt) -> p par pt", par=2)
                    for par in range(2):
                        i = pool.tensor_tensor(gkd.rearrange("p pt (par n) -> p par pt n", par=2)[:, par], kh[:, par],
                                               spread(el[:, par], 2, HD), ALU.mult)
                    i.then_inc(g_kd, 1)
                pool.memset(mst[:, 1], 0.0).then_inc(m_zero, 1)
                for u, (d, t, s) in enumerate(UNITS):
                    pool.wait_ge(m_ex, u + 1)
                    if u == 0:
                        pool.wait_ge(tr_taken, 2 * NT)
                    else:
                        pool.wait_ge(m_st, u)
                    kh = mh_tok[:, t, 0:MW].rearrange("p (pt par n) -> p par pt n", pt=2, par=2)
                    wk = mex[:, 0, :].rearrange("p (par pt) -> p par pt", par=2)
                    for par in range(2):
                        i = pool.tensor_tensor(mkw.rearrange("p pt (par n) -> p par pt n", par=2)[:, par], kh[:, par],
                                               spread(wk[:, par], 2, HD), ALU.mult)
                    i.then_inc(m_kw, 1)
                for u, (d, t, s) in enumerate(UNITS):
                    if u == 0:
                        pool.wait_ge(fo_done, 1)
                    else:
                        pool.wait_ge(h_kT, u)
                        pool.wait_ge(h_kd, u)
                    pool.tensor_scalar(hkt, fgate[:, t, MW * d:MW * d + MW], -1.0, 1.0, ALU.mult, ALU.add).then_inc(h_kt, 1)
                    pool.wait_ge(h_e, u + 1)
                    pool.wait_ge(h_kTs, u + 1)
                    for pt in range(2):
                        i = pool.tensor_tensor(hKE[:, pt], spread(hkT[:, P * pt:P * pt + P], 1, LV), hE[:, pt, 0:LV, :], ALU.mult)
                    i.then_inc(h_ke, 1)
                    pool.wait_ge(h_ek, u + 1)
                    pool.wait_ge(h_kt, u + 1)
                    pool.tensor_tensor(hkd, hkd, hkt, ALU.mult).then_inc(h_kd, 1)

        nc.all_engine_barrier()
        nc.clear_and_free_semaphores(stage_sems)
        stage_sems.clear()
        nc.all_engine_barrier()

        dft_at = r2_at + 3900
        fwd5 = part(dft_at, 4096).rearrange("p (t n) -> p t n", t=4)
        inv5 = part(dft_at + 4096, 4096).rearrange("p (t n) -> p t n", t=8)
        fwd1 = part(dft_at + 8192, 256).rearrange("p (t n) -> p t n", t=1)
        inv1 = part(dft_at + 8448, 256).rearrange("p (t n) -> p t n", t=2)
        dec_at = dft_at + 8704
        decay = part(dec_at, NT * 512).rearrange("p (t n) -> p t n", t=NT)
        feats = part(dec_at + 2560, TOK)[0:33]
        fw1, fw2, fw3 = part(r3_at, HD)[0:33], part(r3_at + 64, HD)[0:HD], part(r3_at + 128, 1024)[0:HD]
        fcol = small(3)[0:HD]
        fz, fn, hid1, hid2 = (part(x_at + TOK * i, TOK)[0:HD] for i in range(4))
        hf = part(r1_at, NT * 1024).rearrange("p (t o s n) -> p t o s n", t=NT, o=2, s=2)
        hsum = part(r1_at + 8960, NT * 512).rearrange("p (t o n) -> p t o n", t=NT, o=2)
        hdif = part(r1_at + 11520, NT * 512).rearrange("p (t o n) -> p t o n", t=NT, o=2)
        hsq = [part(x_at + 2560 + 1024 * i, 1024).rearrange("p (o s n) -> p o s n", o=2, s=2) for i in range(2)]
        rn = part(x_at, 1024).rearrange("p (s n) -> p s n", s=2)
        HA = part(r1_at, 2560).rearrange("p (f n) -> p f n", f=5)
        HB = part(r1_at + 2560, 2560).rearrange("p (f n) -> p f n", f=5)
        HC = part(r1_at + 5120, 1024).rearrange("p (s n) -> p s n", s=2)
        spec = part(x_at + 1024, 2560).rearrange("p (f n) -> p f n", f=10)
        z1 = part(dec_at, 2 * TOK).rearrange("p (k n) -> p k n", k=2)
        ctmp = part(dec_at + 1300, TOK)
        z1_tok = part(r1_at + 14080, NT * MW).rearrange("p (t n) -> p t n", t=NT)
        pr = [part(x_at + 3584, 1024).rearrange("p (k n) -> p k n", k=4), part(r3_at, 1024).rearrange("p (k n) -> p k n", k=4)]
        FT = [(0, f) for f in range(4)] + [(1, 0)]
        (f_in, f_dft, f_1, f_z, f_s, f_h, f_hf, f_sq, f_nrm, f_ne, f_nr, f_rn, f_sd, f_H, f_Ht, f_HC, c_Z, c_pr, c_Y, c_y,
         c_out, c_z1, c_tr, c_trt, f_row) = (sem("f_" + n) for n in
         "in dft 1 z s h hf sq nrm ne nr rn sd H Ht HC cZ cpr cY cy cout cz1 ctr ctrt row".split())
        w_out = part(r1_at, 8192).rearrange("p (k n) -> p k n", k=8)
        xn = part(r1_at + 8192, 5120).rearrange("p (t n) -> p t n", t=NT)
        gate_row = part(r2_at, 4096).rearrange("p (g c n) -> p g c n", g=2, c=2)
        gdiag = [part(r2_at + 4096 + 1024 * i, 1024).rearrange("p (k n) -> p k n", k=8) for i in range(2)]
        acc = part(r2_at + 6144, 5120).rearrange("p (t n) -> p t n", t=NT)
        otmp = [part(r1_at + 13312 + 512 * i, 512) for i in range(2)]
        h2T = part(y_at, 5120).rearrange("p (k n) -> p k n", k=KT)
        rw = part(r3_at, 512).rearrange("p (k n) -> p k n", k=KT)
        rb = part(r3_at + 512, NE)
        score = part(r3_at + 576, NT * NE).rearrange("p (t n) -> p t n", t=NT)
        gate = part(r3_at + 896, NT * NE).rearrange("p (t n) -> p t n", t=NT)
        biased = small(NE)
        top8, gsum = small(8), small(8)
        fin_row = part(r1_at + 14336, 1024)
        scl2 = small(16).rearrange("p (k c) -> p k c", c=2)
        (o_w, o_x, o_rw, o_rb, o_fg, o_scl, o_gd, o_gr, o_gt, o_ps, o_mul, o_x1, n2_sq, n2_mean, n2_root, n2_xn, n2_tr, n2_s,
         n2_p, r_ps, r_sig, r_g, b_ps, b_cp) = (sem("o_" + n) for n in
         "w x rw rb fg scl gd gr gt ps mul x1 sq mean root xn tr s p rps rsig rg bps bcp".split())
        mask = part(r1_at, NT * NE).rearrange("p (t n) -> p t n", t=NT)
        h2 = xn
        U = 4
        BLOCKS = TOK * TOPK // P + NE
        GROUPS = (BLOCKS + U - 1) // U
        PAIRS = NT * TOPK
        LEAST = PAIRS // U
        MAGIC = 12582912.0
        ew = [part(a, 3072) for a in (r2_at + 11264, r2_at + 14336, r1_at + 8192, r1_at + 11264)]
        eg = [w[:, 0:1024].rearrange("p (k f) -> p k f", k=KT) for w in ew]
        eu = [w[:, 1024:2048].rearrange("p (k f) -> p k f", k=KT) for w in ew]
        ed = [w[:, 2048:3072] for w in ew]
        sact, sup, shid = (part(a, TOK) for a in (r2_at + 4096, r2_at + 4736, r2_at + 5376))

        keep = [r2_at + 17408]
        def kept(words):
            keep[0] += words
            assert keep[0] <= r2_at + 19300
            return part(keep[0] - words, words)
        index = kept(P + NT)
        slot_token = kept(BLOCKS + 1).bitcast(U32)
        block_expert = kept(P + 1)[0:1].bitcast(U32)
        dest_u = kept(PAIRS).bitcast(U32)
        token_col = [kept(1).bitcast(U32) for _ in range(U)]
        D1 = kept(NT * NE).rearrange("p (t n) -> p t n", t=NT)
        d8 = kept(PAIRS).rearrange("p (t k) -> p t k", t=NT)
        g8 = kept(PAIRS).rearrange("p (t k) -> p t k", t=NT)
        pick = kept(TOPK * NE).rearrange("p (k n) -> p k n", k=TOPK)
        taken = [r1_at + NT * NE]
        def scratch(words):
            taken[0] += words
            assert taken[0] <= r1_at + 8192
            return part(taken[0] - words, words)
        off = scratch((NT + 1) * NE).rearrange("p (t n) -> p t n", t=NT + 1)
        cum = [scratch(2 * NE) for _ in range(2)]
        cmpb, ecol, ngf, erow = scratch(NE), scratch(1), scratch(1), scratch(P)
        dest, hi, lo = scratch(PAIRS), scratch(PAIRS), scratch(PAIRS)
        at_slot = [scratch(TOPK * P).rearrange("p (k n) -> p k n", k=TOPK) for _ in range(2)]
        at_block = [scratch(TOPK * (BLOCKS + 1)).rearrange("p (k n) -> p k n", k=TOPK) for _ in range(2)]
        xg = [part(r1_at + 1024 * i, 1024) for i in range(U)]
        xT = [part(r1_at + 4096 + 1024 * i, 1024).rearrange("p (k n) -> p k n", k=KT) for i in range(2)]
        yb = [part(r1_at + 6144 + 1024 * i, 1024) for i in range(2)]
        gact = part(r2_at + 4096, P)
        hid = [part(r2_at + 4224 + P * i, P) for i in range(2)]
        GB = 8
        back = [part(r1_at + 1024 * i, 1024) for i in range(GB)]
        fmul = part(r2_at + 11264, 1024)
        fjunk = part(r2_at + 12288, 1024)

        m_idx, m_cnt, m_off, m_hi, m_at, m_bl, m_tab, m_ecol, m_erow, m_exp, m_tok, m_dest, m_beq = (
            sem("m_" + n) for n in "idx cnt off hi at bl tab ecol erow exp tok dest beq".split())
        s_w, s_gu, s_up, s_act, s_hid, s_ps, s_acc = (sem("s_" + n) for n in "w gu up act hid ps acc".split())
        h2_out, x_col = sem("h2_out"), sem("x_col")
        e_w, e_x = [sem(f"e_w{j}") for j in range(U)], [sem(f"e_x{j}") for j in range(U)]
        e_tr, e_xT, e_gu, e_silu, e_hid, e_ps, e_y = (sem("e_" + n) for n in "tr xT gu silu hid ps y".split())
        e_out = [sem("e_out0"), sem("e_out1")]
        g_in, g_used = [sem(f"g_in{j}") for j in range(GB)], sem("g_used")
        y_all = sem("y_all")
        f_x2, f_sq2, f_mn, f_rt, f_y, y_out = (sem("f2_" + n) for n in "x2 sq mn rt y out".split())

        def group_count(eng):
            eng.wait_ge(m_exp, 1)
            return eng.value_load(block_expert[0:1, P:P + 1], min_val=0, max_val=GROUPS - LEAST) + LEAST

        with nc.Block() as block:

            @block.sync
            def _(sp):
                sp.dma_start(feats, T["feats"]).then_inc(f_in, 16)
                sp.dma_start(fw1, T["filt_w1"].rearrange("a k n -> (a k) n")).then_inc(f_in, 16)
                sp.dma_start(fw2, T["filt_w2"].rearrange("a k n -> (a k) n")).then_inc(f_in, 16)
                sp.dma_start(fw3, T["filt_w3"].rearrange("a k n -> (a k) n")).then_inc(f_in, 16)
                for i, n in enumerate(("filt_b1", "filt_freq", "filt_b2")):
                    sp.dma_start(fcol[:, i:i + 1], T[n].rearrange("a n -> n a"), allow_slow_non_contiguous=True).then_inc(f_in, 16)
                sp.dma_start(decay.rearrange("p t n -> p (t n)"), T["decay"]).then_inc(f_in, 16)
                sp.dma_start(part(dft_at, 8704), T["dfts"]).then_inc(f_dft, 16)
                sp.wait_ge(c_z1, 8)
                sp.wait_ge(c_trt, NT)
                sp.dma_start(w_out[:, :, :], T["w_out"].rearrange("a (k p) n -> p (a k) n", p=P)).then_inc(o_w, 16)
                sp.dma_start(xt[:, 0:4, :], T["x_sample"].rearrange("a (t p) d -> p (a t) d", p=P)).then_inc(o_x, 16)
                sp.dma_start(xt[:, 4, :], T["x_prompt"].rearrange("a p d -> p (a d)")).then_inc(o_x, 16)
                sp.dma_start(rw[:, :, :], T["router_w"].rearrange("a (p k) n -> p (a k) n", k=KT)).then_inc(o_rw, 16)
                sp.dma_start(rb, T["router_bias"].to_broadcast([P, NE])).then_inc(o_rb, 16)
                sp.dma_start(fin_row, T["final_g"].rearrange("(a n) -> a n", a=1).to_broadcast([P, D])).then_inc(o_fg, 16)
                wg = T["exp_w_gate"].rearrange("a e (p k) f -> p (a e) k f", k=KT)
                wu = T["exp_w_up"].rearrange("a e (p k) f -> p (a e) k f", k=KT)
                wd = T["exp_w_down"].rearrange("a e f d -> f (a e) d")
                y_rows = T["y_rows"].rearrange("(b p) d -> p b d", p=P)

                sp.dma_start(eg[1], T["sh_w_gate"].rearrange("a (p k) f -> p (a k) f", k=KT)).then_inc(s_w, 16)
                sp.dma_start(eu[1], T["sh_w_up"].rearrange("a (p k) f -> p (a k) f", k=KT)).then_inc(s_w, 16)
                sp.dma_start(ed[1], T["sh_w_down"].rearrange("a f d -> f (a d)")).then_inc(s_w, 16)
                sp.dma_start(index, T["index"]).then_inc(m_idx, 16)
                for t in range(NT):
                    sp.wait_ge(b_cp, 2 * t + 2)
                    sp.dma_start(T["h2_rows"][t * P:(t + 1) * P, :], h2[:, t, :]).then_inc(h2_out, 16)

                def load_block(b, j):
                    e = sp.value_load(block_expert[0:1, bass.ds(b, 1)], min_val=0, max_val=NE - 1)
                    sp.dma_start(eg[j], wg[:, bass.ds(e, 1)].rearrange("p a k f -> p (a k) f")).then_inc(e_w[j], 16)
                    sp.dma_start(eu[j], wu[:, bass.ds(e, 1)].rearrange("p a k f -> p (a k) f")).then_inc(e_w[j], 16)
                    sp.dma_start(ed[j], wd[:, bass.ds(e, 1)].rearrange("p a d -> p (a d)")).then_inc(e_w[j], 16)

                def store_block(b, j):
                    sp.wait_ge(e_y, b + 1)
                    sp.dma_start(y_rows[:, bass.ds(b, 1)].rearrange("p b d -> p (b d)"), yb[j % 2]).then_inc(e_out[j % 2], 16)

                groups = group_count(sp)
                load_block(0, 0)
                sp.wait_ge(s_ps, 2 * NT)
                load_block(1, 1)
                sp.wait_ge(h2_out, 16 * NT)
                load_block(2, 2)
                load_block(3, 3)
                with sp.Fori(1, groups) as i:
                    for j in range(U):
                        sp.wait_ge(e_ps, U * i + (j + 1 - U))
                        load_block(U * i + j, j)
                        store_block(U * i + (j - U), j)
                for j in range(U):
                    store_block(U * groups + (j - U), j)
                for t in range(NT):
                    sp.wait_ge(f_y, t + 1)
                    dst = T["y_sample"].rearrange("a (t p) d -> p (a t) d", p=P)[:, t] if t < 4 else T["y_prompt"][0]
                    sp.dma_start(dst, acc[:, t, :]).then_inc(y_out, 16)
                sp.wait_ge(y_out, 16 * NT)

            @block.tensor
            def _(pe):
                pe.wait_ge(f_in, 16 * 8)
                for i, (w, src, b) in enumerate(((fw1, feats, 0), (fw2, hid1, 2))):
                    if i:
                        pe.wait_ge(f_s, 1)
                    pe.matmul(PS[0:HD, b, :], w, src[:, 0:SMP], start=True, stop=True)
                    pe.matmul(PS[0:HD, b + 1, 0:P], w, src[:, SMP:TOK], start=True, stop=True).then_inc(f_1, 1)
                pe.wait_ge(f_s, 2)
                for t in range(NT):
                    if t >= 2:
                        pe.wait_ge(f_hf, t - 1)
                    for o in range(2):
                        mm = pe.matmul(PS[:, 4 + 2 * (t % 2) + o, :], hid2[:, t * P:(t + 1) * P], fw3[:, 512 * o:512 * o + 512],
                                       start=True, stop=True)
                    mm.then_inc(f_h, 1)
                for t in range(NT):
                    pe.wait_ge(f_sq, t + 1)
                    for side in range(2):
                        mm = pe.matmul(PS[:, t // 4, :], ones, hsq[t % 2][:, :, side, :],
                                       start=t in (0, 4) and side == 0, stop=t in (3, 4) and side == 1)
                    mm.then_inc(f_nrm, 1)
                pe.wait_ge(f_sd, NT)
                pe.wait_ge(f_dft, 16)
                for i, (s, f) in enumerate(FT):
                    m, t0, nt = (fwd1, 4, 1) if s else (fwd5, 0, 4)
                    n = P if s else SMP
                    if i == 0:
                        pe.wait_ge(f_rn, 1)
                        pe.wait_ge(f_hf, NT)
                    if i >= 1:
                        pe.wait_ge(f_Ht, i)
                    for b, base, h in ((2, 0, hsum), (3, n, hdif)) + (((4, n, hsum),) if f == 0 else ()):
                        for t in range(nt):
                            mm = pe.matmul(PS[:, b, :], m[:, t, base + f * P:base + f * P + P],
                                           h[:, t0 + t].rearrange("p o n -> p (o n)"), start=t == 0, stop=t == nt - 1)
                    mm.then_inc(f_H, 1)
                for o in range(2):
                    if o == 1:
                        for t in range(NT):
                            pe.wait_ge(c_z1, 2 if t < 4 else 4)
                            if t >= 2:
                                pe.wait_ge(c_trt, t - 1)
                            for pt in range(2):
                                mm = pe.transpose(PS[:, t % 2, P * pt:P * pt + P], z1[:, pt, t * P:(t + 1) * P], ident)
                            mm.then_inc(c_tr, 1)
                        pe.wait_ge(c_trt, NT)
                    for i, (s, f) in enumerate(FT):
                        m, t0, nt = (fwd1, 4, 1) if s else (fwd5, 0, 4)
                        n = P if s else SMP
                        if o == 0 and i < 2:
                            pe.wait_ge(f_Ht, len(FT))
                        if len(FT) * o + i >= 2:
                            pe.wait_ge(c_pr, len(FT) * o + i - 1)
                        for part_, base in ((0, 0), (1, n)):
                            for t in range(nt):
                                z = z1_tok[:, t0 + t, :] if o else mh_tok[:, t0 + t, MW:512]
                                mm = pe.matmul(PS[:, 2 + (len(FT) * o + i) % 2, MW * part_:MW * part_ + MW],
                                               m[:, t, base + f * P:base + f * P + P], z, start=t == 0, stop=t == nt - 1)
                        mm.then_inc(c_Z, 1)
                    pe.wait_ge(c_Y, len(FT) * (o + 1))
                    if o == 1:
                        pe.wait_ge(c_out, 4)
                    for pt in range(2):
                        for k in range(8):
                            mm = pe.matmul(PS[:, 4 + pt, :], spec[:, k, P * pt:P * pt + P], inv5[:, k, :], start=k == 0, stop=k == 7)
                    mm.then_inc(c_y, 1)
                    for pt in range(2):
                        for k in range(2):
                            mm = pe.matmul(PS[:, 6, P * pt:P * pt + P], spec[:, 8 + k, P * pt:P * pt + P], inv1[:, k, :],
                                           start=k == 0, stop=k == 1)
                    mm.then_inc(c_y, 1)
                for n, (g, c) in enumerate([(g, c) for g in range(2) for c in range(2)]):
                    pe.wait_ge(o_gd, n + 1)
                    if n >= 2:
                        pe.wait_ge(o_gt, n - 1)
                    for half in range(2):
                        mm = pe.matmul(PS[:, 2 * (n % 2) + half, :], ones,
                                       gdiag[n % 2][:, 4 * half:4 * half + 4, :].rearrange("p k n -> p (k n)"), start=True, stop=True)
                    mm.then_inc(o_gr, 1)
                pe.wait_ge(o_w, 16)
                pe.wait_ge(c_z1, 8)
                for n in range(2 * NT):
                    t, half = n // 2, n % 2
                    if n >= 4:
                        pe.wait_ge(o_mul, n - 3)
                    for k in range(8):
                        mm = pe.matmul(PS[:, 4 + n % 4, :], yT[:, k, t * P:(t + 1) * P], w_out[:, k, 512 * half:512 * half + 512],
                                       start=k == 0, stop=k == 7)
                    mm.then_inc(o_ps, 1)
                pe.wait_ge(o_gt, 4)
                pe.wait_ge(n2_xn, NT)
                for k in range(KT):
                    if k >= 2:
                        pe.wait_ge(n2_s, k - 1)
                        pe.wait_ge(n2_p, k - 1)
                    for t in range(NT):
                        dst = PS[:, k % 2, t * P:(t + 1) * P] if t < 4 else PS[:, 2 + k % 2, 0:P]
                        mm = pe.transpose(dst, xn[:, t, k:D:KT], ident)
                    mm.then_inc(n2_tr, 1)
                pe.wait_ge(o_rw, 16)
                pe.wait_ge(n2_s, KT)
                pe.wait_ge(n2_p, KT)
                pe.wait_ge(o_mul, 2 * NT)
                for t in range(NT):
                    if t == 4:
                        pe.wait_ge(r_sig, 1)
                    for k in range(KT):
                        mm = pe.matmul(PS[:, 4 + t % 4, 0:NE], h2T[:, k, t * P:(t + 1) * P], rw[:, k, :], start=k == 0, stop=k == KT - 1)
                    mm.then_inc(r_ps, 1)
                for n in range(2 * NT):
                    t, half = n // 2, n % 2
                    if n >= 4:
                        pe.wait_ge(b_cp, n - 3)
                    for k in range(4):
                        mm = pe.transpose(PS[:, n % 4, k * P:(k + 1) * P], h2T[:, 4 * half + k, t * P:(t + 1) * P], ident)
                    mm.then_inc(b_ps, 1)

                pe.wait_ge(s_w, 48)
                pe.wait_ge(b_cp, 2 * NT)
                for w, b in ((eg[1], 0), (eu[1], 2)):
                    for half in range(2):
                        for k in range(KT):
                            mm = pe.matmul(PS[:, b + half, 0:320], w[:, k, :], h2T[:, k, 320 * half:320 * half + 320],
                                           start=k == 0, stop=k == KT - 1)
                    mm.then_inc(s_gu, 1)
                pe.wait_ge(r_sig, NT)
                pe.wait_ge(r_g, NT)
                mask_all = mask.rearrange("p t n -> p (t n)")
                pe.matmul(PS[:, 6, 0:NT * NE], after[:, 1, :], mask_all, start=True, stop=True)
                pe.matmul(PS[:, 7, 0:NT * NE], ones, mask_all, start=True, stop=True).then_inc(m_cnt, 1)
                for n in range(2 * NT):
                    t, half = n // 2, n % 2
                    if n == 0:
                        pe.wait_ge(s_hid, 1)
                    if n >= 2:
                        pe.wait_ge(s_acc, n - 1)
                    pe.matmul(PS[:, 4 + half, :], shid[:, t * P:(t + 1) * P], ed[1][:, 512 * half:512 * half + 512],
                              start=True, stop=True).then_inc(s_ps, 1)
                pe.wait_ge(m_ecol, 1)
                pe.wait_ge(m_off, NT + 1)
                pe.matmul(PS[0:1, 7, 0:P], ecol, ident, start=True, stop=True).then_inc(m_erow, 1)
                for t in range(NT):
                    pe.wait_ge(m_at, t + 1)
                    pe.wait_ge(m_bl, t + 1)
                    for k in range(TOPK):
                        mm = pe.matmul(PS[:, 6, 0:BLOCKS + 1], at_slot[t % 2][:, k, :], at_block[t % 2][:, k, :],
                                       start=t == 0 and k == 0, stop=t == NT - 1 and k == TOPK - 1)
                    mm.then_inc(m_tab, 1)

                def transpose_x(b, j, i1):
                    pe.wait_ge(e_x[j], 16 * i1)
                    for k in range(KT):
                        mm = pe.transpose(PS[:, k // 4, (k % 4) * P:(k % 4 + 1) * P], xg[j][:, k:D:KT], ident)
                    mm.then_inc(e_tr, 1)

                def gate_up(b, j, i1):
                    pe.wait_ge(e_w[j], 48 * i1)
                    pe.wait_ge(e_xT, b + 1)
                    for w, bank in ((eg[j], 2), (eu[j], 3)):
                        for k in range(KT):
                            mm = pe.matmul(PS[:, bank, 0:P], w[:, k, :], xT[j % 2][:, k, :], start=k == 0, stop=k == KT - 1)
                    mm.then_inc(e_gu, 1)

                def down(b, j, first=False):
                    pe.wait_ge(e_hid, b + 1)
                    if not first:
                        pe.wait_ge(e_y, b - 1)
                    for half in range(2):
                        mm = pe.matmul(PS[:, 4 + 2 * (j % 2) + half, :], hid[j % 2], ed[j][:, 512 * half:512 * half + 512],
                                       start=True, stop=True)
                    mm.then_inc(e_ps, 1)

                groups = group_count(pe)
                pe.wait_ge(m_tok, 1)
                pe.wait_ge(s_acc, 2 * NT)
                pe.wait_ge(s_up, 1)
                for j in range(U):
                    transpose_x(j, j, 1)
                    if j:
                        down(j - 1, j - 1, j <= 2)
                    gate_up(j, j, 1)
                with pe.Fori(1, groups) as i:
                    for j in range(U):
                        transpose_x(U * i + j, j, i + 1)
                        down(U * i + (j - 1), (j - 1) % U)
                        gate_up(U * i + j, j, i + 1)
                down(U * groups - 1, U - 1)

            @block.vector
            def _(dve):
                dve_order = Steps(dve, "dve_order2")
                TWO_PI = 2 * np.pi
                HI = 6.28125
                LO = float(TWO_PI - HI)
                MAGIC = 12582912.0
                for i in range(2):
                    b = 2 * i
                    dve.wait_ge(f_1, i + 1)
                    dve.tensor_scalar(fz[:, 0:SMP], PS[0:HD, b, :], fcol[:, 2 * i:2 * i + 1], fcol[:, 1:2], ALU.add, ALU.mult)
                    dve_order.done(dve.tensor_scalar(fz[:, SMP:TOK], PS[0:HD, b + 1, 0:P], fcol[:, 2 * i:2 * i + 1], fcol[:, 1:2],
                                                     ALU.add, ALU.mult))
                    dve_order.done(dve.tensor_scalar(fn, fz, 1.0 / TWO_PI, MAGIC, ALU.mult, ALU.add))
                    dve_order.done(dve.tensor_scalar(fn, fn, MAGIC, None, ALU.subtract))
                    dve_order.done(dve.scalar_tensor_tensor(out=fz, in0=fn, scalar=-HI, in1=fz, op0=ALU.mult, op1=ALU.add))
                    dve_order.done(dve.scalar_tensor_tensor(out=fz, in0=fn, scalar=-LO, in1=fz, op0=ALU.mult, op1=ALU.add))
                    dve.tensor_scalar(fz, fz, 3.1415925, -3.1415925, ALU.min, ALU.max).then_inc(f_z, 1)
                    dve.wait_ge(f_s, i + 1)
                for t in range(NT):
                    dve.wait_ge(f_h, t + 1)
                    for o in range(2):
                        i = dve.tensor_tensor(hf[:, t, o].rearrange("p s n -> p (s n)"), PS[:, 4 + 2 * (t % 2) + o, :],
                                              decay[:, t, :], ALU.mult)
                    i.then_inc(f_hf, 1)
                dve.wait_ge(f_nrm, NT)
                for s in range(2):
                    i = dve.tensor_scalar(rn[:, s, :], PS[:, s, :], EPS, None, ALU.add)
                i.then_inc(f_ne, 1)
                dve.wait_ge(f_nr, 1)
                dve.reciprocal(rn, rn).then_inc(f_rn, 1)
                dve.wait_ge(f_rn, 1)
                dve.wait_ge(f_sd, NT)
                for i, (s, f) in enumerate(FT):
                    dve.wait_ge(f_H, i + 1)
                    dve.tensor_tensor(HA[:, i, :], PS[:, 2, :], rn[:, s, :], ALU.mult)
                    j = dve.tensor_tensor(HB[:, i, :], PS[:, 3, :], rn[:, s, :], ALU.mult)
                    if f == 0:
                        dve_order.done(j)
                        dve.memset(HB[0:1, i, :], 0.0)
                        dve_order.done(dve.tensor_copy(HC[:, s, :], HA[:, i, :]))
                        j = dve.tensor_tensor(HC[0:1, s, :], PS[0:1, 4, :], rn[0:1, s, :], ALU.mult)
                    j.then_inc(f_Ht, 1)
                dve.wait_ge(f_Ht, len(FT))
                for o in range(2):
                    for i, (s, f) in enumerate(FT):
                        n = len(FT) * o + i
                        dve.wait_ge(c_Z, n + 1)
                        if n >= 2:
                            dve.wait_ge(c_Y, n - 1)
                        b, q = 2 + n % 2, pr[n % 2]
                        w = slice(MW * o, MW * o + MW)
                        hc = HC[:, s, w] if f == 0 else HA[:, i, w]
                        dve.tensor_tensor(q[:, 0, :], PS[:, b, 0:MW], HA[:, i, w], ALU.mult)
                        dve.tensor_tensor(q[:, 1, :], PS[:, b, MW:512], HB[:, i, w], ALU.mult)
                        dve.tensor_tensor(q[:, 2, :], PS[:, b, 0:MW], HB[:, i, w], ALU.mult)
                        dve.tensor_tensor(q[:, 3, :], PS[:, b, MW:512], hc, ALU.mult).then_inc(c_pr, 1)
                    for s in range(2):
                        dve.wait_ge(c_y, 2 * o + s + 1)
                        for pt in range(2):
                            cols = slice(0, SMP) if s == 0 else slice(SMP, TOK)
                            ps = PS[:, 4 + pt, :] if s == 0 else PS[:, 6, P * pt:P * pt + P]
                            z = z1[:, pt, cols] if o else hy[:, pt, cols]
                            dve.scalar_tensor_tensor(out=ctmp[:, cols], in0=z, scalar=tapsT[:, pt, 8 + o:9 + o], in1=ps,
                                                     op0=ALU.mult, op1=ALU.add).then_inc(c_out, 1)
                            dve.wait_ge(c_out, 4 * o + 2 * s + pt + 1)
                            dst, x = (yT[:, 6 + pt, cols], yT[:, 6 + pt, cols]) if o else (z1[:, pt, cols], hy[:, 2 + pt, cols])
                            dve.tensor_tensor(dst, x, ctmp[:, cols], ALU.mult).then_inc(c_z1, 1)
                            dve.wait_ge(c_z1, 4 * o + 2 * s + pt + 1)
                dve.wait_ge(c_z1, 8)
                dve_order.done(dve.tensor_scalar(scl2[:, :, :], modT[:, 4], 1.0, None, ALU.add))
                dve.tensor_tensor(scl2[:, :, :], scl2[:, :, :], spread(g2p, 2, 2), ALU.mult).then_inc(o_scl, 1)
                GR = [(g, c) for g in range(2) for c in range(2)]
                def gate_diag(n):
                    g, c = GR[n]
                    if n >= 2:
                        dve.wait_ge(o_gr, n - 1)
                    dve.tensor_tensor(gdiag[n % 2], spread(ident, 1, KT), spread(modT[:, 2 + 3 * g, :, c], 2, P),
                                      ALU.mult).then_inc(o_gd, 1)
                gate_diag(0)
                for n, (g, c) in enumerate(GR):
                    if n + 1 < 4:
                        gate_diag(n + 1)
                    dve.wait_ge(o_gr, n + 1)
                    dst = gate_row[:, g, c, :].rearrange("p (q k) -> p k q", k=KT)
                    b = 2 * (n % 2)
                    for half in range(2):
                        i = dve.tensor_copy(dst[:, 4 * half:4 * half + 4, :], PS[:, b + half, :].rearrange("p (k q) -> p k q", k=4))
                    i.then_inc(o_gt, 1)
                dve.wait_ge(o_gt, 4)
                dve.wait_ge(o_x, 32)
                for t in range(NT):
                    for half in range(2):
                        n = 2 * t + half
                        w = slice(512 * half, 512 * half + 512)
                        dve.wait_ge(o_ps, n + 1)
                        if n >= 2:
                            dve.wait_ge(o_x1, n - 1)
                        dve.tensor_tensor(otmp[half], PS[:, 4 + n % 4, :], gate_row[:, 0, t // 4, w], ALU.mult).then_inc(o_mul, 1)
                dve.wait_ge(n2_sq, NT)
                dve.tensor_scalar(sumsq[:, 0:NT], sumsq[:, 0:NT], 1.0 / D, EPS, ALU.mult, ALU.add).then_inc(n2_mean, 1)
                dve.wait_ge(n2_root, 1)
                dve_order.done(dve.reciprocal(rstd[:, 0:NT], rstd[:, 0:NT]))
                for t in range(NT):
                    dve.tensor_scalar(xn[:, t, :], xt[:, t, :], rstd[:, t:t + 1], None, ALU.mult).then_inc(n2_xn, 1)
                for k in range(KT):
                    dve.wait_ge(n2_tr, k + 1)
                    dve.tensor_scalar(h2T[:, k, 0:SMP], PS[:, k % 2, :], scl2[:, k, 0:1], modT[:, 3, k, 0:1], ALU.mult,
                                      ALU.add).then_inc(n2_s, 1)
                dve.wait_ge(r_sig, NT)
                dve.wait_ge(o_rb, 16)
                for t in range(NT):
                    dve_order.done(dve.tensor_tensor(biased[:, :], score[:, t, :], rb, ALU.add))
                    dve_order.done(dve.max(top8[:, :], biased[:, :]))
                    dve_order.done(dve.match_replace(gate[:, t, :], top8[:, :], biased[:, :], -BIG))
                    dve_order.done(dve.tensor_tensor(mask[:, t, :], gate[:, t, :], biased[:, :], ALU.not_equal))
                    dve_order.done(dve.tensor_tensor(gate[:, t, :], mask[:, t, :], score[:, t, :], ALU.mult))
                    dve_order.done(dve.tensor_reduce(gsum[:, 0:1], gate[:, t, :], AX.X, ALU.add))
                    dve_order.done(dve.reciprocal(gsum[:, 0:1], gsum[:, 0:1]))
                    dve.tensor_scalar(gate[:, t, :], gate[:, t, :], gsum[:, 0:1], 2.5, ALU.mult, ALU.mult).then_inc(r_g, 1)
                    dve.wait_ge(r_g, t + 1)
                dve.wait_ge(m_idx, 16)
                dve_order.done(dve.memset(off[:, 0, :], 0.0))
                for c in cum:
                    dve_order.done(dve.memset(c[:, 0:NE], 0.0))
                dve.wait_ge(m_cnt, 1)
                for t in range(NT):
                    dve.tensor_tensor(off[:, t + 1, :], off[:, t, :], PS[:, 7, t * NE:(t + 1) * NE], ALU.add).then_inc(m_off, 1)
                    dve.wait_ge(m_off, t + 1)
                a, b = cum
                c = a[:, NE:]
                dve_order.done(dve.tensor_scalar(c, off[:, NT, :], 1.0 / P, (P - 1) / P - (P - 1) / (2 * P), ALU.mult, ALU.add))
                dve_order.done(dve.tensor_scalar(c, c, MAGIC, None, ALU.add))
                dve.tensor_scalar(c, c, -MAGIC, None, ALU.add).then_inc(m_off, 1)
                dve.wait_ge(m_off, NT + 1)
                s = 1
                while s < NE:
                    dve_order.done(dve.tensor_tensor(b[:, NE:], a[:, NE:], a[:, NE - s:2 * NE - s], ALU.add))
                    a, b = b, a
                    s *= 2
                incl, excl = a[:, NE:], a[:, NE - 1:2 * NE - 1]
                dve_order.done(dve.tensor_scalar(cmpb, incl, index[:, P:P + 1], None, ALU.is_le))
                dve.tensor_reduce(ecol, cmpb, AX.X, ALU.add).then_inc(m_ecol, 1)
                dve_order.done(dve.tensor_scalar(ngf, incl[:, NE - 1:NE], 1.0 / U, (U - 1) / (2 * U), ALU.mult, ALU.add))
                dve_order.done(dve.tensor_scalar(ngf, ngf, MAGIC, None, ALU.add))
                dve_order.done(dve.tensor_scalar(ngf, ngf, -MAGIC, -float(LEAST), ALU.add, ALU.add))
                dve_order.done(dve.tensor_copy(block_expert[0:1, P:P + 1], ngf[0:1, :]))
                dve.wait_ge(m_erow, 1)
                dve_order.done(dve.tensor_scalar(erow[0:1, :], PS[0:1, 7, 0:P], float(NE - 1), None, ALU.min))
                dve.tensor_copy(block_expert[0:1, 0:P], erow[0:1, :]).then_inc(m_exp, 1)
                dve_order.done(dve.tensor_tensor(D1[:, :, :], off[:, 0:NT, :], PS[:, 6, 0:NT * NE].rearrange("p (t n) -> p t n", t=NT),
                                                 ALU.add))
                dve_order.done(dve.tensor_scalar(cmpb, excl, float(P), 1.0, ALU.mult, ALU.add))
                dve_order.done(dve.tensor_tensor(D1[:, :, :], D1[:, :, :], spread(cmpb, 1, NT), ALU.add))
                dve_order.done(dve.tensor_tensor(D1[:, :, :], D1[:, :, :], mask[:, :, :], ALU.mult))
                for t in range(NT):
                    i = dve.max(d8[:, t, :], D1[:, t, :])
                dve_order.done(i)
                d8_all = d8.rearrange("p t k -> p (t k)")
                dve_order.done(dve.tensor_scalar(hi, d8_all, 1.0 / P, -(P + 1) / (2 * P), ALU.mult, ALU.add))
                dve_order.done(dve.tensor_scalar(dest, d8_all, -1.0, None, ALU.add))
                dve_order.done(dve.tensor_scalar(hi, hi, MAGIC, None, ALU.add))
                dve.tensor_scalar(hi, hi, -MAGIC, None, ALU.add).then_inc(m_hi, 1)
                dve.wait_ge(m_hi, 1)
                dve_order.done(dve.tensor_scalar(lo, hi, -float(P), None, ALU.mult))
                dve_order.done(dve.tensor_tensor(lo, lo, dest, ALU.add))
                for t in range(NT):
                    if t >= 2:
                        dve.wait_ge(m_tab, t - 1)
                    dve.tensor_tensor(at_block[t % 2][:, :, :], spread(index[:, 0:BLOCKS + 1], 1, TOPK),
                                      spread(hi[:, t * TOPK:(t + 1) * TOPK], 2, BLOCKS + 1), ALU.is_equal).then_inc(m_beq, 1)
                    dve.tensor_tensor(at_slot[t % 2][:, :, :], spread(index[:, 0:P], 1, TOPK),
                                      spread(lo[:, t * TOPK:(t + 1) * TOPK], 2, P), ALU.is_equal).then_inc(m_at, 1)
                dve.tensor_copy(dest_u, dest).then_inc(m_dest, 1)
                dve.wait_ge(m_tab, NT)
                dve.tensor_copy(slot_token, PS[:, 6, 0:BLOCKS + 1]).then_inc(m_tok, 1)

                def hidden(b, j):
                    dve.wait_ge(e_silu, b + 1)
                    dve.tensor_tensor(hid[j % 2], gact, PS[:, 3, 0:P], ALU.mult).then_inc(e_hid, 1)

                def take_y(b, j, stored=None):
                    dve.wait_ge(e_ps, b + 1)
                    if stored is not None:
                        dve.wait_ge(e_out[j % 2], stored)
                    dve.tensor_copy(yb[j % 2].rearrange("p (h n) -> p h n", h=2),
                                    PS[:, 4 + 2 * (j % 2):6 + 2 * (j % 2), :]).then_inc(e_y, 1)

                groups = group_count(dve)
                for j in range(U):
                    if j:
                        take_y(j - 1, j - 1, None if j <= 2 else 16 * ((j - 1) // 2))
                    hidden(j, j)
                with dve.Fori(1, groups) as i:
                    for j in range(U):
                        take_y(U * i + (j - 1), (j - 1) % U, 16 * (U // 2) * i + 16 * ((j - 1) // 2))
                        hidden(U * i + j, j)
                take_y(U * groups - 1, U - 1, 16 * (U // 2) * groups - 16)
                dve.wait_ge(e_out[0], 32 * groups)
                dve.wait_ge(e_out[1], 32 * groups)
                dve.tensor_scalar(d8_all, d8_all, 1.0, None, ALU.mult).then_inc(y_all, 1)
                dve.wait_ge(y_all, 1)
                for t in range(NT):
                    dve_order.done(dve.tensor_tensor(pick[:, :, :], spread(D1[:, t, :], 1, TOPK), spread(d8[:, t, :], 2, NE), ALU.is_equal))
                    dve_order.done(dve.tensor_tensor(pick[:, :, :], pick[:, :, :], spread(gate[:, t, :], 1, TOPK), ALU.mult))
                    dve_order.done(dve.tensor_reduce(g8[:, t, :], pick[:, :, :], AX.X, ALU.add))
                dve.wait_ge(s_acc, 2 * NT)
                dve.wait_ge(o_fg, 16)
                for t in range(NT):
                    for k in range(TOPK):
                        n = TOPK * t + k
                        dve.wait_ge(g_in[n % GB], 16 * (n // GB + 1))
                        dve.scalar_tensor_tensor(out=acc[:, t, :], in0=back[n % GB], scalar=g8[:, t, k:k + 1], in1=acc[:, t, :],
                                                 op0=ALU.mult, op1=ALU.add).then_inc(g_used, 1)
                        dve.wait_ge(g_used, n + 1)
                    dve_order.done(dve.tensor_tensor(fmul, acc[:, t, :], gate_row[:, 1, t // 4, :], ALU.mult))
                    dve.tensor_tensor(xt[:, t, :], xt[:, t, :], fmul, ALU.add).then_inc(f_x2, 1)
                    dve.wait_ge(f_x2, t + 1)
                    dve.wait_ge(f_sq2, t + 1)
                    dve.tensor_scalar(sumsq[:, t:t + 1], sumsq[:, t:t + 1], 1.0 / D, EPS, ALU.mult, ALU.add).then_inc(f_mn, 1)
                    dve.wait_ge(f_rt, t + 1)
                    dve_order.done(dve.reciprocal(rstd[:, t:t + 1], rstd[:, t:t + 1]))
                    dve.scalar_tensor_tensor(out=acc[:, t, :], in0=xt[:, t, :], scalar=rstd[:, t:t + 1], in1=fin_row,
                                             op0=ALU.mult, op1=ALU.mult).then_inc(f_y, 1)

            @block.scalar
            def _(act):
                act_order = Steps(act, "act_order2")
                for i in range(2):
                    act.wait_ge(f_z, i + 1)
                    act.activation(hid1 if i == 0 else hid2, fz, ACT.Sin).then_inc(f_s, 1)
                act.wait_ge(f_ne, 1)
                act.activation(rn, rn, ACT.Sqrt).then_inc(f_nr, 1)
                for t in range(NT):
                    act.wait_ge(c_tr, t + 1)
                    act.activation(z1_tok[:, t, :], PS[:, t % 2, 0:256], ACT.Copy).then_inc(c_trt, 1)

                for t in range(NT):
                    act.wait_ge(o_x1, 2 * t + 2)
                    i = act.activation(part(r1_at + 8192, D), xt[:, t, :], ACT.Square, accum_out=sumsq[:, t:t + 1])
                    i.then_inc(n2_sq, 1)
                    act.wait_ge(n2_sq, t + 1)
                act.wait_ge(n2_mean, 1)
                act.activation(rstd[:, 0:NT], sumsq[:, 0:NT], ACT.Sqrt).then_inc(n2_root, 1)
                act.wait_ge(o_scl, 1)
                for k in range(KT):
                    act.wait_ge(n2_tr, k + 1)
                    act.activation(h2T[:, k, SMP:TOK], PS[:, 2 + k % 2, 0:P], ACT.Identity, scale=scl2[:, k, 1:2],
                                   bias=modT[:, 3, k, 1:2]).then_inc(n2_p, 1)
                for t in range(NT):
                    act.wait_ge(r_ps, t + 1)
                    act.activation(score[:, t, :], PS[:, 4 + t % 4, 0:NE], ACT.Sigmoid).then_inc(r_sig, 1)
                for n in range(2 * NT):
                    t, half = n // 2, n % 2
                    act.wait_ge(b_ps, n + 1)
                    dst = h2[:, t, :].rearrange("p (q k) -> p k q", k=KT)[:, 4 * half:4 * half + 4, :]
                    act.activation(dst, PS[:, n % 4, :].rearrange("p (k q) -> p k q", k=4), ACT.Copy).then_inc(b_cp, 1)
                act.wait_ge(s_gu, 1)
                act.activation(sact.rearrange("p (b n) -> p b n", b=2), PS[:, 0:2, 0:320], ACT.Silu).then_inc(s_act, 1)
                act.wait_ge(s_gu, 2)
                act.activation(sup.rearrange("p (b n) -> p b n", b=2), PS[:, 2:4, 0:320], ACT.Copy).then_inc(s_up, 1)
                for n in range(2 * NT):
                    t, half = n // 2, n % 2
                    act.wait_ge(s_ps, n + 1)
                    act.activation(acc[:, t, 512 * half:512 * half + 512], PS[:, 4 + half, :], ACT.Copy).then_inc(s_acc, 1)

                def copy_xT(b, j):
                    act.wait_ge(e_tr, b + 1)
                    act.activation(xT[j % 2].rearrange("p (h k) n -> p h (k n)", h=2), PS[:, 0:2, :], ACT.Copy).then_inc(e_xT, 1)

                def silu(b, first=False):
                    act.wait_ge(e_gu, b + 1)
                    if not first:
                        act.wait_ge(e_hid, b)
                    act.activation(gact, PS[:, 2, 0:P], ACT.Silu).then_inc(e_silu, 1)

                groups = group_count(act)
                act.wait_ge(m_tok, 1)
                act.wait_ge(s_hid, 1)
                for j in range(U):
                    copy_xT(j, j)
                    silu(j, j == 0)
                with act.Fori(1, groups) as i:
                    for j in range(U):
                        copy_xT(U * i + j, j)
                        silu(U * i + j)
                for t in range(NT):
                    act.wait_ge(f_x2, t + 1)
                    act.activation(fjunk, xt[:, t, :], ACT.Square, accum_out=sumsq[:, t:t + 1]).then_inc(f_sq2, 1)
                    act.wait_ge(f_sq2, t + 1)
                    act.wait_ge(f_mn, t + 1)
                    act.activation(rstd[:, t:t + 1], sumsq[:, t:t + 1], ACT.Sqrt).then_inc(f_rt, 1)

            @block.gpsimd
            def _(pool):
                pool_order = Steps(pool, "pool_order2")
                for t in range(NT):
                    pool.wait_ge(f_hf, t + 1)
                    if t >= 2:
                        pool.wait_ge(f_nrm, t - 1)
                    h = hf[:, t]
                    pool.tensor_tensor(hsq[t % 2].rearrange("p o s n -> p (o s n)"), h.rearrange("p o s n -> p (o s n)"),
                                       h.rearrange("p o s n -> p (o s n)"), ALU.mult).then_inc(f_sq, 1)
                    pool.tensor_tensor(hsum[:, t], h[:, :, 0, :], h[:, :, 1, :], ALU.add)
                    pool.tensor_tensor(hdif[:, t], h[:, :, 0, :], h[:, :, 1, :], ALU.subtract).then_inc(f_sd, 1)
                for o in range(2):
                    for i, (s, f) in enumerate(FT):
                        n = len(FT) * o + i
                        pool.wait_ge(c_pr, n + 1)
                        if o == 1 and i == 0:
                            pool.wait_ge(c_y, 2)
                        q = pr[n % 2]
                        re, im = (8, 9) if s else (f, 4 + f)
                        pool.tensor_tensor(spec[:, re, :], q[:, 0, :], q[:, 1, :], ALU.subtract)
                        pool.tensor_tensor(spec[:, im, :], q[:, 2, :], q[:, 3, :], ALU.add).then_inc(c_Y, 1)
                pool.wait_ge(o_x, 32)
                for n in range(2 * NT):
                    t, half = n // 2, n % 2
                    w = slice(512 * half, 512 * half + 512)
                    pool.wait_ge(o_mul, n + 1)
                    pool.tensor_tensor(xt[:, t, w], xt[:, t, w], otmp[half], ALU.add).then_inc(o_x1, 1)
                pool.wait_ge(s_act, 1)
                pool.wait_ge(s_up, 1)
                pool.tensor_tensor(shid, sact, sup, ALU.mult).then_inc(s_hid, 1)
                pool.wait_ge(m_idx, 16)
                for t in range(NT):
                    pool.wait_ge(m_beq, t + 1)
                    pool.tensor_scalar(at_block[t % 2][:, :, :], at_block[t % 2][:, :, :], index[:, P + t:P + t + 1], None,
                                       ALU.mult).then_inc(m_bl, 1)

                pool.wait_ge(m_tok, 1)
                pool.wait_ge(h2_out, 16 * NT)
                def fetch_x(b, j, first=False):
                    if not first:
                        pool.wait_ge(e_tr, b - (U - 2))
                    pool.wait_ge(x_col, b + 1)
                    pool.tensor_copy(token_col[(j + 1) % U], slot_token[:, bass.ds(b + 1, 1)]).then_inc(x_col, 1)
                    pool.indirect_dma_start(xg[j], None, T["h2_rows"], bass.IndirectOffsetOnAxis(token_col[j], 0)).then_inc(e_x[j], 16)

                pool.tensor_copy(token_col[0], slot_token[:, 0:1]).then_inc(x_col, 1)
                for j in range(U):
                    fetch_x(j, j, j < U - 1)
                groups = group_count(pool)
                with pool.Fori(1, groups) as i:
                    for j in range(U):
                        fetch_x(U * i + j, j)
                pool.wait_ge(m_dest, 1)
                pool.wait_ge(y_all, 1)
                for n in range(PAIRS):
                    if n >= GB:
                        pool.wait_ge(g_used, n - GB + 1)
                    pool.indirect_dma_start(back[n % GB], None, T["y_rows"],
                                            bass.IndirectOffsetOnAxis(dest_u[:, n:n + 1], 0)).then_inc(g_in[n % GB], 16)



_IN = ['x_prompt', 'x_sample', 'c', 'state_gdn', 'state_hgrn', 'state_mlstm_c', 'state_mlstm_n',
       'state_mlstm_m', 'c_ctx', 'norm1_g', 'norm2_g', 'w_mod', 'b_mod', 'w_in', 'gdn_conv', 'gdn_a_log',
       'gdn_dt_bias', 'gdn_norm_g', 'hgrn_lb_logits', 'hgrn_norm_g', 'mlstm_f_bias', 'mlstm_norm_g',
       'hyena_conv', 'filt_w1', 'filt_b1', 'filt_w2', 'filt_b2', 'filt_w3', 'filt_freq', 'hyena_d',
       'w_out', 'router_w', 'router_bias', 'exp_w_gate', 'exp_w_up', 'exp_w_down', 'sh_w_gate',
       'sh_w_up', 'sh_w_down', 'final_g']
_OUT = [("y_prompt", (1, P, D)), ("y_sample", (1, SMP, D)), ("new_gdn", (1, 1, 2, 4, HD, HD)),
        ("new_hgrn", (1, 1, 2, 4, HD, HD)), ("new_c", (1, 1, 2, 4, HD, HD)), ("new_n", (1, 1, 2, 4, HD)),
        ("new_m", (1, 1, 2, 4))]


def kernel(**inputs):
    import concourse.bacc as bacc
    from concourse.bass_utils import run_bass_kernel_spmd

    nc = bacc.Bacc("TRN2", target_bir_lowering=False, num_devices=1)
    arrays, T = {}, {}
    for name in _IN:
        a = np.ascontiguousarray(inputs[name])
        arrays["in_" + name] = a
        T[name] = nc.dram_tensor("in_" + name, a.shape, mybir.dt.float32, kind="ExternalInput").ap()
    for name, a in zip(("masks", "dfts", "feats", "decay"), shape_constants()):
        arrays["const_" + name] = a
        T[name] = nc.dram_tensor("const_" + name, a.shape, mybir.dt.float32, kind="ExternalInput").ap()
    for name, shape in _OUT:
        T[name] = nc.dram_tensor("out_" + name, shape, mybir.dt.float32, kind="ExternalOutput").ap()
    arrays["const_index"] = index = token_numbers()
    T["index"] = nc.dram_tensor("const_index", index.shape, mybir.dt.float32, kind="ExternalInput").ap()
    T["h2_rows"] = nc.dram_tensor("h2_rows", (TOK, D), mybir.dt.float32).ap()
    T["y_rows"] = nc.dram_tensor("y_rows", ((TOK * TOPK // P + NE) * P, D), mybir.dt.float32).ap()
    trunk_program(nc, T)
    r = run_bass_kernel_spmd(nc, [arrays], core_ids=[0])
    return tuple(r.results[0]["out_" + name] for name, _ in _OUT)
```

```python
import concourse.bass as bass
from concourse import mybir
from contextlib import ExitStack
import numpy as np

P = 128
D = 1024
KT = D // P
NT = 5
TOK = NT * P
SMP = 512
GW = 64
NE = 64
TOPK = 8
HD = 64
MW = 256
LV = 7
EPS = 1e-6
BIG = 1e30
TINY = 2.0 ** -63
IN_OFF = dict(qa=0, ka=256, va=512, ga=768, ab=1024, qb=1040, ib=1296, gb=1552, fb=1808,
              qc=2320, kc=2576, vc=2832, oc=3088, fi=3344, ud=3360)
CONST = ["ident", "ones", "blk", "strict", "run", "big", "after"]
CONST_W = dict(ident=P, ones=P, blk=P, strict=2 * LV * P, run=2 * (LV + 1) * P, big=2 * P, after=2 * P)


def shape_constants():
    a = np.arange(P)
    row, col = a[:, None], a[None, :]
    strict, run = np.zeros((P, 2, LV, P)), np.zeros((P, 2, LV + 1, P))
    for l in range(LV):
        s = 64 >> l
        same = row // (2 * s) == col // (2 * s)
        m = same & (row % (2 * s) < s) & (col % (2 * s) >= s)
        strict[:, 0, l], strict[:, 1, l] = m, m.T
        mid = (col // (2 * s)) * 2 * s + s
        first = col < mid
        run[:, 0, l] = np.where(first, (row > col) & (row < mid), (row >= mid) & (row <= col))
        run[:, 1, l] = np.where(first, (row >= col) & (row < mid), (row >= mid) & (row < col))
    run[:, 0, LV], run[:, 1, LV] = row <= col, row >= col
    big = np.stack([np.where(row <= col, 0, BIG), np.where(row >= col, 0, BIG)], 1)
    after = np.stack([row > col, row < col], 1)
    parts = dict(ident=np.eye(P), ones=np.ones((P, P)), blk=row // HD == col // HD, strict=strict,
                 run=run, big=big, after=after)
    masks = np.concatenate([np.asarray(parts[n], np.float32).reshape(P, -1) for n in CONST], 1)

    def dft(length):
        n = 2 * length
        t, f = np.arange(length)[:, None], np.arange(length)[None, :]
        th = 2 * np.pi * ((t * f) % n) / n
        re, im = np.cos(th), -np.sin(th)
        im[:, 0] = (-1.0) ** np.arange(length)
        w = np.where(np.arange(length) == 0, 1.0, 2.0)[None, :] / n
        wi = w.copy()
        fwd = np.concatenate([re, im], 1)
        inv = np.concatenate([(re * w).T, (im * wi).T], 0)
        return fwd, inv
    f5, i5 = dft(SMP)
    f1, i1 = dft(P)
    fwd5 = f5.reshape(4, P, 2 * SMP).transpose(1, 0, 2).reshape(P, -1)
    inv5 = i5.reshape(8, P, SMP).transpose(1, 0, 2).reshape(P, -1)
    inv1 = i1.reshape(2, P, P).transpose(1, 0, 2).reshape(P, -1)
    dfts = np.concatenate([fwd5, inv5, f1, inv1], 1).astype(np.float32)

    def positions(length):
        t = np.arange(length, dtype=np.float64)
        tn = np.linspace(0.0, 1.0, length).astype(np.float32).astype(np.float64)
        bands = np.linspace(1e-4, 15, 16).astype(np.float32).astype(np.float64)
        ang = ((2.0 * np.pi / length) * t[:, None]).astype(np.float32) * bands[None, :].astype(np.float32)
        ang = ang.astype(np.float64)
        feats = np.concatenate([tn[:, None], np.cos(ang), -np.sin(ang)], 1)
        deltas = np.abs(np.linspace(np.log(1e-2) / 1.5, np.log(1e-2) / 0.3, MW))
        dec = np.exp(-tn[:, None] * deltas[None, :])
        dec2 = dec.copy()
        dec2[0] = 0
        return feats, np.stack([dec, dec2], 1)
    (fa, da), (fb, db) = positions(SMP), positions(P)
    feats = np.ascontiguousarray(np.concatenate([fa, fb], 0).T).astype(np.float32)
    decay = np.concatenate([da, db], 0).reshape(NT, P, 2 * MW).transpose(1, 0, 2)
    decay = np.ascontiguousarray(decay).reshape(P, -1).astype(np.float32)
    return masks, dfts, feats, decay


def token_numbers():
    a = np.arange(P)
    return np.concatenate([np.tile(a, (P, 1)), a[:, None] + P * np.arange(NT)[None, :]], 1).astype(np.float32)


def trunk_program(nc, T):
    F = mybir.dt.float32
    U32 = mybir.dt.uint32
    ALU = mybir.AluOpType
    ACT = mybir.ActivationFunctionType
    AX = mybir.AxisListType

    def spread(ap, axis, n):
        shape = list(ap.shape)
        shape.insert(axis, n)
        return ap.unsqueeze(axis).to_broadcast(shape)

    ctx = ExitStack()
    with ctx:
        def sb(name, words, parts=P):
            return ctx.enter_context(nc.sbuf_tensor(name, [parts, words], F))

        stage_sems = []

        def sem(name):
            stage_sems.append(nc.alloc_semaphore(name=name))
            return stage_sems[-1]

        class Steps:

            def __init__(self, eng, name):
                self.eng, self.n = eng, 0
                self.sem = sem(name)

            def done(self, ins):
                self.n += 1
                ins.then_inc(self.sem, 1)
                self.eng.wait_ge(self.sem, self.n)

        PS = ctx.enter_context(nc.psum_tensor("PS", [P, 8, 512], F))

        cst = sb("cst", sum(CONST_W.values()))
        at, off = {}, 0
        for n in CONST:
            at[n] = cst[:, off:off + CONST_W[n]]
            off += CONST_W[n]
        ident, ones, blk = at["ident"], at["ones"], at["blk"]
        strict = at["strict"].rearrange("p (d l n) -> p d l n", d=2, l=LV)
        run = at["run"].rearrange("p (d l n) -> p d l n", d=2, l=LV + 1)
        big = at["big"].rearrange("p (d n) -> p d n", d=2)
        after = at["after"].rearrange("p (d n) -> p d n", d=2)
        ARENA = 53200 - sum(CONST_W.values())
        arena = sb("arena", ARENA)
        top = [0]

        def region(words):
            a = top[0]
            top[0] += words
            assert top[0] <= ARENA, (top[0], ARENA)
            return a

        def part(start, words):
            return arena[:, start:start + words]

        x_at, y_at, r1_at, r2_at, r3_at = region(5120), region(5120), region(15360), region(19300), region(1500)
        par_at = region(ARENA - top[0])
        par_end = [par_at]

        def small(words):
            a = par_end[0]
            par_end[0] += words
            assert par_end[0] <= ARENA, par_end[0] - ARENA
            return part(a, words)

        xt = part(x_at, 5120).rearrange("p (t d) -> p t d", t=NT)
        yT = part(y_at, 5120).rearrange("p (k n) -> p k n", k=KT)
        hT = part(r1_at, 5120).rearrange("p (k n) -> p k n", k=KT)
        hTp = part(r1_at + 5120, 4096).rearrange("p (k n) -> p k n", k=KT)
        w_slot = [part(r1_at + 9216 + 2048 * i, 2048).rearrange("p (k n) -> p k n", k=KT) for i in range(3)]
        mod_slot = [part(r2_at + 8192 * i, 8192).rearrange("p (k n) -> p k n", k=KT) for i in range(2)]

        cond = small(16).rearrange("p (c k) -> p c k", c=2)
        scond = small(16).rearrange("p (k c) -> p k c", c=2)
        g1p, g2p = small(8), small(8)
        bmod = small(48).rearrange("p (j k) -> p j k", j=6)
        modT = small(96).rearrange("p (j k c) -> p j k c", j=6, k=KT)
        scl = small(16).rearrange("p (k c) -> p k c", c=2)
        sumsq, rstd = small(8), small(8)

        consts_in, x_in, x_back = sem("consts_in"), sem("x_in"), sem("x_back")
        cond_in, params_in, cond_silu = sem("cond_in"), sem("params_in"), sem("cond_silu")
        mod_in = [sem("mod_in0"), sem("mod_in1")]
        mod_ready, mod_taken, scl_ready = sem("mod_ready"), sem("mod_taken"), sem("scl_ready")
        sq1_done, root1, xn_done, xT_ready = sem("sq1_done"), sem("root1"), sem("xn_done"), sem("xT_ready")
        mod2_in, mod2_ready, mod2_mul = [sem("mod2_in0"), sem("mod2_in1")], sem("mod2_ready"), sem("mod2_mul")
        mean1, hT_smp, hT_pro, hTp_done = sem("mean1"), sem("hT_smp"), sem("hT_pro"), sem("hTp_done")
        junk = part(y_at, D)
        PRE_W = SMP + P + 6
        CONV_W = PRE_W - 4
        r2 = [r2_at]

        def keep(words):
            a = r2[0]
            r2[0] += words
            assert r2[0] <= r2_at + 19300
            return part(a, words)

        pre = keep(6 * PRE_W).rearrange("p (k n) -> p k n", k=6)
        qkT = keep(4 * TOK).rearrange("p (k n) -> p k n", k=4)
        vT = keep(2 * TOK).rearrange("p (k n) -> p k n", k=2)
        hqT = keep(2 * TOK).rearrange("p (k n) -> p k n", k=2)
        fgate = keep(NT * 512).rearrange("p (t n) -> p t n", t=NT)
        hv = keep(NT * MW).rearrange("p (t n) -> p t n", t=NT)
        mqkT = keep(4 * TOK).rearrange("p (k n) -> p k n", k=4)
        mv = keep(NT * 4 * 65).rearrange("p (t h n) -> p t h n", t=NT, h=4)
        hy = keep(4 * TOK).rearrange("p (k n) -> p k n", k=4)
        mod_chunk = [part(r2_at + 16700 + D * i, D) for i in range(2)]
        CHUNKS = 4 * KT
        mod_acc = [part(r2_at + 12836 + D * c, D) for c in range(2)]
        SUM_AFTER = (7, 13, 19, 25)
        w_small = small(KT * 32).rearrange("p (k n) -> p k n", k=KT)
        smt = small(NT * 32).rearrange("p (t g h) -> p t g h", t=NT, g=8)
        GROUPS = [("qa", 0, "f"), ("ka", 0, "f"), ("va", 0, "f"), ("ga", 0, "f"), ("qb", 0, "f"), ("gb", 0, "f"),
                  ("ib", 0, "t"), ("fb", 0, "t"), ("fb", MW, "t"), ("qc", 0, "f"), ("kc", 0, "f"), ("oc", 0, "f"),
                  ("vc", 0, "t"), ("small", 0, "s"), ("ud", 0, "f"), ("ud", MW, "f"), ("ud", 2 * MW, "f")]
        OUTPUTS = [(g, i) for g, (_, _, kind) in enumerate(GROUPS) for i in range(2 if kind == "f" else NT)]
        LAST = len(OUTPUTS) - 1
        slotted = [g for g, (_, _, kind) in enumerate(GROUPS) if kind != "s"]

        def outputs_before(g):
            return sum(1 for a, _ in OUTPUTS if a < g)

        w_in_sem = [sem(f"w_in{i}") for i in range(3)]
        small_in, proj_ready, proj_taken, pads_zero = sem("small_in"), sem("proj_ready"), sem("proj_taken"), sem("pads_zero")
        gdn_conv_read = sem("gdn_conv_read")
        ones_col, dve_beg = sem("ones_col"), sem("dve_beg")
        cbuf = part(x_at, 6 * CONV_W).rearrange("p (k n) -> p k n", k=6)
        sq = part(r1_at + 5120, 4 * TOK)
        rq = sq
        o_tok = part(r1_at, 3 * NT * MW).rearrange("p (m t n) -> p m t n", m=3, t=NT)
        kv_tok = part(r1_at + 3840, NT * 512).rearrange("p (t n) -> p t n", t=NT)
        mh_tok = part(r1_at + 6400, NT * 512).rearrange("p (t n) -> p t n", t=NT)
        rows_in, rows_T, rows_zero, taps_ready = sem("rows_in"), sem("rows_T"), sem("rows_zero"), sem("taps_ready")
        rows = part(r2_at + 16700, 768)
        tapsT = small(60).rearrange("p (k r) -> p k r", k=6)
        prm_raw, prm = small(24), small(24)
        lb_row = part(x_at, 512)
        lbn = small(8)
        l2_rec, silu_done, sq_done, l2_sum, l2_eps, l2_root, k_unit = (sem(n) for n in
            ("l2_rec", "silu_done", "sq_done", "l2_sum", "l2_eps", "l2_root", "k_unit"))
        hy_conv, hy_out, tr_ready, tr_taken, prm_in = (sem(n) for n in
            ("hy_conv", "hy_out", "tr_ready", "tr_taken", "prm_in"))
        softin, softabs, softexp, softlog, scal_ready, scal_ps = (sem(n) for n in
            ("softin", "softabs", "softexp", "softlog", "scal_ready", "scal_ps"))
        spi = small(NT * 16).rearrange("p (t g h) -> p t g h", t=NT, g=4)
        spa = small(NT * 16).rearrange("p (t g h) -> p t g h", t=NT, g=4)
        beta = small(NT * 8).rearrange("p (t d h) -> p t d h", t=NT, d=2)
        gl = small(NT * 16).rearrange("p (d t w h) -> p d t w h", d=2, t=NT, w=2)
        cs = small(NT * 16).rearrange("p (d t w h) -> p d t w h", d=2, t=NT, w=2)
        tot = small(NT * 16).rearrange("p (d t w h) -> p d t w h", d=2, t=NT, w=2)
        egc = small(NT * 8).rearrange("p (d t h) -> p d t h", d=2, t=NT)
        beg = small(NT * 8).rearrange("p (d t h) -> p d t h", d=2, t=NT)
        cc = small(NT * 8).rearrange("p (d t h) -> p d t h", d=2, t=NT)
        nalog = small(8)
        scal_done, egc_done, alog_exp, beta_done, fo_done = (sem(n) for n in
            ("scal_done", "egc_done", "alog_exp", "beta_done", "fo_done"))
        lb_in, lb_e, lb_work = sem("lb_in"), sem("lb_e"), sem("lb_work")
        lbt = [part(r3_at, 512), part(r3_at + 512, 512)]
        UNITS = [(0, 4, 1), (1, 4, 1)] + [(d, n if d == 0 else 3 - n, 0) for n in range(4) for d in range(2)]
        seen = set()
        FIRST = []
        for _, t, _ in UNITS:
            FIRST.append(t not in seen)
            seen.add(t)

        def last_token(d):
            return P - 1 if d == 0 else 0

        pool_area = {"u1": (r1_at + 8960, 6400), "u2": (x_at, 5120), "u3": (r3_at, 1500), "s": (r2_at, 3876)}
        used = {k: 0 for k in pool_area}

        def scratch(where, words):
            a, n = pool_area[where]
            used[where] += words
            assert used[where] <= n, (where, used[where])
            return part(a + used[where] - words, words)

        def heads(ap):
            return ap.rearrange("p (h n) -> p h n", h=4)

        gS = scratch("s", 4 * 2 * P).rearrange("p (s d pt n) -> p s d pt n", s=2, d=2, pt=2)
        hS = scratch("s", 4 * 2 * P).rearrange("p (s d pt n) -> p s d pt n", s=2, d=2, pt=2)
        mS = scratch("s", 4 * 260).rearrange("p (s d pt n) -> p s d pt n", s=2, d=2, pt=2)
        states_zero, states_in = sem("states_zero"), sem("states_in")

        gDG, gX, gDT, gMT = (heads(scratch("u1", 512)) for _ in range(4))
        gEGB = [heads(scratch("u1" if i == 0 else "u2", 512)) for i in range(2)]
        gMS = [heads(scratch("u1", 512)) for _ in range(2)]
        gT, gTT, gP, gBK = (heads(scratch("u1", 512)) for _ in range(4))
        gAT = [heads(scratch("u1" if i == 0 else "u2", 512)) for i in range(2)]
        gvn, gU, gwt, gwT, gkd = (scratch("u1" if i == 0 else "u2", 256).rearrange("p (pt n) -> p pt n", pt=2)
                                  for i in range(5))
        gqd = [scratch("u2", 256).rearrange("p (pt n) -> p pt n", pt=2) for _ in range(2)]
        gel = small(4)
        (g_tn, g_lvT, g_diag, g_row, g_egb, g_x, g_dt, g_kq, g_mt, g_at, g_ms, g_lv1, g_p, g_lv2, g_t, g_bk, g_uw, g_wt, g_wTr,
         g_wT, g_ws, g_vn, g_qd, g_eld, g_el, g_kd, g_o, g_st, g_otaken, g_staken) = (sem("g_" + n) for n in (
         "tn lvT diag row egb x dt kq mt at ms lv1 p lv2 t bk uw wt wTr wT ws vn qd eld el kd o st otaken staken").split())

        def kq_banks(b):
            return PS[:, b:b + 2, 0:256]

        def by_par(ap):
            return ap.rearrange("p (par pt) n -> p par (pt n)", par=2)
        mDC, mWD = (heads(scratch("u3", 512)) for _ in range(2))
        mWT, mX = heads(scratch("s", 512)), heads(scratch("u2", 512))
        mqd, mkw = (scratch("u2", 256).rearrange("p (pt n) -> p pt n", pt=2) for _ in range(2))
        mtmp = scratch("u3", 256)
        mst = small(16).rearrange("p (s d h) -> p s d h", s=2, d=2)
        m_raw = small(8)
        mmx, mmu, mden = small(4), small(4), small(4)
        mex = small(12).rearrange("p (k h) -> p k h", k=3)
        (m_in, m_zero, m_dc, m_cb, m_qk, m_dmu, m_mb, m_x, m_eqx, m_sm, m_wd, m_eq, m_ex, m_wt, m_qd, m_kw, m_o, m_st,
         m_otaken, m_staken) = (sem("m_" + n) for n in
         "in zero dc cb qk dmu mb x eqx sm wd eq ex wt qd kw o st otaken staken".split())

        used["u1"] = used["u2"] = 0
        hE = [scratch(w, 2 * (LV + 1) * P).rearrange("p (pt l n) -> p pt l n", pt=2, l=LV + 1) for w in ("u1", "u2")]
        hQE = [scratch(w, 2 * (LV + 1) * P).rearrange("p (pt l n) -> p pt l n", pt=2, l=LV + 1) for w in ("u1", "u2")]
        hKE = scratch("u1", 2 * LV * P).rearrange("p (pt l n) -> p pt l n", pt=2, l=LV)
        hAT = heads(scratch("u1", 512))
        hlt, hkt, hkT, hkd = (scratch("u2", 256) for _ in range(4))
        (h_lt, h_kt, h_x, h_xa, h_kT, h_e, h_ek, h_kTs, h_qe, h_ke, h_kd, h_lvl, h_merge, h_o, h_st, h_otaken,
         h_staken) = (sem("h_" + n) for n in "lt kt x xa kT e ek kTs qe ke kd lvl merge o st otaken staken".split())
        norm_row = small(3 * HD).rearrange("p (m n) -> p m n", m=3)
        ho_ss = small(3 * 20)
        (n_in, n_sq, n_ss, n_root, n_on, n_tr, n_taken) = (sem("n_" + x) for x in "in sq ss root on tr taken".split())
        MIX = [0, 2, 1]
        osq = part(r2_at + 3876, NT * MW)
        osq4 = osq.rearrange("p (h n) -> p h n", n=HD)
        tail_out, n_rec, n_last = sem("tail_out"), sem("n_rec"), sem("n_last")

        def head_out(i):
            return o_tok[:, MIX[i]].rearrange("p t n -> p (t n)")

        def head_ss(i):
            return ho_ss[:, 20 * MIX[i]:20 * MIX[i] + 20]
        dft_at = r2_at + 3900
        fwd5 = part(dft_at, 4096).rearrange("p (t n) -> p t n", t=4)
        inv5 = part(dft_at + 4096, 4096).rearrange("p (t n) -> p t n", t=8)
        fwd1 = part(dft_at + 8192, 256).rearrange("p (t n) -> p t n", t=1)
        inv1 = part(dft_at + 8448, 256).rearrange("p (t n) -> p t n", t=2)
        dec_at = dft_at + 8704
        decay = part(dec_at, NT * 512).rearrange("p (t n) -> p t n", t=NT)
        feats = part(dec_at + 2560, TOK)[0:33]
        fw1, fw2, fw3 = part(r3_at, HD)[0:33], part(r3_at + 64, HD)[0:HD], part(r3_at + 128, 1024)[0:HD]
        fcol = small(3)[0:HD]
        filt_in = sem("filt_in")
        s_out = sem("s_out")

        with nc.Block() as block:

            @block.sync
            def _(sp):
                sp.dma_start(cond[:, 0, :], T["c"].rearrange("a (p k) -> p (a k)", k=KT)).then_inc(cond_in, 16)
                sp.dma_start(cond[:, 1, :], T["c_ctx"].rearrange("(p k) -> p k", k=KT)).then_inc(cond_in, 16)
                sp.dma_start(xt[:, 0:4, :], T["x_sample"].rearrange("a (t p) d -> p (a t) d", p=P)).then_inc(x_in, 16)
                sp.dma_start(xt[:, 4, :], T["x_prompt"].rearrange("a p d -> p (a d)")).then_inc(x_in, 16)
                wm = T["w_mod"].rearrange("a (p k) (j n) -> p j (a k) n", k=KT, j=6)
                for j in range(2):
                    sp.dma_start(mod_slot[j], wm[:, j]).then_inc(mod_in[j], 16)
                    if j == 0:
                        sp.dma_start(g1p, T["norm1_g"].rearrange("a (p k) -> p (a k)", k=KT)).then_inc(params_in, 16)
                        sp.dma_start(g2p, T["norm2_g"].rearrange("a (p k) -> p (a k)", k=KT)).then_inc(params_in, 16)
                        sp.dma_start(bmod, T["b_mod"].rearrange("a (j p k) -> p (a j) k", j=6, k=KT)).then_inc(params_in, 16)
                        sp.dma_start(cst[:, :], T["masks"]).then_inc(consts_in, 16)
                sp.wait_ge(rows_zero, 1)
                sp.dma_start(rows[0:5, :], T["gdn_conv"].rearrange("a t n -> (a t) n")).then_inc(rows_in, 16)
                sp.dma_start(rows[5:8, :], T["hyena_conv"].rearrange("a t n -> (a t) n")).then_inc(rows_in, 16)
                sp.dma_start(rows[8:10, 0:MW], T["hyena_d"].rearrange("a t n -> (a t) n")).then_inc(rows_in, 16)
                for i, n in enumerate(("gdn_dt_bias", "gdn_a_log", "mlstm_f_bias")):
                    sp.dma_start(prm_raw[:, 8 * i:8 * i + 8],
                                 T[n].rearrange("a d h -> a (d h)").to_broadcast([P, 8])).then_inc(prm_in, 16)
                sp.dma_start(lbt[0], T["hgrn_lb_logits"].rearrange("a d n -> a (d n)").to_broadcast([P, 512])).then_inc(lb_in, 16)

                wi = T["w_in"].rearrange("a (p k) n -> p (a k) n", k=KT)
                sp.dma_start(w_small[:, :, 0:16], wi[:, :, IN_OFF["ab"]:IN_OFF["ab"] + 16]).then_inc(small_in, 16)
                sp.dma_start(w_small[:, :, 16:32], wi[:, :, IN_OFF["fi"]:IN_OFF["fi"] + 16]).then_inc(small_in, 16)
                sp.wait_ge(rows_T, 1)

                def load_chunk(q):
                    if q >= 2:
                        sp.wait_ge(mod2_mul, 2 * (q - 1))
                    sp.dma_start(mod_chunk[q % 2], wm[:, 2 + q // KT, q % KT, :]).then_inc(mod2_in[q % 2], 16)

                q = 0
                for n, g in enumerate(slotted):
                    name, extra, _ = GROUPS[g]
                    if n >= 3:
                        free = outputs_before(slotted[n - 3] + 1)
                        while q < min(CHUNKS, KT * (1 + sum(a < free for a in SUM_AFTER)), 2 * free):
                            load_chunk(q)
                            q += 1
                        sp.wait_ge(proj_ready, free)
                    c0 = IN_OFF[name] + extra
                    sp.dma_start(w_slot[n % 3], wi[:, :, c0:c0 + MW]).then_inc(w_in_sem[n % 3], 16)
                sp.dma_start(m_raw[:, :], T["state_mlstm_m"].rearrange("a b d h -> (a b) (d h)").to_broadcast([P, 8])).then_inc(m_in, 16)
                sp.wait_ge(states_zero, 1)
                for name, S, w in (("state_gdn", gS, HD), ("state_hgrn", hS, HD), ("state_mlstm_c", mS, 65)):
                    for d in range(2):
                        for h in range(4):
                            par, pt = h % 2, h // 2
                            sp.dma_start(S[HD * par:HD * par + HD, 0, d, pt, w * par:w * par + HD],
                                         T[name][0, 0, d, h]).then_inc(states_in, 16)
                            if w == 65:
                                sp.dma_start(S[HD * par:HD * par + HD, 0, d, pt, w * par + HD:w * par + HD + 1],
                                             T["state_mlstm_n"][0, 0, d, h].rearrange("(n a) -> n a", a=1),
                                             allow_slow_non_contiguous=True).then_inc(states_in, 16)
                for m, n in enumerate(("gdn_norm_g", "hgrn_norm_g", "mlstm_norm_g")):
                    sp.dma_start(norm_row[:, m, :], T[n].to_broadcast([P, HD])).then_inc(n_in, 16)
                y_tail = T["y_rows"].rearrange("(b p) d -> p b d", p=P)[:, TOK * TOPK // P:, :]
                sp.dma_start(y_tail, spread(at["strict"][:, 0:D], 1, NE)).then_inc(tail_out, 16)
                sp.wait_ge(g_staken, 2)
                sp.wait_ge(m_staken, 2)
                sp.wait_ge(h_staken, 2)
                for name, S, w in (("new_gdn", gS, HD), ("new_hgrn", hS, HD), ("new_c", mS, 65)):
                    for d in range(2):
                        for h in range(4):
                            par, pt = h % 2, h // 2
                            sp.dma_start(T[name][0, 0, d, h],
                                         S[HD * par:HD * par + HD, 1, d, pt, w * par:w * par + HD]).then_inc(s_out, 16)
                            if w == 65:
                                sp.dma_start(T["new_n"][0, 0, d, h].rearrange("(n a) -> n a", a=1),
                                             S[HD * par:HD * par + HD, 1, d, pt, w * par + HD:w * par + HD + 1],
                                             allow_slow_non_contiguous=True).then_inc(s_out, 16)
                                sp.dma_start(T["new_m"][0, 0, d:d + 1, h:h + 1],
                                             mst[0:1, 1, d, 2 * par + pt:2 * par + pt + 1]).then_inc(s_out, 16)
                sp.wait_ge(s_out, 16 * 40)
                sp.wait_ge(tail_out, 16)

                sp.wait_ge(m_otaken, len(UNITS))
                sp.wait_ge(m_staken, len(UNITS))
                sp.dma_start(feats, T["feats"]).then_inc(filt_in, 16)
                sp.dma_start(fw1, T["filt_w1"].rearrange("a k n -> (a k) n")).then_inc(filt_in, 16)
                sp.dma_start(fw2, T["filt_w2"].rearrange("a k n -> (a k) n")).then_inc(filt_in, 16)
                sp.dma_start(fw3, T["filt_w3"].rearrange("a k n -> (a k) n")).then_inc(filt_in, 16)
                for i, n in enumerate(("filt_b1", "filt_freq", "filt_b2")):
                    sp.dma_start(fcol[:, i:i + 1], T[n].rearrange("a n -> n a"), allow_slow_non_contiguous=True).then_inc(filt_in, 16)
                sp.wait_ge(filt_in, 16 * 7)


            @block.tensor
            def _(pe):
                def mod_block(j):
                    pe.wait_ge(mod_in[j], 16)
                    for m in range(KT):
                        for k in range(KT):
                            mm = pe.matmul(PS[:, 6 + j, 2 * m:2 * m + 2], mod_slot[j][:, k, m:D:KT],
                                           scond[:, k, :], start=(k == 0), stop=(k == KT - 1))
                    mm.then_inc(mod_ready, 1)

                pe.wait_ge(cond_silu, 1)
                mod_block(0)
                mod_block(1)
                pe.wait_ge(consts_in, 16)
                pe.wait_ge(xn_done, NT)
                for k in range(KT):
                    if k >= 2:
                        pe.wait_ge(hT_smp, k - 1)
                        pe.wait_ge(hT_pro, k - 1)
                    for t in range(NT):
                        dst = PS[:, k % 2, t * P:(t + 1) * P] if t < 4 else PS[:, 2 + k % 2, 0:P]
                        mm = pe.transpose(dst, xt[:, t, k:D:KT], ident)
                    mm.then_inc(xT_ready, 1)
                pe.wait_ge(rows_in, 48)
                for k in range(6):
                    mm = pe.transpose(PS[:, 5, 16 * k:16 * k + 10], rows[0:10, k * P:(k + 1) * P], ident[0:10, 0:10])
                mm.then_inc(rows_T, 1)
                def decay_sums():
                    pe.wait_ge(scal_ready, 1)
                    for d in range(2):
                        pe.matmul(PS[:, 6, 40 * d:40 * d + 40], run[:, d, LV, :], gl[:, d].rearrange("p t w h -> p (t w h)"),
                                  start=True, stop=True)
                    pe.matmul(PS[:, 6, 128:208], ones, gl.rearrange("p d t w h -> p (d t w h)"),
                              start=True, stop=True).then_inc(scal_ps, 1)

                def l2_part(i):
                    if i == 0:
                        pe.wait_ge(sq_done, 1)
                    elif i == 1:
                        pe.wait_ge(scal_done, 1)
                    else:
                        pe.wait_ge(l2_eps, i - 1)
                    pe.matmul(PS[:, 7 - i % 2, :], blk, sq[:, i * 512:(i + 1) * 512], start=True, stop=True).then_inc(l2_sum, 1)

                for n, (g, i) in enumerate(OUTPUTS):
                    name, extra, kind = GROUPS[g]
                    b0, b1 = 2 * (n % 3), 2 * (n % 3) + 1
                    if i == 0:
                        if kind == "s":
                            pe.wait_ge(small_in, 32)
                        else:
                            s = slotted.index(g)
                            pe.wait_ge(w_in_sem[s % 3], 16 * (s // 3 + 1))
                            w = w_slot[s % 3]
                    if n == 0:
                        pe.wait_ge(hT_smp, KT)
                        pe.wait_ge(hT_pro, KT)
                    if n == 2:
                        pe.wait_ge(taps_ready, 1)
                    if n >= 3:
                        pe.wait_ge(proj_taken, n - 2)
                    if kind == "f":
                        for k in range(KT):
                            pe.matmul(PS[:, b0, :], w[:, k, i * P:(i + 1) * P], hT[:, k, 0:SMP], start=(k == 0), stop=(k == KT - 1))
                        for k in range(KT):
                            mm = pe.matmul(PS[:, b1, 0:P], w[:, k, i * P:(i + 1) * P], hT[:, k, SMP:TOK],
                                           start=(k == 0), stop=(k == KT - 1))
                    else:
                        src = hTp if name in ("ib", "fb") and i < 4 else hT
                        if src is hTp:
                            pe.wait_ge(hTp_done, KT)
                        rhs = w_small if kind == "s" else w
                        for k in range(KT):
                            mm = pe.matmul(PS[:, b0, 0:rhs.shape[2]], src[:, k, i * P:(i + 1) * P], rhs[:, k, :],
                                           start=(k == 0), stop=(k == KT - 1))
                    mm.then_inc(proj_ready, 1)
                    if n in SUM_AFTER:
                        j = SUM_AFTER.index(n)
                        if j == 0:
                            pe.wait_ge(mod_taken, 2)
                        pe.wait_ge(mod2_mul, 2 * KT * (j + 1))
                        for m in range(KT):
                            for c in range(2):
                                a = 16 * j + 2 * m + c
                                mm = pe.matmul(PS[:, 6, a:a + 1], mod_acc[c][:, m:D:KT], ones[:, 0:1], start=True, stop=True)
                        mm.then_inc(mod2_ready, 1)
                    if n == LAST - 3:
                        decay_sums()
                        l2_part(0)
                        l2_part(1)
                    elif n == LAST - 2:
                        l2_part(2)
                        l2_part(3)
                    elif n == LAST - 1:
                        l2_part(4)
                pe.wait_ge(proj_taken, len(OUTPUTS))
                def to_tokens(n):
                    if n == 0:
                        pe.wait_ge(k_unit, 1)
                        pe.wait_ge(silu_done, 4)
                    if n == NT:
                        pe.wait_ge(hy_out, 2)
                    if n >= 3:
                        pe.wait_ge(tr_taken, n - 2)
                    c = slice((n % NT) * P, (n % NT + 1) * P)
                    four = (qkT[:, 2, c], qkT[:, 3, c], vT[:, 0, c], vT[:, 1, c]) if n < NT else \
                           (mqkT[:, 2, c], mqkT[:, 3, c], hy[:, 0, c], hy[:, 1, c])
                    for j, src in enumerate(four):
                        mm = pe.transpose(PS[:, 5 + n % 3, j * P:(j + 1) * P], src, ident)
                    mm.then_inc(tr_ready, 1)

                for n in range(NT):
                    to_tokens(n)
                def gdn_head(u):
                    d, t, s = UNITS[u]
                    c = slice(t * P, (t + 1) * P)
                    pe.wait_ge(g_diag, u + 1)
                    if u == 0:
                        pe.wait_ge(k_unit, 1)
                        pe.wait_ge(proj_taken, len(OUTPUTS))
                    else:
                        pe.wait_ge(m_otaken, u)
                        pe.wait_ge(m_staken, u)
                    pe.matmul(PS[:, 0, :], ones, gDG.rearrange("p h n -> p (h n)"), start=True, stop=True).then_inc(g_row, 1)
                    for b, q in ((1, 2), (3, 0)):
                        for pt in range(2):
                            for par in range(2):
                                r = slice(HD * par, HD * par + HD)
                                mm = pe.matmul(PS[:, b + par, P * pt:P * pt + P], qkT[r, 2 + pt, c], qkT[r, q + pt, c],
                                               start=True, stop=True)
                    mm.then_inc(g_kq, 1)

                def mlstm_rows(u, n):
                    d, t, s = UNITS[u]
                    c = slice(t * P, (t + 1) * P)
                    if n == 0:
                        pe.wait_ge(m_dc, u + 1)
                        pe.wait_ge(g_egb, u + 1)
                        pe.wait_ge(g_at, u + 1)
                        pe.matmul(PS[:, 0, :], ones, mDC.rearrange("p h n -> p (h n)"), start=True, stop=True).then_inc(m_cb, 1)
                    elif n == 1:
                        for pt in range(2):
                            for par in range(2):
                                r = slice(HD * par, HD * par + HD)
                                mm = pe.matmul(PS[:, 2 + par, P * pt:P * pt + P], mqkT[r, 2 + pt, c], mqkT[r, pt, c],
                                               start=True, stop=True)
                        mm.then_inc(m_qk, 1)
                    elif n == 2:
                        pe.wait_ge(m_dmu, u + 1)
                        pe.matmul(PS[:, 1, :], ones, mDC.rearrange("p h n -> p (h n)"), start=True, stop=True).then_inc(m_mb, 1)
                    elif n == 4:
                        pe.wait_ge(m_qd, u + 1)
                        pe.wait_ge(m_wt, u + 1)
                        if u == 0:
                            pe.wait_ge(ones_col, 1)
                        if s == 0 and u < 4:
                            pe.wait_ge(states_in, 16 * 32)
                        for pt in range(2):
                            pe.matmul(PS[:, 4, 130 * pt:130 * pt + 130], mqd[:, pt, :], mS[:, s, d, pt, :], start=True, stop=False)
                            for par in range(2):
                                o = 130 * pt + 65 * par
                                mm = pe.matmul(PS[:, 4, o:o + 65], mWT[:, 2 * par + pt, :], mv[:, t, 2 * pt + par, :],
                                               start=False, stop=par == 1)
                        mm.then_inc(m_o, 1)
                    elif n == 5:
                        pe.wait_ge(m_kw, u + 1)
                        for pt in range(2):
                            mm = pe.matmul(PS[:, 0, 130 * pt:130 * pt + 130], mkw[:, pt, :],
                                           mv[:, t, 2 * pt:2 * pt + 2, :].rearrange("p h n -> p (h n)"), start=True, stop=True)
                        mm.then_inc(m_st, 1)

                pe.wait_ge(states_zero, 1)
                gdn_head(0)
                for n in range(NT, 2 * NT):
                    to_tokens(n)
                pe.wait_ge(tr_taken, 2 * NT)
                for u, (d, t, s) in enumerate(UNITS):
                    for n in range(LV):
                        pe.wait_ge(g_ms, LV * u + n + 1)
                        if n > 0:
                            pe.wait_ge(g_tn, (LV - 1) * u + n)
                        elif u > 0:
                            pe.wait_ge(g_otaken, u)
                        for h in range(4):
                            mm = pe.matmul(PS[:, 5, P * h:P * h + P], gMS[n % 2][:, h, :], gT[:, h, :] if n else ident,
                                           start=True, stop=True)
                        mm.then_inc(g_lv1, 1)
                        mlstm_rows(u, n)
                        pe.wait_ge(g_p, LV * u + n + 1)
                        if n > 0:
                            pe.wait_ge(g_t, LV * u + n)
                        elif u > 0:
                            pe.wait_ge(g_staken, u)
                        if 0 < n < LV - 1:
                            for h in range(4):
                                mm = pe.matmul(PS[:, 6, P * h:P * h + P], gTT[:, h, :], gP[:, h, :], start=True, stop=True)
                            mm.then_inc(g_lvT, 1)
                        for h in range(4):
                            mm = pe.matmul(PS[:, 7, P * h:P * h + P], gP[:, h, :], gTT[:, h, :] if n else ident,
                                           start=True, stop=True)
                        mm.then_inc(g_lv2, 1)
                    if u + 1 < len(UNITS):
                        gdn_head(u + 1)
                    pe.wait_ge(g_t, LV * (u + 1))
                    pe.wait_ge(g_bk, u + 1)
                    for h in range(4):
                        mm = pe.matmul(PS[:, 5, P * h:P * h + P], gTT[:, h, :], gBK[:, h, :], start=True, stop=True)
                    mm.then_inc(g_uw, 1)
                    pe.wait_ge(g_wt, u + 1)
                    for pt in range(2):
                        mm = pe.transpose(PS[:, 6, P * pt:P * pt + P], gwt[:, pt, :], ident)
                    mm.then_inc(g_wTr, 1)
                    pe.wait_ge(g_wT, u + 1)
                    if s == 0 and u < 4:
                        pe.wait_ge(states_in, 16 * 32)
                    for pt in range(2):
                        mm = pe.matmul(PS[:, 7, P * pt:P * pt + P], gwT[:, pt, :], gS[:, s, d, pt, :], start=True, stop=True)
                    mm.then_inc(g_ws, 1)
                    pe.wait_ge(g_vn, u + 1)
                    pe.wait_ge(g_qd, u + 1)
                    for pt in range(2):
                        pe.matmul(PS[:, 5, P * pt:P * pt + P], gqd[u % 2][:, pt, :], gS[:, s, d, pt, :], start=True, stop=False)
                        for par in range(2):
                            o = P * pt + HD * par
                            mm = pe.matmul(PS[:, 5, o:o + HD], gAT[u % 2][:, 2 * par + pt, :], gvn[:, pt, HD * par:HD * par + HD],
                                           start=False, stop=par == 1)
                    mm.then_inc(g_o, 1)
                    pe.wait_ge(g_kd, u + 1)
                    for pt in range(2):
                        mm = pe.matmul(PS[:, 6, P * pt:P * pt + P], gkd[:, pt, :], gvn[:, pt, :], start=True, stop=True)
                    mm.then_inc(g_st, 1)
                def hgrn_exponents(u, q):
                    d = UNITS[u][0]
                    if q == 0:
                        pe.wait_ge(h_lt, u + 1)
                        if u == 0:
                            pe.wait_ge(m_otaken, len(UNITS))
                            pe.wait_ge(m_staken, len(UNITS))
                            pe.wait_ge(g_staken, len(UNITS))
                        else:
                            pe.wait_ge(h_e, u)
                    pt, half = q // 2, q % 2
                    mm = pe.matmul(PS[:, q, :], hlt[:, P * pt:P * pt + P],
                                   run[:, d, 4 * half:4 * half + 4, :].rearrange("p l n -> p (l n)"), start=True, stop=True)
                    if q == 3:
                        mm.then_inc(h_x, 1)

                def hgrn_keys(u):
                    if u > 0:
                        pe.wait_ge(h_merge, (LV + 1) * (u - 1) + LV)
                    pe.matmul(PS[:, 5, 0:256], after[:, UNITS[u][0], :], hlt, start=True, stop=True).then_inc(h_xa, 1)
                    pe.wait_ge(h_kt, u + 1)
                    for pt in range(2):
                        mm = pe.transpose(PS[:, 4, P * pt:P * pt + P], hkt[:, P * pt:P * pt + P], ident)
                    mm.then_inc(h_kT, 1)

                for q in range(4):
                    hgrn_exponents(0, q)
                hgrn_keys(0)
                for u, (d, t, s) in enumerate(UNITS):
                    c = slice(t * P, (t + 1) * P)
                    for r in range(LV + 1):
                        if r == 0:
                            pe.wait_ge(h_kTs, u + 1)
                            pe.wait_ge(h_ek, u + 1)
                        if r == 1:
                            pe.wait_ge(h_ke, u + 1)
                            pe.wait_ge(h_qe, u + 1)
                            if u > 0:
                                pe.wait_ge(h_otaken, u)
                                pe.wait_ge(h_staken, u)
                        if r >= 2:
                            pe.wait_ge(h_merge, (LV + 1) * u + r - 1)
                        for pt in range(2):
                            for par in range(2):
                                q = slice(HD * par, HD * par + HD)
                                k_, q_ = (hkT[q, P * pt:P * pt + P], hqT[q, pt, c]) if r == 0 else \
                                         (hKE[q, pt, r - 1, :], hQE[u % 2][q, pt, r - 1, :])
                                mm = pe.matmul(PS[:, 4 + 2 * (r % 2) + par, P * pt:P * pt + P], k_, q_, start=True, stop=True)
                        mm.then_inc(h_lvl, 1)
                        if 1 <= r <= 4 and u + 1 < len(UNITS):
                            hgrn_exponents(u + 1, r - 1)
                    if u + 1 < len(UNITS):
                        hgrn_keys(u + 1)
                    pe.wait_ge(h_merge, (LV + 1) * (u + 1))
                    for pt in range(2):
                        pe.matmul(PS[:, 6, P * pt:P * pt + P], hQE[u % 2][:, pt, LV, :], hS[:, s, d, pt, :], start=True, stop=False)
                        for par in range(2):
                            o = P * pt + HD * par
                            mm = pe.matmul(PS[:, 6, o:o + HD], hAT[:, 2 * par + pt, :], hv[:, t, o:o + HD],
                                           start=False, stop=par == 1)
                    mm.then_inc(h_o, 1)
                    pe.wait_ge(h_kd, u + 1)
                    for pt in range(2):
                        mm = pe.matmul(PS[:, 7, P * pt:P * pt + P], hkd[:, P * pt:P * pt + P], hv[:, t, P * pt:P * pt + P],
                                       start=True, stop=True)
                    mm.then_inc(h_st, 1)
                pe.wait_ge(h_e, len(UNITS))
                for i, m in enumerate(MIX):
                    if i < 2:
                        pe.wait_ge(n_on, i + 1)
                    else:
                        pe.wait_ge(n_last, 1)
                    for pt in range(2):
                        if i > 0:
                            pe.wait_ge(n_taken, 2 * (i - 1) + pt + 1)
                        for t in range(NT):
                            dst = PS[:, 2 * pt, t * P:(t + 1) * P] if t < 4 else PS[:, 2 * pt + 1, 0:P]
                            mm = pe.transpose(dst, o_tok[:, m, t, P * pt:P * pt + P], ident)
                        mm.then_inc(n_tr, 1)


            @block.vector
            def _(dve):
                dve_order = Steps(dve, "dve_order1")
                def mod_take(j):
                    dve.wait_ge(mod_ready, j + 1)
                    dve.tensor_tensor(modT[:, j], PS[:, 6 + j, 0:16].rearrange("p (k c) -> p k c", c=2),
                                      spread(bmod[:, j], 2, 2), ALU.add).then_inc(mod_taken, 1)

                dve.wait_ge(sq1_done, 1)
                dve.tensor_scalar(sumsq[:, 0:NT], sumsq[:, 0:NT], 1.0 / D, EPS, ALU.mult, ALU.add).then_inc(mean1, 1)
                dve.wait_ge(root1, 1)
                dve_order.done(dve.reciprocal(rstd[:, 0:NT], rstd[:, 0:NT]))
                for t in range(NT):
                    dve.tensor_scalar(xt[:, t, :], xt[:, t, :], rstd[:, t:t + 1], None, ALU.mult).then_inc(xn_done, 1)
                dve.wait_ge(params_in, 48)
                mod_take(0)
                mod_take(1)
                dve.wait_ge(mod_taken, 2)
                dve_order.done(dve.tensor_scalar(scl[:, :, :], modT[:, 1], 1.0, None, ALU.add))
                dve.tensor_tensor(scl[:, :, :], scl[:, :, :], spread(g1p, 2, 2), ALU.mult).then_inc(scl_ready, 1)
                dve.wait_ge(scl_ready, 1)
                for k in range(KT):
                    dve.wait_ge(xT_ready, k + 1)
                    dve.tensor_scalar(hT[:, k, 0:SMP], PS[:, k % 2, :], scl[:, k, 0:1], modT[:, 0, k, 0:1], ALU.mult,
                                      ALU.add).then_inc(hT_smp, 1)
                dve.wait_ge(rows_T, 1)
                dve.tensor_copy(tapsT[:, :, :], PS[:, 5, 0:96].rearrange("p (k r) -> p k r", k=6)[:, :, 0:10]).then_inc(taps_ready, 1)
                dve.wait_ge(prm_in, 48)
                dve_order.done(dve.tensor_copy(prm.rearrange("p (g par pt) -> p g par pt", g=6, par=2),
                                               prm_raw.rearrange("p (g pt par) -> p g par pt", g=6, par=2)))
                dve.wait_ge(lb_in, 16)
                dve.tensor_tensor(lbt[1], lbt[0], lbt[0], ALU.subtract).then_inc(lb_work, 1)
                dve.wait_ge(lb_e, 1)
                dve_order.done(dve.reciprocal(lbt[1], lbt[0]))
                dve_order.done(dve.tensor_tensor(lbt[0], lbt[0], lbt[1], ALU.mult))
                dve_order.done(dve.tensor_tensor(lbt[0], lbt[0], lbt[0], ALU.subtract))
                dve_order.done(dve.tensor_scalar(lbt[1], lbt[0], -1.0, 1.0, ALU.mult, ALU.add))

                dve.wait_ge(cond_silu, 1)
                dve.wait_ge(mod_ready, 2)
                for q in range(CHUNKS):
                    j, k = q // KT, q % KT
                    dve.wait_ge(mod2_in[q % 2], 16 * (q // 2 + 1))
                    if k == 0 and j > 0:
                        dve.wait_ge(mod2_ready, j)
                    for c in range(2):
                        if k == 0:
                            i = dve.tensor_scalar(mod_acc[c], mod_chunk[q % 2], scond[:, k, c:c + 1], None, ALU.mult)
                        else:
                            dve.wait_ge(mod2_mul, 2 * q + c - 1)
                            i = dve.scalar_tensor_tensor(out=mod_acc[c], in0=mod_chunk[q % 2], scalar=scond[:, k, c:c + 1],
                                                         in1=mod_acc[c], op0=ALU.mult, op1=ALU.add)
                        i.then_inc(mod2_mul, 1)

                dve.wait_ge(proj_taken, 6)
                dve.wait_ge(taps_ready, 1)
                for tap in range(5):
                    for k in range(6):
                        src = pre[:, k, tap:tap + CONV_W]
                        if tap == 0:
                            i = dve.tensor_scalar(cbuf[:, k, :], src, tapsT[:, k, 0:1], None, ALU.mult)
                        else:
                            i = dve.scalar_tensor_tensor(out=cbuf[:, k, :], in0=src, scalar=tapsT[:, k, tap:tap + 1],
                                                         in1=cbuf[:, k, :], op0=ALU.mult, op1=ALU.add)
                    if tap < 4:
                        dve_order.done(i)
                i.then_inc(gdn_conv_read, 1)

                dve.wait_ge(mod2_ready, 4)
                dve_order.done(dve.tensor_tensor(modT[:, 2:6], PS[:, 6, 0:64].rearrange("p (j k c) -> p j k c", j=4, c=2),
                                                 spread(bmod[:, 2:6], 3, 2), ALU.add))

                dve.wait_ge(proj_taken, outputs_before(14))
                for g in range(2):
                    dve.tensor_tensor(spi[:, :, g, :], smt[:, :, g, :], spread(prm[:, 4 * g:4 * g + 4], 1, NT), ALU.add)
                    i = dve.tensor_tensor(spi[:, :, 2 + g, :], smt[:, :, 6 + g, :], spread(prm[:, 16 + 4 * g:20 + 4 * g], 1, NT), ALU.add)
                dve_order.done(i)
                dve.tensor_scalar(spi[:, :, 2:4, :], spi[:, :, 2:4, :], -1.0, None, ALU.mult).then_inc(softin, 1)
                for t in range(NT):
                    i = dve.scalar_tensor_tensor(out=fgate[:, t, :], in0=fgate[:, t, :], scalar=TINY, in1=lbt[1],
                                                 op0=ALU.max, op1=ALU.mult)
                dve_order.done(i)
                for t in range(NT):
                    i = dve.tensor_tensor(fgate[:, t, :], fgate[:, t, :], lbt[0], ALU.add)
                i.then_inc(fo_done, 1)
                dve.wait_ge(softlog, 1)
                for d in range(2):
                    for w in range(2):
                        i = dve.scalar_tensor_tensor(out=gl[:, d, :, w, :], in0=spi[:, :, 2 * w + d, :], scalar=0.0,
                                                     in1=spa[:, :, 2 * w + d, :], op0=ALU.max, op1=ALU.add)
                dve_order.done(i)
                dve.wait_ge(alog_exp, 1)
                for d in range(2):
                    dve.tensor_scalar(gl[:, d, :, 1, :], gl[:, d, :, 1, :], -1.0, None, ALU.mult)
                    i = dve.scalar_tensor_tensor(out=gl[:, d, :, 0, :], in0=gl[:, d, :, 0, :], scalar=-1.0,
                                                 in1=spread(nalog[:, 4 * d:4 * d + 4], 1, NT), op0=ALU.mult, op1=ALU.mult)
                i.then_inc(scal_ready, 1)
                dve.wait_ge(scal_ps, 1)
                dve.tensor_copy(cs.rearrange("p d t w h -> p (d t w h)"), PS[:, 6, 0:80])
                dve.tensor_copy(tot.rearrange("p d t w h -> p (d t w h)"), PS[:, 6, 128:208]).then_inc(scal_done, 1)
                dve.wait_ge(scal_done, 1)
                dve.wait_ge(egc_done, 1)
                dve.wait_ge(beta_done, 1)
                for d in range(2):
                    dve.tensor_tensor(beg[:, d], egc[:, d], beta[:, :, d, :], ALU.mult)
                    i = dve.tensor_tensor(cc[:, d], smt[:, :, 4 + d, :], cs[:, d, :, 1, :], ALU.subtract)
                i.then_inc(dve_beg, 1)

                def l2_take(i):
                    dve.wait_ge(l2_sum, i + 1)
                    part_i = rq[:, i * 512:(i + 1) * 512]
                    dve.tensor_scalar(part_i, PS[:, 7 - i % 2, :], EPS, None, ALU.add).then_inc(l2_eps, 1)
                    dve.wait_ge(l2_eps, i + 1)
                    dve.reciprocal(part_i, part_i).then_inc(l2_rec, 1)

                def hyena_conv(k):
                    dve.wait_ge(proj_taken, LAST - 5 + k + 1)
                    dve.wait_ge(silu_done, 4)
                    for tap in range(3):
                        src = pre[:, k, tap + 1:tap + 1 + CONV_W]
                        if tap == 0:
                            i = dve.tensor_scalar(cbuf[:, k, :], src, tapsT[:, k, 5:6], None, ALU.mult)
                        else:
                            i = dve.scalar_tensor_tensor(out=cbuf[:, k, :], in0=src, scalar=tapsT[:, k, 5 + tap:6 + tap],
                                                         in1=cbuf[:, k, :], op0=ALU.mult, op1=ALU.add)
                        if tap < 2:
                            dve_order.done(i)
                    i.then_inc(hy_conv, 1)

                l2_take(0)
                l2_take(1)
                hyena_conv(0)
                l2_take(2)
                l2_take(3)
                hyena_conv(1)
                l2_take(4)
                hyena_conv(2)
                dve.wait_ge(l2_root, 1)
                qk_flat = qkT.rearrange("p k n -> p (k n)")
                dve.scalar_tensor_tensor(out=qk_flat[:, 0:2 * TOK], in0=qk_flat[:, 0:2 * TOK], scalar=HD ** -0.5,
                                         in1=rq[:, 0:2 * TOK], op0=ALU.mult, op1=ALU.mult)
                dve.tensor_tensor(qk_flat[:, 2 * TOK:], qk_flat[:, 2 * TOK:], rq[:, 2 * TOK:], ALU.mult).then_inc(k_unit, 1)
                for k in range(3, 6):
                    hyena_conv(k)
                dve.wait_ge(m_in, 16)
                dve_order.done(dve.tensor_copy(mst[:, 0].rearrange("p d (par pt) -> p d par pt", par=2),
                                               m_raw.rearrange("p (d pt par) -> p d par pt", d=2, pt=2)))
                dve.wait_ge(m_zero, 1)

                def gdn_diag(u):
                    d, t, s = UNITS[u]
                    dve.tensor_tensor(gDG, spread(ident, 1, 4), spread(cs[:, d, t, 0, :], 2, P), ALU.mult).then_inc(g_diag, 1)

                def gdn_decays(u):
                    d, t, s = UNITS[u]
                    gc, end = cs[:, d, t, 0, :], last_token(d)
                    dve.wait_ge(g_row, u + 1)
                    if u > 0:
                        dve.wait_ge(g_kd, u)
                    row = heads(PS[:, 0, :])
                    dve.tensor_tensor(gel, row[:, :, end:end + 1].rearrange("p h a -> p (h a)"), gc, ALU.subtract).then_inc(g_eld, 1)
                    dve_order.done(dve.tensor_tensor(gX, spread(gc, 2, P), row, ALU.subtract))
                    dve.scalar_tensor_tensor(out=gX, in0=gX, scalar=0.0, in1=spread(big[:, d, :], 1, 4),
                                             op0=ALU.max, op1=ALU.add).then_inc(g_x, 1)

                def gdn_scores(u):
                    d, t, s = UNITS[u]
                    c = slice(t * P, (t + 1) * P)
                    dve.wait_ge(g_dt, u + 1)
                    dve.wait_ge(g_kq, u + 1)
                    dve.tensor_tensor(by_par(gMT), kq_banks(1), by_par(gDT), ALU.mult).then_inc(g_mt, 1)
                    dve.tensor_tensor(by_par(gAT[u % 2]), kq_banks(3), by_par(gDT), ALU.mult).then_inc(g_at, 1)
                    dve.wait_ge(g_egb, u + 1)
                    for par in range(2):
                        r = slice(HD * par, HD * par + HD)
                        i = dve.tensor_tensor(gqd[u % 2][r], qkT[r, 0:2, c], gEGB[u % 2][r, 2 * par:2 * par + 2, :], ALU.mult)
                    i.then_inc(g_qd, 1)

                def mlstm_c(u):
                    d, t, s = UNITS[u]
                    dve.tensor_tensor(mDC, spread(ident, 1, 4), spread(cc[:, d, t, :], 2, P), ALU.mult).then_inc(m_dc, 1)

                def mlstm_step(u, n):
                    d, t, s = UNITS[u]
                    c = slice(t * P, (t + 1) * P)
                    cj, m0, end = cc[:, d, t, :], mst[:, s, d, :], last_token(d)
                    row = heads(PS[:, 1, :])
                    row_end = row[:, :, end:end + 1].rearrange("p h a -> p (h a)")
                    if n == 1:
                        dve.wait_ge(m_cb, u + 1)
                        dve_order.done(dve.tensor_tensor(mX, heads(PS[:, 0, :]), spread(big[:, 1 - d, :], 1, 4), ALU.subtract))
                        dve_order.done(dve.tensor_reduce(mmx, mX, AX.X, ALU.max))
                        dve_order.done(dve.tensor_tensor(mmu, mmx, m0, ALU.max))
                        dve.tensor_tensor(mDC, spread(ident, 1, 4), spread(mmu, 2, P), ALU.mult).then_inc(m_dmu, 1)
                    elif n == 2:
                        dve.wait_ge(m_mb, u + 1)
                        dve.tensor_tensor(mex[:, 0, :], cj, row_end, ALU.subtract)
                        dve.tensor_tensor(mex[:, 1, :], m0, row_end, ALU.subtract)
                        dve.scalar_tensor_tensor(out=mex[:, 2, :], in0=cs[:, d, t, 1, :], scalar=-1.0, in1=mmu, op0=ALU.mult,
                                                 op1=ALU.subtract).then_inc(m_sm, 1)
                        dve_order.done(dve.tensor_tensor(mX, row, spread(cj, 2, P), ALU.subtract))
                        dve.scalar_tensor_tensor(out=mX, in0=mX, scalar=0.0, in1=spread(big[:, d, :], 1, 4),
                                                 op0=ALU.max, op1=ALU.add).then_inc(m_x, 1)
                        dve.tensor_tensor(mDC, row, spread(m0, 2, P), ALU.subtract).then_inc(m_eqx, 1)
                    elif n == 3:
                        dve.wait_ge(m_eq, u + 1)
                        dve.tensor_tensor(m0, tot[:, d, t, 1, :], row_end, ALU.add)
                        for par in range(2):
                            r = slice(HD * par, HD * par + HD)
                            i = dve.tensor_tensor(mqd[r], mqkT[r, 0:2, c], mDC[r, 2 * par:2 * par + 2, :], ALU.mult)
                        i.then_inc(m_qd, 1)
                        dve.wait_ge(m_wd, u + 1)
                        dve.wait_ge(m_qk, u + 1)
                        dve.tensor_tensor(by_par(mWT), kq_banks(2), by_par(mWD), ALU.mult).then_inc(m_wt, 1)
                    elif n == 5:
                        dve.wait_ge(m_ex, u + 1)
                        dve.wait_ge(m_o, u + 1)
                        num = PS[:, 4, 0:260].rearrange("p (h n) -> p h n", h=4)
                        den = num[:, :, HD:HD + 1].rearrange("p h a -> p (h a)")
                        dve_order.done(dve.tensor_scalar(mden, den, -1.0, None, ALU.mult))
                        dve_order.done(dve.tensor_tensor(mden, mden, den, ALU.max))
                        dve_order.done(dve.tensor_tensor(mden.rearrange("p (pt par) -> p pt par", pt=2),
                                                         mden.rearrange("p (pt par) -> p pt par", pt=2),
                                                         mex[:, 2, :].rearrange("p (par pt) -> p pt par", par=2), ALU.max))
                        dve_order.done(dve.reciprocal(mden, mden))
                        out = heads(o_tok[:, 2, t, :])
                        if FIRST[u]:
                            dve.tensor_tensor(out, num[:, :, 0:HD], spread(mden, 2, HD), ALU.mult).then_inc(m_otaken, 1)
                        else:
                            dve.tensor_tensor(heads(mtmp), num[:, :, 0:HD], spread(mden, 2, HD), ALU.mult).then_inc(m_otaken, 1)
                            dve.wait_ge(m_otaken, u + 1)
                            dve.tensor_tensor(out, out, heads(mtmp), ALU.add)
                    elif n == 6:
                        dve.wait_ge(m_st, u + 1)
                        for pt in range(2):
                            for par in range(2):
                                r, n = slice(HD * par, HD * par + HD), 65 * par
                                i = dve.scalar_tensor_tensor(out=mS[r, s, d, pt, n:n + 65], in0=mS[r, s, d, pt, n:n + 65],
                                                             scalar=mex[r, 1, 2 * par + pt:2 * par + pt + 1],
                                                             in1=PS[r, 0, 130 * pt + n:130 * pt + n + 65], op0=ALU.mult, op1=ALU.add)
                        i.then_inc(m_staken, 1)
                        dve.wait_ge(m_staken, u + 1)

                dve.wait_ge(proj_ready, len(OUTPUTS))
                gdn_diag(0)
                gdn_decays(0)
                dve.wait_ge(hy_out, 2)
                gdn_scores(0)
                for u, (d, t, s) in enumerate(UNITS):
                    end = last_token(d)
                    mlstm_c(u)
                    for n in range(LV):
                        dve.wait_ge(g_lv1, LV * u + n + 1)
                        dve.tensor_tensor(gP, heads(PS[:, 5, :]), spread(beta[:, t, d, :], 2, P), ALU.mult).then_inc(g_p, 1)
                        if n == 0:
                            dve.wait_ge(g_p, LV * u + 1)
                            dve.tensor_tensor(gT, spread(ident, 1, 4), gP, ALU.subtract).then_inc(g_tn, 1)
                            dve.wait_ge(g_lv2, LV * u + 1)
                            dve.tensor_tensor(gTT, spread(ident, 1, 4), heads(PS[:, 7, :]), ALU.subtract).then_inc(g_t, 1)
                        else:
                            mlstm_step(u, n)
                            if n == LV - 1 and u + 1 < len(UNITS):
                                gdn_diag(u + 1)
                            if n < LV - 1:
                                dve.wait_ge(g_lvT, (LV - 2) * u + n)
                                dve.wait_ge(g_tn, (LV - 1) * u + n)
                                dve.tensor_tensor(gT, gT, heads(PS[:, 6, :]), ALU.subtract).then_inc(g_tn, 1)
                            dve.wait_ge(g_lv2, LV * u + n + 1)
                            dve.wait_ge(g_t, LV * u + n)
                            dve.tensor_tensor(gTT, gTT, heads(PS[:, 7, :]), ALU.subtract).then_inc(g_t, 1)
                    if u + 1 < len(UNITS):
                        gdn_decays(u + 1)
                    dve.wait_ge(g_ws, u + 1)
                    dve.tensor_tensor(gvn.rearrange("p pt n -> p (pt n)"), gU.rearrange("p pt n -> p (pt n)"), PS[:, 7, 0:256],
                                      ALU.add).then_inc(g_vn, 1)
                    if u + 1 < len(UNITS):
                        gdn_scores(u + 1)
                    dve.wait_ge(g_o, u + 1)
                    if FIRST[u]:
                        dve.tensor_copy(o_tok[:, 0, t, :], PS[:, 5, 0:256]).then_inc(g_otaken, 1)
                    else:
                        dve.tensor_tensor(o_tok[:, 0, t, :], o_tok[:, 0, t, :], PS[:, 5, 0:256], ALU.add).then_inc(g_otaken, 1)
                    dve.wait_ge(g_st, u + 1)
                    for pt in range(2):
                        for par in range(2):
                            r, n = slice(HD * par, HD * par + HD), HD * par
                            i = dve.scalar_tensor_tensor(out=gS[r, s, d, pt, n:n + HD], in0=gS[r, s, d, pt, n:n + HD],
                                                         scalar=gEGB[u % 2][r, 2 * par + pt, end:end + 1],
                                                         in1=PS[r, 6, P * pt + n:P * pt + n + HD], op0=ALU.mult, op1=ALU.add)
                    i.then_inc(g_staken, 1)
                def norm_means(i):
                    ss = head_ss(i)
                    dve_order.done(dve.tensor_reduce(ss, osq4, AX.X, ALU.add))
                    dve.tensor_scalar(ss, ss, 1.0 / HD, EPS, ALU.mult, ALU.add).then_inc(n_ss, 1)

                def norm_reciprocal(i):
                    dve.wait_ge(n_root, i + 1)
                    dve.reciprocal(head_ss(i), head_ss(i)).then_inc(n_rec, 1)

                def hgrn_queries(u, pt):
                    t = UNITS[u][1]
                    dve.wait_ge(h_e, u + 1)
                    i = dve.tensor_tensor(hQE[u % 2][:, pt], spread(hqT[:, pt, t * P:(t + 1) * P], 1, LV + 1), hE[u % 2][:, pt], ALU.mult)
                    if pt == 1:
                        i.then_inc(h_qe, 1)

                for pt in range(2):
                    hgrn_queries(0, pt)
                for u, (d, t, s) in enumerate(UNITS):
                    end = last_token(d)
                    A4 = hAT.rearrange("p (par pt) n -> p par pt n", par=2)
                    for r in range(LV + 1):
                        dve.wait_ge(h_lvl, (LV + 1) * u + r + 1)
                        b = 4 + 2 * (r % 2)
                        src = PS[:, b:b + 2, 0:256].rearrange("p par (pt n) -> p par pt n", pt=2)
                        if r == 0:
                            dve.tensor_tensor(A4, src, spread(spread(ident, 1, 2), 1, 2), ALU.mult).then_inc(h_merge, 1)
                        else:
                            dve.wait_ge(h_merge, (LV + 1) * u + r)
                            mask = strict[:, d, r - 1, :].bitcast(U32)
                            dve.copy_predicated(A4, spread(spread(mask, 1, 2), 1, 2), src).then_inc(h_merge, 1)
                        if r >= LV - 1 and u + 1 < len(UNITS):
                            hgrn_queries(u + 1, r - LV + 1)
                    dve.wait_ge(h_o, u + 1)
                    if FIRST[u]:
                        dve.tensor_copy(o_tok[:, 1, t, :], PS[:, 6, 0:256]).then_inc(h_otaken, 1)
                    else:
                        dve.tensor_tensor(o_tok[:, 1, t, :], o_tok[:, 1, t, :], PS[:, 6, 0:256], ALU.add).then_inc(h_otaken, 1)
                    dve.wait_ge(h_st, u + 1)
                    for pt in range(2):
                        for par in range(2):
                            r, n = slice(HD * par, HD * par + HD), HD * par
                            i = dve.scalar_tensor_tensor(out=hS[r, s, d, pt, n:n + HD], in0=hS[r, s, d, pt, n:n + HD],
                                                         scalar=hE[u % 2][r, pt, LV, end:end + 1],
                                                         in1=PS[r, 7, P * pt + n:P * pt + n + HD], op0=ALU.mult, op1=ALU.add)
                    i.then_inc(h_staken, 1)
                    if u in (4, 7):
                        dve.wait_ge(n_sq, 1 if u == 4 else 2)
                        norm_means(0 if u == 4 else 1)
                    elif u in (5, 8):
                        norm_reciprocal(0 if u == 5 else 1)

                def gate_heads(i):
                    m = MIX[i]
                    for pt in range(2):
                        dve.wait_ge(n_tr, 2 * i + pt + 1)
                        y = yT[:, 2 * m + pt, :]
                        b = 2 * pt
                        if m == 1:
                            dst = y[:, 0:SMP].rearrange("p (r w) -> p w r", w=GW)
                            src = PS[:, b, :].rearrange("p (w r) -> p w r", r=SMP // GW)
                        else:
                            dst, src = y[:, 0:SMP], PS[:, b, :]
                        dve.tensor_tensor(dst, dst, src, ALU.mult)
                        dve.tensor_tensor(y[:, SMP:TOK], y[:, SMP:TOK], PS[:, b + 1, 0:P], ALU.mult).then_inc(n_taken, 1)

                dve.wait_ge(h_otaken, len(UNITS))
                dve_order.done(dve.tensor_tensor(osq, head_out(2), head_out(2), ALU.mult))
                norm_means(2)
                gate_heads(0)
                norm_reciprocal(2)
                dve.wait_ge(n_rec, 3)
                last_heads = head_out(2).rearrange("p (h n) -> p h n", n=HD)
                dve_order.done(dve.tensor_tensor(last_heads, last_heads, spread(head_ss(2), 2, HD), ALU.mult))
                dve.wait_ge(n_in, 48)
                dve.tensor_tensor(last_heads, last_heads, spread(norm_row[:, MIX[2], :], 1, 20), ALU.mult).then_inc(n_last, 1)
                gate_heads(1)
                gate_heads(2)

            @block.scalar
            def _(act):
                act_order = Steps(act, "act_order1")
                act.wait_ge(cond_in, 32)
                act.activation(scond[:, :, :].rearrange("p k c -> p c k"), cond[:, :, :], ACT.Silu).then_inc(cond_silu, 1)
                act.wait_ge(x_in, 32)
                for t in range(NT):
                    i = act.activation(junk, xt[:, t, :], ACT.Square, accum_out=sumsq[:, t:t + 1])
                    if t < NT - 1:
                        act_order.done(i)
                i.then_inc(sq1_done, 1)
                act.wait_ge(mean1, 1)
                act.activation(rstd[:, 0:NT], sumsq[:, 0:NT], ACT.Sqrt).then_inc(root1, 1)
                for k in range(KT):
                    act.wait_ge(xT_ready, k + 1)
                    act.wait_ge(scl_ready, 1)
                    act.activation(hT[:, k, SMP:TOK], PS[:, 2 + k % 2, 0:P], ACT.Identity, scale=scl[:, k, 1:2],
                                   bias=modT[:, 0, k, 1:2]).then_inc(hT_pro, 1)
                act.wait_ge(lb_work, 1)
                act.activation(lbt[0], lbt[1], ACT.Exp).then_inc(lb_e, 1)
                def leave(dst_s, dst_p, b0, func, scale=1.0):
                    act.activation(dst_s, PS[:, b0, :], func, scale=scale)
                    act.activation(dst_p, PS[:, b0 + 1, 0:P], func, scale=scale).then_inc(proj_taken, 1)

                PRO = slice(SMP + 2, SMP + 2 + P)

                def silu_qkv():
                    act.wait_ge(gdn_conv_read, 1)
                    act.activation(qkT[:, :, 0:SMP], cbuf[:, 0:4, 0:SMP], ACT.Silu).then_inc(silu_done, 1)
                    act.activation(qkT[:, :, SMP:TOK], cbuf[:, 0:4, PRO], ACT.Silu).then_inc(silu_done, 1)
                    act.activation(vT[:, :, 0:SMP], cbuf[:, 4:6, 0:SMP], ACT.Silu).then_inc(silu_done, 1)
                    act.activation(vT[:, :, SMP:TOK], cbuf[:, 4:6, PRO], ACT.Silu).then_inc(silu_done, 1)

                def decay_inputs():
                    act.activation(beta[:, :, :, :], smt[:, :, 2:4, :], ACT.Sigmoid).then_inc(beta_done, 1)
                    act.wait_ge(softin, 1)
                    act_order.done(act.activation(spa[:, :, :, :], spi[:, :, :, :], ACT.Abs))
                    act_order.done(act.activation(spa[:, :, :, :], spa[:, :, :, :], ACT.Exp, scale=-1.0))
                    act.activation(nalog[:, :], prm[:, 8:16], ACT.Exp).then_inc(alog_exp, 1)
                    act.activation(spa[:, :, :, :], spa[:, :, :, :], ACT.Ln, bias=1.0).then_inc(softlog, 1)

                GATE_AT = dict(ga=0, gb=2, oc=4)
                for n, (g, i) in enumerate(OUTPUTS):
                    name, extra, kind = GROUPS[g]
                    b0 = 2 * (n % 3)
                    if n == LAST - 4:
                        act.wait_ge(proj_taken, n)
                        decay_inputs()
                    elif n == LAST - 2:
                        act.wait_ge(scal_done, 1)
                        act.activation(egc[:, :, :, :], cs[:, :, :, 0, :], ACT.Exp).then_inc(egc_done, 1)
                    act.wait_ge(proj_ready, n + 1)
                    if name in ("qa", "ka", "va", "ud"):
                        j = {"qa": 0, "ka": 2, "va": 4, "ud": 2 * (extra // MW)}[name] + i
                        if n == 0:
                            act.wait_ge(pads_zero, 3)
                        if name == "ud" and extra == 0 and i == 0:
                            silu_qkv()
                        leave(pre[:, j, 2:2 + SMP], pre[:, j, SMP + 4:SMP + 4 + P], b0, ACT.Copy)
                    elif name in GATE_AT:
                        j = GATE_AT[name] + i
                        leave(yT[:, j, 0:SMP], yT[:, j, SMP:TOK], b0, ACT.Silu if name == "ga" else ACT.Sigmoid)
                    elif name == "qb":
                        act.activation(hqT[:, i, 0:SMP].rearrange("p (w r) -> p w r", r=SMP // GW),
                                       PS[:, b0, :].rearrange("p (r w) -> p w r", w=GW), ACT.Copy)
                        act.activation(hqT[:, i, SMP:TOK], PS[:, b0 + 1, 0:P], ACT.Copy).then_inc(proj_taken, 1)
                    elif name in ("qc", "kc"):
                        j = i if name == "qc" else 2 + i
                        leave(mqkT[:, j, 0:SMP], mqkT[:, j, SMP:TOK], b0, ACT.Copy, 1.0 if name == "qc" else HD ** -0.5)
                    elif name == "ib":
                        act.activation(hv[:, i, :], PS[:, b0, 0:MW], ACT.Copy).then_inc(proj_taken, 1)
                    elif name == "fb":
                        act.activation(fgate[:, i, extra:extra + MW], PS[:, b0, 0:MW], ACT.Sigmoid).then_inc(proj_taken, 1)
                    elif name == "vc":
                        act.activation(mv[:, i, :, 0:HD], PS[:, b0, 0:MW].rearrange("p (h n) -> p h n", h=4),
                                       ACT.Copy).then_inc(proj_taken, 1)
                    else:
                        act.activation(smt[:, i].rearrange("p g (par pt) -> p g par pt", par=2),
                                       PS[:, b0, 0:32].rearrange("p (g pt par) -> p g par pt", pt=2, par=2),
                                       ACT.Copy).then_inc(proj_taken, 1)
                act.wait_ge(l2_rec, 5)
                act.activation(rq, rq, ACT.Sqrt).then_inc(l2_root, 1)
                def take_tokens(n):
                    dst = kv_tok[:, n, :] if n < NT else mh_tok[:, n - NT, :]
                    act.wait_ge(tr_ready, n + 1)
                    act.activation(dst, PS[:, 5 + n % 3, :], ACT.Copy).then_inc(tr_taken, 1)

                for n in range(NT):
                    take_tokens(n)
                act.wait_ge(hy_conv, 6)
                act.activation(hy[:, :, 0:SMP], cbuf[:, 0:4, 0:SMP], ACT.Copy)
                act.activation(hy[:, :, SMP:TOK], cbuf[:, 0:4, PRO], ACT.Copy).then_inc(hy_out, 1)
                act.activation(yT[:, 6:8, 0:SMP], cbuf[:, 4:6, 0:SMP], ACT.Copy)
                act.activation(yT[:, 6:8, SMP:TOK], cbuf[:, 4:6, PRO], ACT.Copy).then_inc(hy_out, 1)

                def gdn_exps(u):
                    act.wait_ge(g_x, u + 1)
                    act.activation(gDT, gX, ACT.Exp, scale=-1.0).then_inc(g_dt, 1)
                    if u >= 2:
                        act.wait_ge(g_staken, u - 1)
                    act.activation(gEGB[u % 2], heads(PS[:, 0, :]), ACT.Exp).then_inc(g_egb, 1)
                    act.activation(gel, gel, ACT.Exp).then_inc(g_el, 1)

                gdn_exps(0)
                for n in range(NT, 2 * NT):
                    take_tokens(n)
                for u in range(len(UNITS)):
                    act.wait_ge(m_sm, u + 1)
                    if u > 0:
                        act.wait_ge(m_kw, u)
                    act.activation(mex[:, :, :], mex[:, :, :], ACT.Exp).then_inc(m_ex, 1)
                    act.wait_ge(m_x, u + 1)
                    act.activation(mWD, mX, ACT.Exp, scale=-1.0).then_inc(m_wd, 1)
                    act.wait_ge(m_eqx, u + 1)
                    act.activation(mDC, mDC, ACT.Exp, scale=-1.0).then_inc(m_eq, 1)
                    act.wait_ge(g_uw, u + 1)
                    uw = PS[:, 5, :].rearrange("p (par pt n) -> p pt par n", par=2, pt=2)
                    act.activation(gU.rearrange("p pt (par n) -> p pt par n", par=2), uw[:, :, :, 0:HD], ACT.Copy)
                    act.activation(gwt.rearrange("p pt (par n) -> p pt par n", par=2), uw[:, :, :, HD:P], ACT.Copy,
                                   scale=-1.0).then_inc(g_wt, 1)
                    act.wait_ge(g_wTr, u + 1)
                    act.activation(gwT.rearrange("p pt n -> p (pt n)"), PS[:, 6, 0:256], ACT.Copy).then_inc(g_wT, 1)
                    if u + 1 < len(UNITS):
                        gdn_exps(u + 1)

                def norm_root(i):
                    act.wait_ge(n_ss, i + 1)
                    ss = head_ss(i)
                    act.activation(ss, ss, ACT.Sqrt).then_inc(n_root, 1)

                for u, (d, t, s) in enumerate(UNITS):
                    if u in (6, 9):
                        norm_root(0 if u == 6 else 1)
                    if u == 0:
                        act.wait_ge(fo_done, 1)
                        act.wait_ge(g_staken, len(UNITS))
                        act.wait_ge(m_staken, len(UNITS))
                    else:
                        act.wait_ge(h_xa, u)
                    act.activation(hlt, fgate[:, t, MW * d:MW * d + MW], ACT.Ln).then_inc(h_lt, 1)
                    act.wait_ge(h_x, u + 1)
                    if u >= 2:
                        act.wait_ge(h_staken, u - 1)
                    act.activation(hE[u % 2].rearrange("p pt l n -> p (pt l n)"), PS[:, 0:4, :].rearrange("p b n -> p (b n)"),
                                   ACT.Exp).then_inc(h_e, 1)
                    act.wait_ge(h_kT, u + 1)
                    if u >= 1:
                        act.wait_ge(h_ke, u)
                    act.activation(hkT, PS[:, 4, 0:256], ACT.Copy).then_inc(h_kTs, 1)
                    if u >= 1:
                        act.wait_ge(h_st, u)
                    act.activation(hkd, PS[:, 5, 0:256], ACT.Exp).then_inc(h_ek, 1)
                norm_root(2)

            @block.gpsimd
            def _(pool):
                pool_order = Steps(pool, "pool_order1")
                pool.memset(rows[:, :], 0.0).then_inc(rows_zero, 1)

                for k in range(KT):
                    pool.wait_ge(hT_smp, k + 1)
                    pool.tensor_copy(hTp[:, k].rearrange("p (w r) -> p w r", r=SMP // GW),
                                     hT[:, k, 0:SMP].rearrange("p (r w) -> p w r", w=GW)).then_inc(hTp_done, 1)

                pool.wait_ge(mod_ready, 2)
                pool.memset(pre[:, :, 0:2], 0.0).then_inc(pads_zero, 1)
                pool.memset(pre[:, :, SMP + 2:SMP + 4], 0.0).then_inc(pads_zero, 1)
                pool.memset(pre[:, :, PRE_W - 2:PRE_W], 0.0).then_inc(pads_zero, 1)

                pool.memset(mv[:, :, :, HD:HD + 1], 1.0).then_inc(ones_col, 1)
                pool.wait_ge(silu_done, 2)
                pool.tensor_tensor(sq, qkT.rearrange("p k n -> p (k n)"), qkT.rearrange("p k n -> p (k n)"), ALU.mult).then_inc(sq_done, 1)
                pool.wait_ge(hy_conv, 6)
                pool.memset(part(r2_at, 3088), 0.0).then_inc(states_zero, 1)
                pool.memset(mst[:, 1], 0.0).then_inc(m_zero, 1)

                def mlstm_keys(u, t):
                    pool.wait_ge(m_ex, u + 1)
                    if u == 0:
                        pool.wait_ge(tr_taken, 2 * NT)
                    else:
                        pool.wait_ge(m_st, u)
                    kh = mh_tok[:, t, 0:MW].rearrange("p (pt par n) -> p par pt n", pt=2, par=2)
                    wk = mex[:, 0, :].rearrange("p (par pt) -> p par pt", par=2)
                    for par in range(2):
                        i = pool.tensor_tensor(mkw.rearrange("p pt (par n) -> p par pt n", par=2)[:, par], kh[:, par],
                                               spread(wk[:, par], 2, HD), ALU.mult)
                    i.then_inc(m_kw, 1)

                for u, (d, t, s) in enumerate(UNITS):
                    if u == 0:
                        pool.wait_ge(tr_taken, 5)
                        pool.wait_ge(scal_done, 1)
                        pool.wait_ge(dve_beg, 1)
                    else:
                        pool.wait_ge(g_uw, u)
                    kh = kv_tok[:, t, 0:MW].rearrange("p (pt par n) -> p par pt n", pt=2, par=2)
                    vh = kv_tok[:, t, MW:512].rearrange("p (pt par n) -> p par pt n", pt=2, par=2)
                    bkv = gBK.rearrange("p (par pt) n -> p par pt n", par=2)
                    bt = beta[:, t, d, :].rearrange("p (par pt) -> p par pt", par=2)
                    bg = beg[:, d, t, :].rearrange("p (par pt) -> p par pt", par=2)
                    for par in range(2):
                        pool.tensor_tensor(bkv[:, par, :, 0:HD], vh[:, par], spread(bt[:, par], 2, HD), ALU.mult)
                        i = pool.tensor_tensor(bkv[:, par, :, HD:P], kh[:, par], spread(bg[:, par], 2, HD), ALU.mult)
                    i.then_inc(g_bk, 1)
                    pool.wait_ge(g_mt, u + 1)
                    for n in range(LV):
                        if LV * u + n >= 2:
                            pool.wait_ge(g_lv1, LV * u + n - 1)
                        pool.tensor_tensor(gMS[n % 2], gMT, spread(strict[:, d, LV - 1 - n, :], 1, 4), ALU.mult).then_inc(g_ms, 1)
                        if n == 4:
                            mlstm_keys(u, t)
                    pool.wait_ge(g_el, u + 1)
                    el = gel.rearrange("p (par pt) -> p par pt", par=2)
                    for par in range(2):
                        i = pool.tensor_tensor(gkd.rearrange("p pt (par n) -> p par pt n", par=2)[:, par], kh[:, par],
                                               spread(el[:, par], 2, HD), ALU.mult)
                    i.then_inc(g_kd, 1)
                def norm_squares(i):
                    pool.tensor_tensor(osq, head_out(i), head_out(i), ALU.mult).then_inc(n_sq, 1)

                def norm_apply(i):
                    o4 = head_out(i).rearrange("p (h n) -> p h n", n=HD)
                    pool.wait_ge(n_rec, i + 1)
                    pool_order.done(pool.tensor_tensor(o4, o4, spread(head_ss(i), 2, HD), ALU.mult))
                    if i == 0:
                        pool.wait_ge(n_in, 48)
                    pool.tensor_tensor(o4, o4, spread(norm_row[:, MIX[i], :], 1, 20), ALU.mult).then_inc(n_on, 1)

                for u, (d, t, s) in enumerate(UNITS):
                    if u == 0:
                        pool.wait_ge(fo_done, 1)
                        pool.wait_ge(g_staken, len(UNITS))
                        pool.wait_ge(m_staken, len(UNITS))
                    else:
                        pool.wait_ge(h_kT, u)
                        pool.wait_ge(h_kd, u)
                    pool.tensor_scalar(hkt, fgate[:, t, MW * d:MW * d + MW], -1.0, 1.0, ALU.mult, ALU.add).then_inc(h_kt, 1)
                    pool.wait_ge(h_e, u + 1)
                    pool.wait_ge(h_kTs, u + 1)
                    for pt in range(2):
                        i = pool.tensor_tensor(hKE[:, pt], spread(hkT[:, P * pt:P * pt + P], 1, LV), hE[u % 2][:, pt, 0:LV, :], ALU.mult)
                    i.then_inc(h_ke, 1)
                    pool.wait_ge(h_ek, u + 1)
                    pool.wait_ge(h_kt, u + 1)
                    pool.tensor_tensor(hkd, hkd, hkt, ALU.mult).then_inc(h_kd, 1)
                    if u == 3:
                        norm_squares(0)
                    elif u == 6:
                        norm_apply(0)
                        norm_squares(1)
                    elif u == 9:
                        norm_apply(1)

        nc.all_engine_barrier()
        nc.clear_and_free_semaphores(stage_sems)
        stage_sems.clear()
        nc.all_engine_barrier()

        fz, fn, hid1, hid2 = (part(x_at + TOK * i, TOK)[0:HD] for i in range(4))
        hf = part(r1_at, NT * 1024).rearrange("p (t o s n) -> p t o s n", t=NT, o=2, s=2)
        hsum = part(r1_at + 8960, NT * 512).rearrange("p (t o n) -> p t o n", t=NT, o=2)
        hdif = part(r1_at + 11520, NT * 512).rearrange("p (t o n) -> p t o n", t=NT, o=2)
        hsq = [part(x_at + 2560 + 1024 * i, 1024).rearrange("p (o s n) -> p o s n", o=2, s=2) for i in range(2)]
        rn = part(x_at, 1024).rearrange("p (s n) -> p s n", s=2)
        HA = part(r1_at, 2560).rearrange("p (f n) -> p f n", f=5)
        HB = part(r1_at + 2560, 2560).rearrange("p (f n) -> p f n", f=5)
        HC = part(r1_at + 5120, 1024).rearrange("p (s n) -> p s n", s=2)
        spec = part(x_at + 1024, 2560).rearrange("p (f n) -> p f n", f=10)
        z1 = part(dec_at, 2 * TOK).rearrange("p (k n) -> p k n", k=2)
        ctmp = part(dec_at + 1300, TOK)
        z1_tok = part(r1_at + 14080, NT * MW).rearrange("p (t n) -> p t n", t=NT)
        pr = [part(x_at + 3584, 1024).rearrange("p (k n) -> p k n", k=4), part(r3_at, 1024).rearrange("p (k n) -> p k n", k=4)]
        FT = [(0, f) for f in range(4)] + [(1, 0)]
        (f_in, f_dft, f_1, f_z, f_s, f_h, f_hf, f_sq, f_nrm, f_ne, f_nr, f_rn, f_sd, f_H, f_Ht, f_HC, c_Z, c_pr, c_Y, c_y,
         c_out, c_z1, c_tr, c_trt, f_row) = (sem("f_" + n) for n in
         "in dft 1 z s h hf sq nrm ne nr rn sd H Ht HC cZ cpr cY cy cout cz1 ctr ctrt row".split())
        w_out = part(r1_at, 8192).rearrange("p (k n) -> p k n", k=8)
        xn = part(r1_at + 8192, 5120).rearrange("p (t n) -> p t n", t=NT)
        gate_row = part(r2_at, 4096).rearrange("p (g c n) -> p g c n", g=2, c=2)
        gdiag = [part(r2_at + 4096 + 1024 * i, 1024).rearrange("p (k n) -> p k n", k=8) for i in range(2)]
        acc = part(r2_at + 6144, 5120).rearrange("p (t n) -> p t n", t=NT)
        otmp = [part(r1_at + 13312 + 512 * i, 512) for i in range(2)]
        h2T = part(y_at, 5120).rearrange("p (k n) -> p k n", k=KT)
        rw = part(r3_at, 512).rearrange("p (k n) -> p k n", k=KT)
        rb = part(r3_at + 512, NE)
        score = part(r3_at + 576, NT * NE).rearrange("p (t n) -> p t n", t=NT)
        gate = part(r3_at + 896, NT * NE).rearrange("p (t n) -> p t n", t=NT)
        biased = small(NE)
        top8, gsum = small(8), small(8)
        fin_row = part(r1_at + 14336, 1024)
        scl2 = small(16).rearrange("p (k c) -> p k c", c=2)
        (o_w, o_x, o_rw, o_rb, o_fg, o_scl, o_gd, o_gr, o_gt, o_ps, o_mul, o_x1, n2_sq, n2_mean, n2_root, n2_xn, n2_tr, n2_s,
         n2_p, r_ps, r_sig, r_g, b_ps, b_cp) = (sem("o_" + n) for n in
         "w x rw rb fg scl gd gr gt ps mul x1 sq mean root xn tr s p rps rsig rg bps bcp".split())
        mask = part(r1_at, NT * NE).rearrange("p (t n) -> p t n", t=NT)
        h2 = xn
        U = 4
        BLOCKS = TOK * TOPK // P + NE
        GROUPS = (BLOCKS + U - 1) // U
        PAIRS = NT * TOPK
        LEAST = PAIRS // U
        MAGIC = 12582912.0
        ew = [part(a, 3072) for a in (r2_at + 11264, r2_at + 14336, r1_at + 8192, r1_at + 11264)]
        eg = [w[:, 0:1024].rearrange("p (k f) -> p k f", k=KT) for w in ew]
        eu = [w[:, 1024:2048].rearrange("p (k f) -> p k f", k=KT) for w in ew]
        ed = [w[:, 2048:3072] for w in ew]
        sact, sup, shid = (part(a, TOK) for a in (r2_at + 4096, r2_at + 4736, r2_at + 5376))

        keep = [r2_at + 17408]
        def kept(words):
            keep[0] += words
            assert keep[0] <= r2_at + 19300
            return part(keep[0] - words, words)
        index = kept(P + NT)
        slot_token = kept(BLOCKS + 1).bitcast(U32)
        block_expert = kept(P + 1)[0:1].bitcast(U32)
        dest_u = kept(PAIRS).bitcast(U32)
        token_col = [kept(1).bitcast(U32) for _ in range(U)]
        D1 = kept(NT * NE).rearrange("p (t n) -> p t n", t=NT)
        d8 = kept(PAIRS).rearrange("p (t k) -> p t k", t=NT)
        g8 = kept(PAIRS).rearrange("p (t k) -> p t k", t=NT)
        pick = kept(TOPK * NE).rearrange("p (k n) -> p k n", k=TOPK)
        taken = [r1_at + NT * NE]
        def scratch(words):
            taken[0] += words
            assert taken[0] <= r1_at + 8192
            return part(taken[0] - words, words)
        off = scratch((NT + 1) * NE).rearrange("p (t n) -> p t n", t=NT + 1)
        cum = [scratch(2 * NE) for _ in range(2)]
        cmpb, ecol, ngf, erow = scratch(NE), scratch(1), scratch(1), scratch(P)
        dest, hi, lo = scratch(PAIRS), scratch(PAIRS), scratch(PAIRS)
        at_slot = [scratch(TOPK * P).rearrange("p (k n) -> p k n", k=TOPK) for _ in range(2)]
        at_block = [scratch(TOPK * (BLOCKS + 1)).rearrange("p (k n) -> p k n", k=TOPK) for _ in range(2)]
        xg = [part(r1_at + 1024 * i, 1024) for i in range(U)]
        xT = [part(r1_at + 4096 + 1024 * i, 1024).rearrange("p (k n) -> p k n", k=KT) for i in range(2)]
        yb = [part(r1_at + 6144 + 1024 * i, 1024) for i in range(2)]
        gact = part(r2_at + 4096, P)
        hid = [part(r2_at + 4224 + P * i, P) for i in range(2)]
        GB = 8
        back = [part(r1_at + 1024 * i, 1024) for i in range(GB)]
        fmul = part(r2_at + 11264, 1024)
        fjunk = part(r2_at + 12288, 1024)

        m_idx, m_cnt, m_off, m_hi, m_at, m_bl, m_tab, m_ecol, m_erow, m_exp, m_tok, m_dest, m_beq = (
            sem("m_" + n) for n in "idx cnt off hi at bl tab ecol erow exp tok dest beq".split())
        s_w, s_gu, s_up, s_act, s_hid, s_ps, s_acc = (sem("s_" + n) for n in "w gu up act hid ps acc".split())
        h2_out, x_col = sem("h2_out"), sem("x_col")
        e_w, e_x = [sem(f"e_w{j}") for j in range(U)], [sem(f"e_x{j}") for j in range(U)]
        e_tr, e_xT, e_gu, e_silu, e_hid, e_ps, e_y = (sem("e_" + n) for n in "tr xT gu silu hid ps y".split())
        e_out = [sem("e_out0"), sem("e_out1")]
        g_in, g_used = [sem(f"g_in{j}") for j in range(GB)], sem("g_used")
        y_all = sem("y_all")
        f_x2, f_sq2, f_mn, f_rt, f_y, y_out = (sem("f2_" + n) for n in "x2 sq mn rt y out".split())

        def group_count(eng):
            eng.wait_ge(m_exp, 1)
            return eng.value_load(block_expert[0:1, P:P + 1], min_val=0, max_val=GROUPS - LEAST) + LEAST

        with nc.Block() as block:

            @block.sync
            def _(sp):
                sp.dma_start(decay.rearrange("p t n -> p (t n)"), T["decay"]).then_inc(f_in, 16)
                sp.dma_start(part(dft_at, 8704), T["dfts"]).then_inc(f_dft, 16)
                sp.wait_ge(c_z1, 8)
                sp.wait_ge(c_trt, NT)
                sp.dma_start(w_out[:, :, :], T["w_out"].rearrange("a (k p) n -> p (a k) n", p=P)).then_inc(o_w, 16)
                sp.dma_start(xt[:, 0:4, :], T["x_sample"].rearrange("a (t p) d -> p (a t) d", p=P)).then_inc(o_x, 16)
                sp.dma_start(xt[:, 4, :], T["x_prompt"].rearrange("a p d -> p (a d)")).then_inc(o_x, 16)
                sp.dma_start(rw[:, :, :], T["router_w"].rearrange("a (p k) n -> p (a k) n", k=KT)).then_inc(o_rw, 16)
                sp.dma_start(rb, T["router_bias"].to_broadcast([P, NE])).then_inc(o_rb, 16)
                sp.dma_start(fin_row, T["final_g"].rearrange("(a n) -> a n", a=1).to_broadcast([P, D])).then_inc(o_fg, 16)
                wg = T["exp_w_gate"].rearrange("a e (p k) f -> p (a e) k f", k=KT)
                wu = T["exp_w_up"].rearrange("a e (p k) f -> p (a e) k f", k=KT)
                wd = T["exp_w_down"].rearrange("a e f d -> f (a e) d")
                y_rows = T["y_rows"].rearrange("(b p) d -> p b d", p=P)

                sp.dma_start(eg[1], T["sh_w_gate"].rearrange("a (p k) f -> p (a k) f", k=KT)).then_inc(s_w, 16)
                sp.dma_start(eu[1], T["sh_w_up"].rearrange("a (p k) f -> p (a k) f", k=KT)).then_inc(s_w, 16)
                sp.dma_start(ed[1], T["sh_w_down"].rearrange("a f d -> f (a d)")).then_inc(s_w, 16)
                sp.dma_start(index, T["index"]).then_inc(m_idx, 16)
                for t in range(NT):
                    sp.wait_ge(b_cp, 2 * t + 2)
                    sp.dma_start(T["h2_rows"][t * P:(t + 1) * P, :], h2[:, t, :]).then_inc(h2_out, 16)

                def load_block(b, j):
                    e = sp.value_load(block_expert[0:1, bass.ds(b, 1)], min_val=0, max_val=NE - 1)
                    sp.dma_start(eg[j], wg[:, bass.ds(e, 1)].rearrange("p a k f -> p (a k) f")).then_inc(e_w[j], 16)
                    sp.dma_start(eu[j], wu[:, bass.ds(e, 1)].rearrange("p a k f -> p (a k) f")).then_inc(e_w[j], 16)
                    sp.dma_start(ed[j], wd[:, bass.ds(e, 1)].rearrange("p a d -> p (a d)")).then_inc(e_w[j], 16)

                def store_block(b, j):
                    sp.wait_ge(e_y, b + 1)
                    sp.dma_start(y_rows[:, bass.ds(b, 1)].rearrange("p b d -> p (b d)"), yb[j % 2]).then_inc(e_out[j % 2], 16)

                groups = group_count(sp)
                load_block(0, 0)
                sp.wait_ge(s_ps, 2 * NT)
                load_block(1, 1)
                sp.wait_ge(h2_out, 16 * NT)
                load_block(2, 2)
                load_block(3, 3)
                with sp.Fori(1, groups) as i:
                    for j in range(U):
                        sp.wait_ge(e_ps, U * i + (j + 1 - U))
                        load_block(U * i + j, j)
                        store_block(U * i + (j - U), j)
                for j in range(U):
                    store_block(U * groups + (j - U), j)
                for t in range(NT):
                    sp.wait_ge(f_y, t + 1)
                    dst = T["y_sample"].rearrange("a (t p) d -> p (a t) d", p=P)[:, t] if t < 4 else T["y_prompt"][0]
                    sp.dma_start(dst, acc[:, t, :]).then_inc(y_out, 16)
                sp.wait_ge(y_out, 16 * NT)

            @block.tensor
            def _(pe):
                for i, (w, src, b) in enumerate(((fw1, feats, 0), (fw2, hid1, 2))):
                    if i:
                        pe.wait_ge(f_s, 1)
                    pe.matmul(PS[0:HD, b, :], w, src[:, 0:SMP], start=True, stop=True)
                    pe.matmul(PS[0:HD, b + 1, 0:P], w, src[:, SMP:TOK], start=True, stop=True).then_inc(f_1, 1)
                pe.wait_ge(f_s, 2)
                for t in range(NT):
                    if t >= 2:
                        pe.wait_ge(f_hf, t - 1)
                    for o in range(2):
                        mm = pe.matmul(PS[:, 4 + 2 * (t % 2) + o, :], hid2[:, t * P:(t + 1) * P], fw3[:, 512 * o:512 * o + 512],
                                       start=True, stop=True)
                    mm.then_inc(f_h, 1)
                for t in range(NT):
                    pe.wait_ge(f_sq, t + 1)
                    for side in range(2):
                        mm = pe.matmul(PS[:, t // 4, :], ones, hsq[t % 2][:, :, side, :],
                                       start=t in (0, 4) and side == 0, stop=t in (3, 4) and side == 1)
                    mm.then_inc(f_nrm, 1)
                pe.wait_ge(f_sd, NT)
                pe.wait_ge(f_dft, 16)
                for i, (s, f) in enumerate(FT):
                    m, t0, nt = (fwd1, 4, 1) if s else (fwd5, 0, 4)
                    n = P if s else SMP
                    if i == 0:
                        pe.wait_ge(f_rn, 1)
                        pe.wait_ge(f_hf, NT)
                    if i >= 1:
                        pe.wait_ge(f_Ht, i)
                    for b, base, h in ((2, 0, hsum), (3, n, hdif)) + (((4, n, hsum),) if f == 0 else ()):
                        for t in range(nt):
                            mm = pe.matmul(PS[:, b, :], m[:, t, base + f * P:base + f * P + P],
                                           h[:, t0 + t].rearrange("p o n -> p (o n)"), start=t == 0, stop=t == nt - 1)
                    mm.then_inc(f_H, 1)
                for o in range(2):
                    if o == 1:
                        for t in range(NT):
                            pe.wait_ge(c_z1, 2 if t < 4 else 4)
                            if t >= 2:
                                pe.wait_ge(c_trt, t - 1)
                            for pt in range(2):
                                mm = pe.transpose(PS[:, t % 2, P * pt:P * pt + P], z1[:, pt, t * P:(t + 1) * P], ident)
                            mm.then_inc(c_tr, 1)
                        pe.wait_ge(c_trt, NT)
                    for i, (s, f) in enumerate(FT):
                        m, t0, nt = (fwd1, 4, 1) if s else (fwd5, 0, 4)
                        n = P if s else SMP
                        if o == 0 and i < 2:
                            pe.wait_ge(f_Ht, len(FT))
                        if len(FT) * o + i >= 2:
                            pe.wait_ge(c_pr, len(FT) * o + i - 1)
                        for part_, base in ((0, 0), (1, n)):
                            for t in range(nt):
                                z = z1_tok[:, t0 + t, :] if o else mh_tok[:, t0 + t, MW:512]
                                mm = pe.matmul(PS[:, 2 + (len(FT) * o + i) % 2, MW * part_:MW * part_ + MW],
                                               m[:, t, base + f * P:base + f * P + P], z, start=t == 0, stop=t == nt - 1)
                        mm.then_inc(c_Z, 1)
                    pe.wait_ge(c_Y, len(FT) * (o + 1))
                    if o == 1:
                        pe.wait_ge(c_out, 4)
                    for pt in range(2):
                        for k in range(8):
                            mm = pe.matmul(PS[:, 4 + pt, :], spec[:, k, P * pt:P * pt + P], inv5[:, k, :], start=k == 0, stop=k == 7)
                    mm.then_inc(c_y, 1)
                    for pt in range(2):
                        for k in range(2):
                            mm = pe.matmul(PS[:, 6, P * pt:P * pt + P], spec[:, 8 + k, P * pt:P * pt + P], inv1[:, k, :],
                                           start=k == 0, stop=k == 1)
                    mm.then_inc(c_y, 1)
                for n, (g, c) in enumerate([(g, c) for g in range(2) for c in range(2)]):
                    pe.wait_ge(o_gd, n + 1)
                    if n >= 2:
                        pe.wait_ge(o_gt, n - 1)
                    for half in range(2):
                        mm = pe.matmul(PS[:, 2 * (n % 2) + half, :], ones,
                                       gdiag[n % 2][:, 4 * half:4 * half + 4, :].rearrange("p k n -> p (k n)"), start=True, stop=True)
                    mm.then_inc(o_gr, 1)
                pe.wait_ge(o_w, 16)
                pe.wait_ge(c_z1, 8)
                for n in range(2 * NT):
                    t, half = n // 2, n % 2
                    if n >= 4:
                        pe.wait_ge(o_mul, n - 3)
                    for k in range(8):
                        mm = pe.matmul(PS[:, 4 + n % 4, :], yT[:, k, t * P:(t + 1) * P], w_out[:, k, 512 * half:512 * half + 512],
                                       start=k == 0, stop=k == 7)
                    mm.then_inc(o_ps, 1)
                pe.wait_ge(o_gt, 4)
                pe.wait_ge(n2_xn, NT)
                for k in range(KT):
                    if k >= 2:
                        pe.wait_ge(n2_s, k - 1)
                        pe.wait_ge(n2_p, k - 1)
                    for t in range(NT):
                        dst = PS[:, k % 2, t * P:(t + 1) * P] if t < 4 else PS[:, 2 + k % 2, 0:P]
                        mm = pe.transpose(dst, xn[:, t, k:D:KT], ident)
                    mm.then_inc(n2_tr, 1)
                pe.wait_ge(o_rw, 16)
                pe.wait_ge(n2_s, KT)
                pe.wait_ge(n2_p, KT)
                pe.wait_ge(o_mul, 2 * NT)
                for t in range(NT):
                    if t == 4:
                        pe.wait_ge(r_sig, 1)
                    for k in range(KT):
                        mm = pe.matmul(PS[:, 4 + t % 4, 0:NE], h2T[:, k, t * P:(t + 1) * P], rw[:, k, :], start=k == 0, stop=k == KT - 1)
                    mm.then_inc(r_ps, 1)
                for n in range(2 * NT):
                    t, half = n // 2, n % 2
                    if n >= 4:
                        pe.wait_ge(b_cp, n - 3)
                    for k in range(4):
                        mm = pe.transpose(PS[:, n % 4, k * P:(k + 1) * P], h2T[:, 4 * half + k, t * P:(t + 1) * P], ident)
                    mm.then_inc(b_ps, 1)

                def count():
                    pe.wait_ge(r_sig, NT)
                    pe.wait_ge(r_g, NT)
                    mask_all = mask.rearrange("p t n -> p (t n)")
                    pe.matmul(PS[:, 6, 0:NT * NE], after[:, 1, :], mask_all, start=True, stop=True)
                    pe.matmul(PS[:, 7, 0:NT * NE], ones, mask_all, start=True, stop=True).then_inc(m_cnt, 1)

                pe.wait_ge(s_w, 48)
                pe.wait_ge(b_cp, 2 * NT)
                for w, b in ((eg[1], 0), (eu[1], 2)):
                    for half in range(2):
                        for k in range(KT):
                            mm = pe.matmul(PS[:, b + half, 0:320], w[:, k, :], h2T[:, k, 320 * half:320 * half + 320],
                                           start=k == 0, stop=k == KT - 1)
                    mm.then_inc(s_gu, 1)
                    if b == 0:
                        count()
                for n in range(2 * NT):
                    t, half = n // 2, n % 2
                    if n == 0:
                        pe.wait_ge(s_hid, 1)
                    if n >= 2:
                        pe.wait_ge(s_acc, n - 1)
                    pe.matmul(PS[:, 4 + half, :], shid[:, t * P:(t + 1) * P], ed[1][:, 512 * half:512 * half + 512],
                              start=True, stop=True).then_inc(s_ps, 1)
                pe.wait_ge(m_ecol, 1)
                pe.wait_ge(m_off, NT + 1)
                pe.matmul(PS[0:1, 7, 0:P], ecol, ident, start=True, stop=True).then_inc(m_erow, 1)
                for t in range(NT):
                    pe.wait_ge(m_at, t + 1)
                    pe.wait_ge(m_bl, t + 1)
                    for k in range(TOPK):
                        mm = pe.matmul(PS[:, 6, 0:BLOCKS + 1], at_slot[t % 2][:, k, :], at_block[t % 2][:, k, :],
                                       start=t == 0 and k == 0, stop=t == NT - 1 and k == TOPK - 1)
                    mm.then_inc(m_tab, 1)

                def transpose_x(b, j, i1):
                    pe.wait_ge(e_x[j], 16 * i1)
                    for k in range(KT):
                        mm = pe.transpose(PS[:, k // 4, (k % 4) * P:(k % 4 + 1) * P], xg[j][:, k:D:KT], ident)
                    mm.then_inc(e_tr, 1)

                def gate_up(b, j, i1):
                    pe.wait_ge(e_w[j], 48 * i1)
                    pe.wait_ge(e_xT, b + 1)
                    for w, bank in ((eg[j], 2), (eu[j], 3)):
                        for k in range(KT):
                            mm = pe.matmul(PS[:, bank, 0:P], w[:, k, :], xT[j % 2][:, k, :], start=k == 0, stop=k == KT - 1)
                    mm.then_inc(e_gu, 1)

                def down(b, j, first=False):
                    pe.wait_ge(e_hid, b + 1)
                    if not first:
                        pe.wait_ge(e_y, b - 1)
                    for half in range(2):
                        mm = pe.matmul(PS[:, 4 + 2 * (j % 2) + half, :], hid[j % 2], ed[j][:, 512 * half:512 * half + 512],
                                       start=True, stop=True)
                    mm.then_inc(e_ps, 1)

                groups = group_count(pe)
                pe.wait_ge(m_tok, 1)
                pe.wait_ge(s_acc, 2 * NT)
                pe.wait_ge(s_up, 1)
                for j in range(U):
                    transpose_x(j, j, 1)
                    if j:
                        down(j - 1, j - 1, j <= 2)
                    gate_up(j, j, 1)
                with pe.Fori(1, groups) as i:
                    for j in range(U):
                        transpose_x(U * i + j, j, i + 1)
                        down(U * i + (j - 1), (j - 1) % U)
                        gate_up(U * i + j, j, i + 1)
                down(U * groups - 1, U - 1)

            @block.vector
            def _(dve):
                dve_order = Steps(dve, "dve_order2")
                TWO_PI = 2 * np.pi
                HI = 6.28125
                LO = float(TWO_PI - HI)
                MAGIC = 12582912.0
                for i in range(2):
                    b = 2 * i
                    dve.wait_ge(f_1, i + 1)
                    dve.tensor_scalar(fz[:, 0:SMP], PS[0:HD, b, :], fcol[:, 2 * i:2 * i + 1], fcol[:, 1:2], ALU.add, ALU.mult)
                    dve_order.done(dve.tensor_scalar(fz[:, SMP:TOK], PS[0:HD, b + 1, 0:P], fcol[:, 2 * i:2 * i + 1], fcol[:, 1:2],
                                                     ALU.add, ALU.mult))
                    dve_order.done(dve.tensor_scalar(fn, fz, 1.0 / TWO_PI, MAGIC, ALU.mult, ALU.add))
                    dve_order.done(dve.tensor_scalar(fn, fn, MAGIC, None, ALU.subtract))
                    dve_order.done(dve.scalar_tensor_tensor(out=fz, in0=fn, scalar=-HI, in1=fz, op0=ALU.mult, op1=ALU.add))
                    dve_order.done(dve.scalar_tensor_tensor(out=fz, in0=fn, scalar=-LO, in1=fz, op0=ALU.mult, op1=ALU.add))
                    dve.tensor_scalar(fz, fz, 3.1415925, -3.1415925, ALU.min, ALU.max).then_inc(f_z, 1)
                    dve.wait_ge(f_s, i + 1)
                dve.wait_ge(f_in, 16)
                for t in range(NT):
                    dve.wait_ge(f_h, t + 1)
                    for o in range(2):
                        i = dve.tensor_tensor(hf[:, t, o].rearrange("p s n -> p (s n)"), PS[:, 4 + 2 * (t % 2) + o, :],
                                              decay[:, t, :], ALU.mult)
                    i.then_inc(f_hf, 1)
                dve.wait_ge(f_nrm, NT)
                for s in range(2):
                    i = dve.tensor_scalar(rn[:, s, :], PS[:, s, :], EPS, None, ALU.add)
                i.then_inc(f_ne, 1)
                dve.wait_ge(f_nr, 1)
                dve.reciprocal(rn, rn).then_inc(f_rn, 1)
                dve.wait_ge(f_rn, 1)
                dve.wait_ge(f_sd, NT)
                for i, (s, f) in enumerate(FT):
                    dve.wait_ge(f_H, i + 1)
                    dve.tensor_tensor(HA[:, i, :], PS[:, 2, :], rn[:, s, :], ALU.mult)
                    j = dve.tensor_tensor(HB[:, i, :], PS[:, 3, :], rn[:, s, :], ALU.mult)
                    if f == 0:
                        dve_order.done(j)
                        dve.memset(HB[0:1, i, :], 0.0)
                        dve_order.done(dve.tensor_copy(HC[:, s, :], HA[:, i, :]))
                        j = dve.tensor_tensor(HC[0:1, s, :], PS[0:1, 4, :], rn[0:1, s, :], ALU.mult)
                    j.then_inc(f_Ht, 1)
                dve.wait_ge(f_Ht, len(FT))
                for o in range(2):
                    for i, (s, f) in enumerate(FT):
                        n = len(FT) * o + i
                        dve.wait_ge(c_Z, n + 1)
                        if n >= 2:
                            dve.wait_ge(c_Y, n - 1)
                        b, q = 2 + n % 2, pr[n % 2]
                        w = slice(MW * o, MW * o + MW)
                        hc = HC[:, s, w] if f == 0 else HA[:, i, w]
                        dve.tensor_tensor(q[:, 0, :], PS[:, b, 0:MW], HA[:, i, w], ALU.mult)
                        dve.tensor_tensor(q[:, 1, :], PS[:, b, MW:512], HB[:, i, w], ALU.mult)
                        dve.tensor_tensor(q[:, 2, :], PS[:, b, 0:MW], HB[:, i, w], ALU.mult)
                        dve.tensor_tensor(q[:, 3, :], PS[:, b, MW:512], hc, ALU.mult).then_inc(c_pr, 1)
                    for s in range(2):
                        dve.wait_ge(c_y, 2 * o + s + 1)
                        for pt in range(2):
                            cols = slice(0, SMP) if s == 0 else slice(SMP, TOK)
                            ps = PS[:, 4 + pt, :] if s == 0 else PS[:, 6, P * pt:P * pt + P]
                            z = z1[:, pt, cols] if o else hy[:, pt, cols]
                            dve.scalar_tensor_tensor(out=ctmp[:, cols], in0=z, scalar=tapsT[:, pt, 8 + o:9 + o], in1=ps,
                                                     op0=ALU.mult, op1=ALU.add).then_inc(c_out, 1)
                            dve.wait_ge(c_out, 4 * o + 2 * s + pt + 1)
                            dst, x = (yT[:, 6 + pt, cols], yT[:, 6 + pt, cols]) if o else (z1[:, pt, cols], hy[:, 2 + pt, cols])
                            dve.tensor_tensor(dst, x, ctmp[:, cols], ALU.mult).then_inc(c_z1, 1)
                            dve.wait_ge(c_z1, 4 * o + 2 * s + pt + 1)
                dve.wait_ge(c_z1, 8)
                dve_order.done(dve.tensor_scalar(scl2[:, :, :], modT[:, 4], 1.0, None, ALU.add))
                dve.tensor_tensor(scl2[:, :, :], scl2[:, :, :], spread(g2p, 2, 2), ALU.mult).then_inc(o_scl, 1)
                GR = [(g, c) for g in range(2) for c in range(2)]
                def gate_diag(n):
                    g, c = GR[n]
                    if n >= 2:
                        dve.wait_ge(o_gr, n - 1)
                    dve.tensor_tensor(gdiag[n % 2], spread(ident, 1, KT), spread(modT[:, 2 + 3 * g, :, c], 2, P),
                                      ALU.mult).then_inc(o_gd, 1)
                gate_diag(0)
                for n, (g, c) in enumerate(GR):
                    if n + 1 < 4:
                        gate_diag(n + 1)
                    dve.wait_ge(o_gr, n + 1)
                    dst = gate_row[:, g, c, :].rearrange("p (q k) -> p k q", k=KT)
                    b = 2 * (n % 2)
                    for half in range(2):
                        i = dve.tensor_copy(dst[:, 4 * half:4 * half + 4, :], PS[:, b + half, :].rearrange("p (k q) -> p k q", k=4))
                    i.then_inc(o_gt, 1)
                dve.wait_ge(o_gt, 4)
                dve.wait_ge(o_x, 32)
                for t in range(NT):
                    for half in range(2):
                        n = 2 * t + half
                        w = slice(512 * half, 512 * half + 512)
                        dve.wait_ge(o_ps, n + 1)
                        if n >= 2:
                            dve.wait_ge(o_x1, n - 1)
                        dve.tensor_tensor(otmp[half], PS[:, 4 + n % 4, :], gate_row[:, 0, t // 4, w], ALU.mult).then_inc(o_mul, 1)
                dve.wait_ge(n2_sq, NT)
                dve.tensor_scalar(sumsq[:, 0:NT], sumsq[:, 0:NT], 1.0 / D, EPS, ALU.mult, ALU.add).then_inc(n2_mean, 1)
                dve.wait_ge(n2_root, 1)
                dve_order.done(dve.reciprocal(rstd[:, 0:NT], rstd[:, 0:NT]))
                for t in range(NT):
                    dve.tensor_scalar(xn[:, t, :], xt[:, t, :], rstd[:, t:t + 1], None, ALU.mult).then_inc(n2_xn, 1)
                for k in range(KT):
                    dve.wait_ge(n2_tr, k + 1)
                    dve.tensor_scalar(h2T[:, k, 0:SMP], PS[:, k % 2, :], scl2[:, k, 0:1], modT[:, 3, k, 0:1], ALU.mult,
                                      ALU.add).then_inc(n2_s, 1)
                dve.wait_ge(r_sig, NT)
                dve.wait_ge(o_rb, 16)
                for t in range(NT):
                    dve_order.done(dve.tensor_tensor(biased[:, :], score[:, t, :], rb, ALU.add))
                    dve_order.done(dve.max(top8[:, :], biased[:, :]))
                    dve_order.done(dve.match_replace(gate[:, t, :], top8[:, :], biased[:, :], -BIG))
                    dve_order.done(dve.tensor_tensor(mask[:, t, :], gate[:, t, :], biased[:, :], ALU.not_equal))
                    dve_order.done(dve.tensor_tensor(gate[:, t, :], mask[:, t, :], score[:, t, :], ALU.mult))
                    dve_order.done(dve.tensor_reduce(gsum[:, 0:1], gate[:, t, :], AX.X, ALU.add))
                    dve_order.done(dve.reciprocal(gsum[:, 0:1], gsum[:, 0:1]))
                    dve.tensor_scalar(gate[:, t, :], gate[:, t, :], gsum[:, 0:1], 2.5, ALU.mult, ALU.mult).then_inc(r_g, 1)
                    dve.wait_ge(r_g, t + 1)
                dve.wait_ge(m_idx, 16)
                dve_order.done(dve.memset(off[:, 0, :], 0.0))
                for c in cum:
                    dve_order.done(dve.memset(c[:, 0:NE], 0.0))
                dve.wait_ge(m_cnt, 1)
                for t in range(NT):
                    dve.tensor_tensor(off[:, t + 1, :], off[:, t, :], PS[:, 7, t * NE:(t + 1) * NE], ALU.add).then_inc(m_off, 1)
                    dve.wait_ge(m_off, t + 1)
                a, b = cum
                c = a[:, NE:]
                dve_order.done(dve.tensor_scalar(c, off[:, NT, :], 1.0 / P, (P - 1) / P - (P - 1) / (2 * P), ALU.mult, ALU.add))
                dve_order.done(dve.tensor_scalar(c, c, MAGIC, None, ALU.add))
                dve.tensor_scalar(c, c, -MAGIC, None, ALU.add).then_inc(m_off, 1)
                dve.wait_ge(m_off, NT + 1)
                s = 1
                while s < NE:
                    dve_order.done(dve.tensor_tensor(b[:, NE:], a[:, NE:], a[:, NE - s:2 * NE - s], ALU.add))
                    a, b = b, a
                    s *= 2
                incl, excl = a[:, NE:], a[:, NE - 1:2 * NE - 1]
                dve_order.done(dve.tensor_scalar(cmpb, incl, index[:, P:P + 1], None, ALU.is_le))
                dve.tensor_reduce(ecol, cmpb, AX.X, ALU.add).then_inc(m_ecol, 1)
                dve_order.done(dve.tensor_scalar(ngf, incl[:, NE - 1:NE], 1.0 / U, (U - 1) / (2 * U), ALU.mult, ALU.add))
                dve_order.done(dve.tensor_scalar(ngf, ngf, MAGIC, None, ALU.add))
                dve_order.done(dve.tensor_scalar(ngf, ngf, -MAGIC, -float(LEAST), ALU.add, ALU.add))
                dve_order.done(dve.tensor_copy(block_expert[0:1, P:P + 1], ngf[0:1, :]))
                dve.wait_ge(m_erow, 1)
                dve_order.done(dve.tensor_scalar(erow[0:1, :], PS[0:1, 7, 0:P], float(NE - 1), None, ALU.min))
                dve.tensor_copy(block_expert[0:1, 0:P], erow[0:1, :]).then_inc(m_exp, 1)
                dve_order.done(dve.tensor_tensor(D1[:, :, :], off[:, 0:NT, :], PS[:, 6, 0:NT * NE].rearrange("p (t n) -> p t n", t=NT),
                                                 ALU.add))
                dve_order.done(dve.tensor_scalar(cmpb, excl, float(P), 1.0, ALU.mult, ALU.add))
                dve_order.done(dve.tensor_tensor(D1[:, :, :], D1[:, :, :], spread(cmpb, 1, NT), ALU.add))
                dve_order.done(dve.tensor_tensor(D1[:, :, :], D1[:, :, :], mask[:, :, :], ALU.mult))
                for t in range(NT):
                    i = dve.max(d8[:, t, :], D1[:, t, :])
                dve_order.done(i)
                d8_all = d8.rearrange("p t k -> p (t k)")
                dve_order.done(dve.tensor_scalar(hi, d8_all, 1.0 / P, -(P + 1) / (2 * P), ALU.mult, ALU.add))
                dve_order.done(dve.tensor_scalar(dest, d8_all, -1.0, None, ALU.add))
                dve_order.done(dve.tensor_scalar(hi, hi, MAGIC, None, ALU.add))
                dve.tensor_scalar(hi, hi, -MAGIC, None, ALU.add).then_inc(m_hi, 1)
                dve.wait_ge(m_hi, 1)
                dve_order.done(dve.tensor_scalar(lo, hi, -float(P), None, ALU.mult))
                dve_order.done(dve.tensor_tensor(lo, lo, dest, ALU.add))
                for t in range(NT):
                    if t >= 2:
                        dve.wait_ge(m_tab, t - 1)
                    dve.tensor_tensor(at_block[t % 2][:, :, :], spread(index[:, 0:BLOCKS + 1], 1, TOPK),
                                      spread(hi[:, t * TOPK:(t + 1) * TOPK], 2, BLOCKS + 1), ALU.is_equal).then_inc(m_beq, 1)
                    dve.tensor_tensor(at_slot[t % 2][:, :, :], spread(index[:, 0:P], 1, TOPK),
                                      spread(lo[:, t * TOPK:(t + 1) * TOPK], 2, P), ALU.is_equal).then_inc(m_at, 1)
                dve.tensor_copy(dest_u, dest).then_inc(m_dest, 1)
                dve.wait_ge(m_tab, NT)
                dve.tensor_copy(slot_token, PS[:, 6, 0:BLOCKS + 1]).then_inc(m_tok, 1)

                def hidden(b, j):
                    dve.wait_ge(e_silu, b + 1)
                    dve.tensor_tensor(hid[j % 2], gact, PS[:, 3, 0:P], ALU.mult).then_inc(e_hid, 1)

                def take_y(b, j, stored=None):
                    dve.wait_ge(e_ps, b + 1)
                    if stored is not None:
                        dve.wait_ge(e_out[j % 2], stored)
                    dve.tensor_copy(yb[j % 2].rearrange("p (h n) -> p h n", h=2),
                                    PS[:, 4 + 2 * (j % 2):6 + 2 * (j % 2), :]).then_inc(e_y, 1)

                def choice_gates(t):
                    dve_order.done(dve.tensor_tensor(pick[:, :, :], spread(D1[:, t, :], 1, TOPK), spread(d8[:, t, :], 2, NE), ALU.is_equal))
                    dve_order.done(dve.tensor_tensor(pick[:, :, :], pick[:, :, :], spread(gate[:, t, :], 1, TOPK), ALU.mult))
                    dve_order.done(dve.tensor_reduce(g8[:, t, :], pick[:, :, :], AX.X, ALU.add))

                groups = group_count(dve)
                choice_gates(NT - 1)
                for j in range(U):
                    if j:
                        take_y(j - 1, j - 1, None if j <= 2 else 16 * ((j - 1) // 2))
                    hidden(j, j)
                    choice_gates(j)
                with dve.Fori(1, groups) as i:
                    for j in range(U):
                        take_y(U * i + (j - 1), (j - 1) % U, 16 * (U // 2) * i + 16 * ((j - 1) // 2))
                        hidden(U * i + j, j)
                take_y(U * groups - 1, U - 1, 16 * (U // 2) * groups - 16)
                dve.wait_ge(e_out[0], 32 * groups)
                dve.wait_ge(e_out[1], 32 * groups)
                dve.tensor_scalar(d8_all, d8_all, 1.0, None, ALU.mult).then_inc(y_all, 1)
                dve.wait_ge(y_all, 1)
                dve.wait_ge(s_acc, 2 * NT)
                dve.wait_ge(o_fg, 16)
                def last_mean(t):
                    dve.wait_ge(f_sq2, t + 1)
                    dve.tensor_scalar(sumsq[:, t:t + 1], sumsq[:, t:t + 1], 1.0 / D, EPS, ALU.mult, ALU.add).then_inc(f_mn, 1)

                def last_scale(t):
                    dve.wait_ge(f_rt, t + 1)
                    dve_order.done(dve.reciprocal(rstd[:, t:t + 1], rstd[:, t:t + 1]))
                    dve.scalar_tensor_tensor(out=acc[:, t, :], in0=xt[:, t, :], scalar=rstd[:, t:t + 1], in1=fin_row,
                                             op0=ALU.mult, op1=ALU.mult).then_inc(f_y, 1)

                for t in range(NT):
                    for k in range(TOPK):
                        n = TOPK * t + k
                        dve.wait_ge(g_in[n % GB], 16 * (n // GB + 1))
                        dve.scalar_tensor_tensor(out=acc[:, t, :], in0=back[n % GB], scalar=g8[:, t, k:k + 1], in1=acc[:, t, :],
                                                 op0=ALU.mult, op1=ALU.add).then_inc(g_used, 1)
                        if t > 0 and k == 2:
                            last_mean(t - 1)
                        if t > 0 and k == 4:
                            last_scale(t - 1)
                        dve.wait_ge(g_used, n + 1)
                    dve_order.done(dve.tensor_tensor(fmul, acc[:, t, :], gate_row[:, 1, t // 4, :], ALU.mult))
                    dve.tensor_tensor(xt[:, t, :], xt[:, t, :], fmul, ALU.add).then_inc(f_x2, 1)
                    dve.wait_ge(f_x2, t + 1)
                last_mean(NT - 1)
                last_scale(NT - 1)

            @block.scalar
            def _(act):
                act_order = Steps(act, "act_order2")
                for i in range(2):
                    act.wait_ge(f_z, i + 1)
                    act.activation(hid1 if i == 0 else hid2, fz, ACT.Sin).then_inc(f_s, 1)
                act.wait_ge(f_ne, 1)
                act.activation(rn, rn, ACT.Sqrt).then_inc(f_nr, 1)
                for t in range(NT):
                    act.wait_ge(c_tr, t + 1)
                    act.activation(z1_tok[:, t, :], PS[:, t % 2, 0:256], ACT.Copy).then_inc(c_trt, 1)

                for t in range(NT):
                    act.wait_ge(o_x1, 2 * t + 2)
                    i = act.activation(part(r1_at + 8192, D), xt[:, t, :], ACT.Square, accum_out=sumsq[:, t:t + 1])
                    i.then_inc(n2_sq, 1)
                    act.wait_ge(n2_sq, t + 1)
                act.wait_ge(n2_mean, 1)
                act.activation(rstd[:, 0:NT], sumsq[:, 0:NT], ACT.Sqrt).then_inc(n2_root, 1)
                act.wait_ge(o_scl, 1)
                for k in range(KT):
                    act.wait_ge(n2_tr, k + 1)
                    act.activation(h2T[:, k, SMP:TOK], PS[:, 2 + k % 2, 0:P], ACT.Identity, scale=scl2[:, k, 1:2],
                                   bias=modT[:, 3, k, 1:2]).then_inc(n2_p, 1)
                for t in range(NT):
                    act.wait_ge(r_ps, t + 1)
                    act.activation(score[:, t, :], PS[:, 4 + t % 4, 0:NE], ACT.Sigmoid).then_inc(r_sig, 1)
                for n in range(2 * NT):
                    t, half = n // 2, n % 2
                    act.wait_ge(b_ps, n + 1)
                    dst = h2[:, t, :].rearrange("p (q k) -> p k q", k=KT)[:, 4 * half:4 * half + 4, :]
                    act.activation(dst, PS[:, n % 4, :].rearrange("p (k q) -> p k q", k=4), ACT.Copy).then_inc(b_cp, 1)
                act.wait_ge(s_gu, 1)
                act.activation(sact.rearrange("p (b n) -> p b n", b=2), PS[:, 0:2, 0:320], ACT.Silu).then_inc(s_act, 1)
                act.wait_ge(s_gu, 2)
                act.activation(sup.rearrange("p (b n) -> p b n", b=2), PS[:, 2:4, 0:320], ACT.Copy).then_inc(s_up, 1)
                for n in range(2 * NT):
                    t, half = n // 2, n % 2
                    act.wait_ge(s_ps, n + 1)
                    act.activation(acc[:, t, 512 * half:512 * half + 512], PS[:, 4 + half, :], ACT.Copy).then_inc(s_acc, 1)

                def copy_xT(b, j):
                    act.wait_ge(e_tr, b + 1)
                    act.activation(xT[j % 2].rearrange("p (h k) n -> p h (k n)", h=2), PS[:, 0:2, :], ACT.Copy).then_inc(e_xT, 1)

                def silu(b, first=False):
                    act.wait_ge(e_gu, b + 1)
                    if not first:
                        act.wait_ge(e_hid, b)
                    act.activation(gact, PS[:, 2, 0:P], ACT.Silu).then_inc(e_silu, 1)

                act.wait_ge(m_idx, 16)
                for t in range(NT):
                    act.wait_ge(m_beq, t + 1)
                    act.activation(at_block[t % 2].rearrange("p k n -> p (k n)"), at_block[t % 2].rearrange("p k n -> p (k n)"),
                                   ACT.Copy, scale=index[:, P + t:P + t + 1]).then_inc(m_bl, 1)
                groups = group_count(act)
                act.wait_ge(m_tok, 1)
                act.wait_ge(s_hid, 1)
                for j in range(U):
                    copy_xT(j, j)
                    silu(j, j == 0)
                with act.Fori(1, groups) as i:
                    for j in range(U):
                        copy_xT(U * i + j, j)
                        silu(U * i + j)
                for t in range(NT):
                    act.wait_ge(f_x2, t + 1)
                    act.activation(fjunk, xt[:, t, :], ACT.Square, accum_out=sumsq[:, t:t + 1]).then_inc(f_sq2, 1)
                    act.wait_ge(f_sq2, t + 1)
                    act.wait_ge(f_mn, t + 1)
                    act.activation(rstd[:, t:t + 1], sumsq[:, t:t + 1], ACT.Sqrt).then_inc(f_rt, 1)

            @block.gpsimd
            def _(pool):
                pool_order = Steps(pool, "pool_order2")
                for t in range(NT):
                    pool.wait_ge(f_hf, t + 1)
                    if t >= 2:
                        pool.wait_ge(f_nrm, t - 1)
                    h = hf[:, t]
                    pool.tensor_tensor(hsq[t % 2].rearrange("p o s n -> p (o s n)"), h.rearrange("p o s n -> p (o s n)"),
                                       h.rearrange("p o s n -> p (o s n)"), ALU.mult).then_inc(f_sq, 1)
                    pool.tensor_tensor(hsum[:, t], h[:, :, 0, :], h[:, :, 1, :], ALU.add)
                    pool.tensor_tensor(hdif[:, t], h[:, :, 0, :], h[:, :, 1, :], ALU.subtract).then_inc(f_sd, 1)
                for o in range(2):
                    for i, (s, f) in enumerate(FT):
                        n = len(FT) * o + i
                        pool.wait_ge(c_pr, n + 1)
                        if o == 1 and i == 0:
                            pool.wait_ge(c_y, 2)
                        q = pr[n % 2]
                        re, im = (8, 9) if s else (f, 4 + f)
                        pool.tensor_tensor(spec[:, re, :], q[:, 0, :], q[:, 1, :], ALU.subtract)
                        pool.tensor_tensor(spec[:, im, :], q[:, 2, :], q[:, 3, :], ALU.add).then_inc(c_Y, 1)
                pool.wait_ge(o_x, 32)
                for n in range(2 * NT):
                    t, half = n // 2, n % 2
                    w = slice(512 * half, 512 * half + 512)
                    pool.wait_ge(o_mul, n + 1)
                    pool.tensor_tensor(xt[:, t, w], xt[:, t, w], otmp[half], ALU.add).then_inc(o_x1, 1)
                pool.wait_ge(s_act, 1)
                pool.wait_ge(s_up, 1)
                pool.tensor_tensor(shid, sact, sup, ALU.mult).then_inc(s_hid, 1)
                pool.wait_ge(m_tok, 1)
                pool.wait_ge(h2_out, 16 * NT)

                def fetch_x(b, j, first=False):
                    if not first:
                        pool.wait_ge(e_tr, b - (U - 2))
                    pool.wait_ge(x_col, b + 1)
                    pool.tensor_copy(token_col[(j + 1) % U], slot_token[:, bass.ds(b + 1, 1)]).then_inc(x_col, 1)
                    pool.indirect_dma_start(xg[j], None, T["h2_rows"], bass.IndirectOffsetOnAxis(token_col[j], 0)).then_inc(e_x[j], 16)

                pool.tensor_copy(token_col[0], slot_token[:, 0:1]).then_inc(x_col, 1)
                for j in range(U):
                    fetch_x(j, j, j < U - 1)
                groups = group_count(pool)
                with pool.Fori(1, groups) as i:
                    for j in range(U):
                        fetch_x(U * i + j, j)
                pool.wait_ge(m_dest, 1)
                pool.wait_ge(y_all, 1)
                for n in range(PAIRS):
                    if n >= GB:
                        pool.wait_ge(g_used, n - GB + 1)
                    pool.indirect_dma_start(back[n % GB], None, T["y_rows"],
                                            bass.IndirectOffsetOnAxis(dest_u[:, n:n + 1], 0)).then_inc(g_in[n % GB], 16)



_IN = ['x_prompt', 'x_sample', 'c', 'state_gdn', 'state_hgrn', 'state_mlstm_c', 'state_mlstm_n',
       'state_mlstm_m', 'c_ctx', 'norm1_g', 'norm2_g', 'w_mod', 'b_mod', 'w_in', 'gdn_conv', 'gdn_a_log',
       'gdn_dt_bias', 'gdn_norm_g', 'hgrn_lb_logits', 'hgrn_norm_g', 'mlstm_f_bias', 'mlstm_norm_g',
       'hyena_conv', 'filt_w1', 'filt_b1', 'filt_w2', 'filt_b2', 'filt_w3', 'filt_freq', 'hyena_d',
       'w_out', 'router_w', 'router_bias', 'exp_w_gate', 'exp_w_up', 'exp_w_down', 'sh_w_gate',
       'sh_w_up', 'sh_w_down', 'final_g']
_OUT = [("y_prompt", (1, P, D)), ("y_sample", (1, SMP, D)), ("new_gdn", (1, 1, 2, 4, HD, HD)),
        ("new_hgrn", (1, 1, 2, 4, HD, HD)), ("new_c", (1, 1, 2, 4, HD, HD)), ("new_n", (1, 1, 2, 4, HD)),
        ("new_m", (1, 1, 2, 4))]


def kernel(**inputs):
    import concourse.bacc as bacc
    from concourse.bass_utils import run_bass_kernel_spmd

    nc = bacc.Bacc("TRN2", target_bir_lowering=False, num_devices=1)
    arrays, T = {}, {}
    for name in _IN:
        a = np.ascontiguousarray(inputs[name])
        arrays["in_" + name] = a
        T[name] = nc.dram_tensor("in_" + name, a.shape, mybir.dt.float32, kind="ExternalInput").ap()
    for name, a in zip(("masks", "dfts", "feats", "decay"), shape_constants()):
        arrays["const_" + name] = a
        T[name] = nc.dram_tensor("const_" + name, a.shape, mybir.dt.float32, kind="ExternalInput").ap()
    for name, shape in _OUT:
        T[name] = nc.dram_tensor("out_" + name, shape, mybir.dt.float32, kind="ExternalOutput").ap()
    arrays["const_index"] = index = token_numbers()
    T["index"] = nc.dram_tensor("const_index", index.shape, mybir.dt.float32, kind="ExternalInput").ap()
    T["h2_rows"] = nc.dram_tensor("h2_rows", (TOK, D), mybir.dt.float32).ap()
    T["y_rows"] = nc.dram_tensor("y_rows", ((TOK * TOPK // P + NE) * P, D), mybir.dt.float32).ap()
    trunk_program(nc, T)
    r = run_bass_kernel_spmd(nc, [arrays], core_ids=[0])
    return tuple(r.results[0]["out_" + name] for name, _ in _OUT)
```
